# Optimizing a Trainium2 kernel written in Bass

```python
import jax
import jax.numpy as jnp
from jax import lax
import numpy as np

D_MODEL = 1024
BATCH = 1
SEQ = 512
DEPTH = 2
DEC_BATCH = 8
DEC_SEQ = 8
PAST_LEN = 512
PAGE_SIZE = 128

HEAD_DIM = 64
ROPE_DIM = HEAD_DIM // 4
ROPE_THETA = 500000.0
NSA_HEADS = 8
NSA_KV_HEADS = 2
NSA_GROUP = NSA_HEADS // NSA_KV_HEADS
CMP_BLOCK = 32
CMP_STRIDE = 16
SEL_BLOCK = 64
N_SEL = 8
WINDOW = 512
Q_BLOCK = 128
LRU_WIDTH = D_MODEL // 2
LRU_BLOCKS = 8
LRU_BLOCK_DIM = LRU_WIDTH // LRU_BLOCKS
LRU_C = 8.0
SHORT_CONV = 4
SSD_HEADS = 16
SSD_HEAD_DIM = 64
SSD_INNER = SSD_HEADS * SSD_HEAD_DIM
SSD_GROUPS = 2
SSD_STATE = 128
SSD_CHUNK = 64
SSD_CONV_DIM = SSD_INNER + 2 * SSD_GROUPS * SSD_STATE
GLA_HEADS = 4
GLA_DK = 128
GLA_DV = 128
GLA_RANK = 16
GLA_TAU = 16.0
GLA_CHUNK = 32
D_FF = 2816
FFN_CONV = 3
N_EVEN = (DEPTH + 1) // 2
N_ODD = DEPTH // 2
ALPHA = (2.0 * DEPTH) ** 0.25
BETA = (8.0 * DEPTH) ** -0.25
LN_EPS = 1e-5
NEG = -1e30
EV_Q = NSA_HEADS * HEAD_DIM
EV_KV = 6 * NSA_KV_HEADS * HEAD_DIM
EV_GATE = 3 * NSA_HEADS
EVEN_IN = EV_Q + EV_KV + EV_GATE + 2 * LRU_WIDTH
EVEN_OUT = EV_Q + LRU_WIDTH
ODD_SIZES = (SSD_INNER, SSD_CONV_DIM, SSD_HEADS, GLA_HEADS * GLA_DK, GLA_HEADS * GLA_DK, GLA_HEADS * GLA_DV, GLA_HEADS * GLA_DV, GLA_RANK)
ODD_IN = sum(ODD_SIZES)
ODD_OUT = SSD_INNER + GLA_HEADS * GLA_DV
F32 = jnp.float32

kernel_name = 'hybrid_nsa_rglru_ssd_gla_step'

def split_cols(h, sizes):
    cuts = [int(c) for c in np.cumsum(sizes)[:-1]]
    return jnp.split(h, cuts, axis=-1)

def pad_time(a, pad):
    return jnp.pad(a, [(0, 0), (0, pad)] + [(0, 0)] * (a.ndim - 2))

def layer_norm(x, g, b):
    xf = x.astype(F32)
    mu = jnp.mean(xf, -1, keepdims=True)
    var = jnp.mean(jnp.square(xf - mu), -1, keepdims=True)
    return ((xf - mu) * lax.rsqrt(var + LN_EPS) * g + b).astype(x.dtype)

def rms_norm(x, w):
    xf = x.astype(F32)
    return xf * lax.rsqrt(jnp.mean(xf * xf, -1, keepdims=True) + LN_EPS) * w

def masked_softmax(s, mask):
    p = jax.nn.softmax(jnp.where(mask, s, NEG), axis=-1)
    return jnp.where(mask, p, 0.0)

def partial_rope(x, pos):
    half = ROPE_DIM // 2
    inv = jnp.power(ROPE_THETA, -2.0 * jnp.arange(half, dtype=F32) / ROPE_DIM)
    ang = pos.astype(F32)[:, None] * inv[None, :]
    cos = jnp.cos(ang)[None, :, None, :]
    sin = jnp.sin(ang)[None, :, None, :]
    x1 = x[..., :half].astype(F32)
    x2 = x[..., half:ROPE_DIM].astype(F32)
    rot = jnp.concatenate([x1 * cos - x2 * sin, x2 * cos + x1 * sin], -1).astype(x.dtype)
    return jnp.concatenate([rot, x[..., ROPE_DIM:]], -1)

def causal_dwconv(x, buf, w, b):
    K = w.shape[0]
    T = x.shape[1]
    xp = jnp.concatenate([buf.astype(x.dtype), x], axis=1)
    y = b + sum(w[j] * xp[:, j:j + T] for j in range(K))
    return y, xp[:, T:]

def segsum(x):
    L = x.shape[-1]
    xe = jnp.where(jnp.tril(jnp.ones((L, L), bool), -1), jnp.broadcast_to(x[..., None], x.shape + (L,)), 0.0)
    ss = jnp.cumsum(xe, axis=-2)
    return jnp.where(jnp.tril(jnp.ones((L, L), bool)), ss, -jnp.inf)

def linear_scan(a, u, h0):
    u = u.at[:, 0].add(a[:, 0] * h0)
    def combine(l, r):
        return (l[0] * r[0], r[0] * l[1] + r[1])
    _, h = lax.associative_scan(combine, (a, u), axis=1)
    return h

def overlap_matrix(n_cmp, n_sel):
    s1 = np.arange(n_cmp)[:, None] * CMP_STRIDE
    s2 = np.arange(n_sel)[None, :] * SEL_BLOCK
    ov = np.clip(np.minimum(s1 + CMP_BLOCK, s2 + SEL_BLOCK) - np.maximum(s1, s2), 0, None)
    return jnp.asarray(ov / CMP_BLOCK, dtype=F32)

def compress_blocks(kv, cmp_w):
    B, Tk = kv.shape[:2]
    r = CMP_BLOCK // CMP_STRIDE
    nh = Tk // CMP_STRIDE
    n_cmp = nh - r + 1
    halves = kv[:, :nh * CMP_STRIDE].reshape(B, nh, CMP_STRIDE, 2, NSA_KV_HEADS, HEAD_DIM)
    w = cmp_w.astype(F32).reshape(r, CMP_STRIDE, 2, NSA_KV_HEADS)
    parts = jnp.einsum('bnschd,rsch->rbnchd', halves, w)
    return sum(parts[m][:, m:m + n_cmp] for m in range(r))

def nsa_attention(q, kv_full, win_full, gates, cmp_w):
    B, Tq = q.shape[:2]
    dh = HEAD_DIM
    Tk = kv_full.shape[1]
    t = (Tk - Tq) + jnp.arange(Tq)
    qg = (q.astype(F32) * dh ** -0.5).reshape(B, Tq, NSA_KV_HEADS, NSA_GROUP, dh)
    kv = kv_full.astype(F32)
    qb_len = Q_BLOCK if Tq % Q_BLOCK == 0 else Tq
    nb = Tq // qb_len

    ck = compress_blocks(kv[:, :, :2], cmp_w)
    n_cmp = ck.shape[1]
    end_c = jnp.arange(n_cmp) * CMP_STRIDE + CMP_BLOCK - 1
    mask_c = (end_c[None, :] <= t[:, None])[None, :, None, None, :]
    p_c = masked_softmax(jnp.einsum('bqhgd,bnhd->bqhgn', qg, ck[:, :, 0]), mask_c)
    o_cmp = jnp.einsum('bqhgn,bnhd->bqhgd', p_c, ck[:, :, 1])

    n_sel = -(-Tk // SEL_BLOCK)
    k_top = min(N_SEL, n_sel)
    imp = jnp.einsum('bqhgn,nj->bqhj', p_c, overlap_matrix(n_cmp, n_sel))
    blk = jnp.arange(n_sel)[None, :]
    cur = (t // SEL_BLOCK)[:, None]
    future = blk * SEL_BLOCK > t[:, None]
    forced = (blk == 0) | (blk == cur) | (blk == cur - 1)
    imp = jnp.where(future[None, :, None], -1.0, jnp.where(forced[None, :, None], 1e6, imp))
    _, idx = lax.top_k(imp, k_top)
    pad = n_sel * SEL_BLOCK - Tk

    def to_blocks(a):
        a = jnp.pad(a, ((0, 0), (0, pad), (0, 0), (0, 0)))
        a = a.reshape(B, n_sel, SEL_BLOCK, NSA_KV_HEADS, dh).transpose(0, 3, 1, 2, 4)
        return a.reshape(B, NSA_KV_HEADS, n_sel, SEL_BLOCK * dh)

    ks_b = to_blocks(kv[:, :, 2])
    vs_b = to_blocks(kv[:, :, 3])
    bi = jnp.arange(B)[:, None, None]
    hi = jnp.arange(NSA_KV_HEADS)[None, :, None]
    offs = jnp.arange(SEL_BLOCK)

    def sel_block(args):
        qb, ib, tb = args
        flat = ib.transpose(0, 2, 1, 3).reshape(B, NSA_KV_HEADS, qb_len * k_top)
        kg = ks_b[bi, hi, flat].reshape(B, NSA_KV_HEADS, qb_len, k_top, SEL_BLOCK, dh)
        vg = vs_b[bi, hi, flat].reshape(B, NSA_KV_HEADS, qb_len, k_top, SEL_BLOCK, dh)
        s = jnp.einsum('bqhgd,bhqkpd->bqhgkp', qb, kg)
        kpos = ib[..., None] * SEL_BLOCK + offs
        m = (kpos <= tb[None, :, None, None, None])[:, :, :, None]
        shp = s.shape
        p = masked_softmax(s.reshape(shp[:4] + (-1,)), jnp.broadcast_to(m, shp).reshape(shp[:4] + (-1,))).reshape(shp)
        return jnp.einsum('bqhgkp,bhqkpd->bqhgd', p, vg)

    o_slc = lax.map(sel_block, (
        qg.reshape(B, nb, qb_len, NSA_KV_HEADS, NSA_GROUP, dh).swapaxes(0, 1),
        idx.reshape(B, nb, qb_len, NSA_KV_HEADS, k_top).swapaxes(0, 1),
        t.reshape(nb, qb_len)))
    o_slc = o_slc.swapaxes(0, 1).reshape(B, Tq, NSA_KV_HEADS, NSA_GROUP, dh)

    Tw = win_full.shape[1]
    padl = WINDOW - (Tw - Tq)
    wf = jnp.pad(win_full.astype(F32), ((0, 0), (padl, 0), (0, 0), (0, 0), (0, 0)))
    kidx = (jnp.arange(nb) * qb_len)[:, None] + jnp.arange(qb_len + WINDOW)[None, :]
    wb = wf[:, kidx]
    qw = qg.reshape(B, nb, qb_len, NSA_KV_HEADS, NSA_GROUP, dh)
    s_w = jnp.einsum('bnqhgd,bnkhd->bnqhgk', qw, wb[:, :, :, 0])
    qidx = WINDOW + (jnp.arange(nb) * qb_len)[:, None] + jnp.arange(qb_len)[None, :]
    kk = kidx[:, None, :]
    qq = qidx[:, :, None]
    m_w = (kk <= qq) & (kk > qq - WINDOW) & (kk >= padl)
    p_w = masked_softmax(s_w, m_w[None, :, :, None, None, :])
    o_win = jnp.einsum('bnqhgk,bnkhd->bnqhgd', p_w, wb[:, :, :, 1]).reshape(B, Tq, NSA_KV_HEADS, NSA_GROUP, dh)

    g = jax.nn.sigmoid(gates.astype(F32)).reshape(B, Tq, NSA_KV_HEADS, NSA_GROUP, 3)
    o = g[..., 0:1] * o_cmp + g[..., 1:2] * o_slc + g[..., 2:3] * o_win
    return o.reshape(B, Tq, NSA_HEADS * dh).astype(q.dtype)

def even_mixer(x, past_kv, win_buf, win_keep, lru_h0, lru_conv0, w_in, w_out, cmp_w, conv_w, conv_b, w_gates, b_gates, lam):
    B, T, _ = x.shape
    pos = past_kv.shape[1] + jnp.arange(T)
    hq, hkv, hg, hx, hgate = split_cols(x @ w_in, (EV_Q, EV_KV, EV_GATE, LRU_WIDTH, LRU_WIDTH))
    q = partial_rope(hq.reshape(B, T, NSA_HEADS, HEAD_DIM), pos)
    kv = hkv.reshape(B, T, 3, 2, NSA_KV_HEADS, HEAD_DIM)
    k = partial_rope(kv[:, :, :, 0].reshape(B, T, 3 * NSA_KV_HEADS, HEAD_DIM), pos).reshape(B, T, 3, NSA_KV_HEADS, HEAD_DIM)
    kv = jnp.stack([k, kv[:, :, :, 1]], axis=3).reshape(B, T, 6, NSA_KV_HEADS, HEAD_DIM)
    new_rows = kv[:, :, :4]
    kv_full = jnp.concatenate([past_kv.astype(kv.dtype), new_rows], axis=1)
    win_full = jnp.concatenate([win_buf.astype(kv.dtype), kv[:, :, 4:]], axis=1)
    o_nsa = nsa_attention(q, kv_full, win_full, hg.reshape(B, T, NSA_HEADS, 3), cmp_w)
    xc, lru_conv = causal_dwconv(hx, lru_conv0, conv_w, conv_b)
    gt = jnp.einsum('btnd,knde->kbtne', xc.reshape(B, T, LRU_BLOCKS, LRU_BLOCK_DIM), w_gates).reshape(2, B, T, LRU_WIDTH)
    gt = gt.astype(F32) + b_gates[:, None, None, :]
    r_gate = jax.nn.sigmoid(gt[0])
    i_gate = jax.nn.sigmoid(gt[1])
    log_a = -LRU_C * r_gate * jax.nn.softplus(-lam.astype(F32))
    a = jnp.exp(log_a)
    u = jnp.sqrt(-jnp.expm1(2.0 * log_a)) * i_gate * xc.astype(F32)
    h = linear_scan(a, u, lru_h0.astype(F32))
    y_lru = (h * jax.nn.gelu(hgate.astype(F32))).astype(x.dtype)
    out = jnp.concatenate([o_nsa, y_lru], axis=-1) @ w_out
    return out, new_rows, win_full[:, win_full.shape[1] - win_keep:], h[:, -1], lru_conv

def ssd_scan(xdt, log_a, bm, cm, h0):
    B, T, H, P = xdt.shape
    G, N = bm.shape[2], bm.shape[3]
    J = H // G
    l = min(SSD_CHUNK, T)
    c = -(-T // l)
    pad = c * l - T
    X = pad_time(xdt, pad).reshape(B, c, l, G, J, P)
    A = pad_time(log_a, pad).reshape(B, c, l, G, J).transpose(0, 3, 4, 1, 2)
    Bc = pad_time(bm, pad).reshape(B, c, l, G, N)
    Cc = pad_time(cm, pad).reshape(B, c, l, G, N)
    A_cum = jnp.cumsum(A, axis=-1)
    L = jnp.exp(segsum(A))
    CB = jnp.einsum('bclgn,bcsgn->bgcls', Cc, Bc)
    y_diag = jnp.einsum('bgcls,bgjcls,bcsgjp->bclgjp', CB, L, X)
    decay_states = jnp.exp(A_cum[..., -1:] - A_cum)
    states = jnp.einsum('bclgn,bgjcl,bclgjp->bcgjpn', Bc, decay_states, X)
    states = jnp.concatenate([h0.reshape(B, 1, G, J, P, N), states], axis=1)
    decay_chunk = jnp.exp(segsum(jnp.pad(A_cum[..., -1], ((0, 0), (0, 0), (0, 0), (1, 0)))))
    new_states = jnp.einsum('bgjzc,bcgjpn->bzgjpn', decay_chunk, states)
    prev, final = new_states[:, :-1], new_states[:, -1]
    y_off = jnp.einsum('bclgn,bcgjpn,bgjcl->bclgjp', Cc, prev, jnp.exp(A_cum))
    y = (y_diag + y_off).reshape(B, c * l, H, P)[:, :T]
    return y, final.reshape(B, H, P, N)

def gla_scan(q, k, v, log_alpha, s0):
    B, T, H, K = q.shape
    V = v.shape[-1]
    l = min(GLA_CHUNK, T)
    c = -(-T // l)
    pad = c * l - T
    q, k, v, la = [pad_time(a, pad).reshape(B, c, l, H, a.shape[-1]) for a in (q, k, v, log_alpha)]
    b = jnp.cumsum(la, axis=2)
    qe = q * jnp.exp(b)
    ke = k * jnp.exp(-b)
    causal = jnp.tril(jnp.ones((l, l), bool))
    att = jnp.where(causal, jnp.einsum('bclhk,bcshk->bchls', qe, ke), 0.0)
    o_intra = jnp.einsum('bchls,bcshv->bclhv', att, v)
    b_end = b[:, :, -1]
    kv_chunk = jnp.einsum('bclhk,bclhv->bchkv', k * jnp.exp(b_end[:, :, None] - b), v)

    def step(s, inp):
        dec, kvc = inp
        return dec[..., None] * s + kvc, s

    s_final, s_prev = lax.scan(step, s0, (jnp.exp(b_end).swapaxes(0, 1), kv_chunk.swapaxes(0, 1)))
    o_inter = jnp.einsum('bclhk,cbhkv->bclhv', qe, s_prev)
    o = (o_intra + o_inter).reshape(B, c * l, H, V)[:, :T]
    return o, s_final

def odd_mixer(x, ssd_h0, ssd_conv0, gla_s0, w_in, w_out, conv_w, conv_b, dt_bias, a_log, d_skip, norm_w, w_alpha, b_alpha, gla_norm_w):
    B, T, _ = x.shape
    z, xbc, dt, gq, gk, gv, gg, ga = split_cols(x @ w_in, ODD_SIZES)
    xbc, ssd_conv = causal_dwconv(xbc, ssd_conv0, conv_w, conv_b)
    xbc = jax.nn.silu(xbc.astype(F32))
    xs, bm, cm = split_cols(xbc, (SSD_INNER, SSD_GROUPS * SSD_STATE, SSD_GROUPS * SSD_STATE))
    xs = xs.reshape(B, T, SSD_HEADS, SSD_HEAD_DIM)
    dt = jax.nn.softplus(dt.astype(F32) + dt_bias)
    log_decay = dt * -jnp.exp(a_log.astype(F32))
    y, ssd_h = ssd_scan(xs * dt[..., None], log_decay, bm.reshape(B, T, SSD_GROUPS, SSD_STATE),
                        cm.reshape(B, T, SSD_GROUPS, SSD_STATE), ssd_h0.astype(F32))
    y = y + d_skip[:, None] * xs
    y = rms_norm(y.reshape(B, T, SSD_INNER) * jax.nn.silu(z.astype(F32)), norm_w)
    q = gq.reshape(B, T, GLA_HEADS, GLA_DK).astype(F32) * GLA_DK ** -0.5
    k = gk.reshape(B, T, GLA_HEADS, GLA_DK).astype(F32)
    v = gv.reshape(B, T, GLA_HEADS, GLA_DV).astype(F32)
    log_alpha = (jax.nn.log_sigmoid(ga.astype(F32) @ w_alpha + b_alpha) / GLA_TAU).reshape(B, T, GLA_HEADS, GLA_DK)
    o, gla_s = gla_scan(q, k, v, log_alpha, gla_s0.astype(F32))
    o = rms_norm(o, gla_norm_w).reshape(B, T, GLA_HEADS * GLA_DV) * jax.nn.silu(gg.astype(F32))
    out = jnp.concatenate([y, o], axis=-1).astype(x.dtype) @ w_out
    return out, ssd_h, ssd_conv, gla_s

def conv_ffn(x, buf, w_up, conv_w, conv_b, w_down):
    u, new_buf = causal_dwconv(x @ w_up, buf, conv_w, conv_b)
    gate, val = jnp.split(u, 2, axis=-1)
    return (jax.nn.gelu(gate) * val) @ w_down, new_buf

def trunk(x, get_past, win_bufs, win_keep, lru_h, lru_conv, ssd_h, ssd_conv, gla_s, ffn_conv, p):
    kv_rows, wins, lh, lc, sh, sc, gs, fc = [], [], [], [], [], [], [], []
    for layer in range(DEPTH):
        j = layer // 2
        if layer % 2 == 0:
            mix, rows, win, h, c = even_mixer(
                x, get_past(j), win_bufs[j], win_keep, lru_h[j], lru_conv[j],
                p['w_in_even'][j], p['w_out_even'][j], p['nsa_cmp_w'][j], p['lru_conv_w'][j],
                p['lru_conv_b'][j], p['lru_w_gates'][j], p['lru_b_gates'][j], p['lru_lambda'][j])
            kv_rows.append(rows)
            wins.append(win)
            lh.append(h)
            lc.append(c)
        else:
            mix, s, c, g = odd_mixer(
                x, ssd_h[j], ssd_conv[j], gla_s[j], p['w_in_odd'][j], p['w_out_odd'][j],
                p['ssd_conv_w'][j], p['ssd_conv_b'][j], p['ssd_dt_bias'][j], p['ssd_a_log'][j],
                p['ssd_d'][j], p['ssd_norm_w'][j], p['gla_w_alpha'][j], p['gla_b_alpha'][j], p['gla_norm_w'][j])
            sh.append(s)
            sc.append(c)
            gs.append(g)
        x = layer_norm(ALPHA * x + mix, p['ln_mix_g'][layer], p['ln_mix_b'][layer])
        f, fb = conv_ffn(x, ffn_conv[layer], p['ffn_w_up'][layer], p['ffn_conv_w'][layer],
                         p['ffn_conv_b'][layer], p['ffn_w_down'][layer])
        fc.append(fb)
        x = layer_norm(ALPHA * x + f, p['ln_ffn_g'][layer], p['ln_ffn_b'][layer])
    stk = jnp.stack
    return x, (stk(kv_rows), stk(wins), stk(lh), stk(lc), stk(sh), stk(sc), stk(gs), stk(fc))

def setup_inputs(seed: int = 0) -> dict:
    key = jax.random.key(seed)
    ks = iter(jax.random.split(key, 48))

    def nrm(shape, scale):
        return jax.random.normal(next(ks), shape, F32) * scale

    def uni(shape, lo, hi):
        return jax.random.uniform(next(ks), shape, F32, lo, hi)

    n_pages = PAST_LEN // PAGE_SIZE
    n_used = DEC_BATCH * n_pages
    n_phys = n_used + n_used // 4
    wbuf = min(WINDOW, PAST_LEN)
    inp = {}
    inp['x_prompt'] = nrm((BATCH, SEQ, D_MODEL), 1.0)
    inp['x_sample'] = nrm((DEC_BATCH, DEC_SEQ, D_MODEL), 1.0)
    inp['cache_nsa_kv'] = nrm((N_EVEN, n_phys, PAGE_SIZE, 4, NSA_KV_HEADS, HEAD_DIM), 1.0)
    inp['cache_nsa_win'] = nrm((N_EVEN, DEC_BATCH, wbuf, 2, NSA_KV_HEADS, HEAD_DIM), 1.0)
    inp['state_lru_h'] = nrm((N_EVEN, DEC_BATCH, LRU_WIDTH), 0.5)
    inp['state_lru_conv'] = nrm((N_EVEN, DEC_BATCH, SHORT_CONV - 1, LRU_WIDTH), 1.0)
    inp['state_ssd'] = nrm((N_ODD, DEC_BATCH, SSD_HEADS, SSD_HEAD_DIM, SSD_STATE), 0.2)
    inp['state_ssd_conv'] = nrm((N_ODD, DEC_BATCH, SHORT_CONV - 1, SSD_CONV_DIM), 1.0)
    inp['state_gla'] = nrm((N_ODD, DEC_BATCH, GLA_HEADS, GLA_DK, GLA_DV), 1.0)
    inp['state_ffn_conv'] = nrm((DEPTH, DEC_BATCH, FFN_CONV - 1, 2 * D_FF), 1.0)
    perm = jax.random.permutation(next(ks), n_phys)
    inp['page_table'] = perm[:n_used].reshape(DEC_BATCH, n_pages).astype(jnp.int32)
    inp['w_in_even'] = nrm((N_EVEN, D_MODEL, EVEN_IN), D_MODEL ** -0.5)
    inp['w_out_even'] = nrm((N_EVEN, EVEN_OUT, D_MODEL), EVEN_OUT ** -0.5 * BETA)
    inp['nsa_cmp_w'] = (1.0 + nrm((N_EVEN, CMP_BLOCK, 2, NSA_KV_HEADS), 0.2)) * CMP_BLOCK ** -0.5
    inp['lru_conv_w'] = nrm((N_EVEN, SHORT_CONV, LRU_WIDTH), SHORT_CONV ** -0.5)
    inp['lru_conv_b'] = nrm((N_EVEN, LRU_WIDTH), 0.01)
    inp['lru_w_gates'] = nrm((N_EVEN, 2, LRU_BLOCKS, LRU_BLOCK_DIM, LRU_BLOCK_DIM), LRU_BLOCK_DIM ** -0.5)
    inp['lru_b_gates'] = nrm((N_EVEN, 2, LRU_WIDTH), 0.1)
    a_c = uni((N_EVEN, LRU_WIDTH), 0.9, 0.999) ** (1.0 / LRU_C)
    inp['lru_lambda'] = jnp.log(a_c) - jnp.log1p(-a_c)
    inp['w_in_odd'] = nrm((N_ODD, D_MODEL, ODD_IN), D_MODEL ** -0.5)
    inp['w_out_odd'] = nrm((N_ODD, ODD_OUT, D_MODEL), ODD_OUT ** -0.5 * BETA)
    inp['ssd_conv_w'] = nrm((N_ODD, SHORT_CONV, SSD_CONV_DIM), SHORT_CONV ** -0.5)
    inp['ssd_conv_b'] = nrm((N_ODD, SSD_CONV_DIM), 0.01)
    dt0 = jnp.exp(uni((N_ODD, SSD_HEADS), float(np.log(1e-3)), float(np.log(1e-1))))
    inp['ssd_dt_bias'] = dt0 + jnp.log(-jnp.expm1(-dt0))
    inp['ssd_a_log'] = jnp.log(uni((N_ODD, SSD_HEADS), 1.0, 16.0))
    inp['ssd_d'] = 1.0 + nrm((N_ODD, SSD_HEADS), 0.1)
    inp['ssd_norm_w'] = 1.0 + nrm((N_ODD, SSD_INNER), 0.1)
    inp['gla_w_alpha'] = nrm((N_ODD, GLA_RANK, GLA_HEADS * GLA_DK), GLA_RANK ** -0.5)
    inp['gla_b_alpha'] = nrm((N_ODD, GLA_HEADS * GLA_DK), 0.1)
    inp['gla_norm_w'] = 1.0 + nrm((N_ODD, GLA_DV), 0.1)
    inp['ffn_w_up'] = nrm((DEPTH, D_MODEL, 2 * D_FF), D_MODEL ** -0.5)
    inp['ffn_conv_w'] = nrm((DEPTH, FFN_CONV, 2 * D_FF), FFN_CONV ** -0.5)
    inp['ffn_conv_b'] = nrm((DEPTH, 2 * D_FF), 0.01)
    inp['ffn_w_down'] = nrm((DEPTH, D_FF, D_MODEL), D_FF ** -0.5 * BETA)
    inp['ln_mix_g'] = 1.0 + nrm((DEPTH, D_MODEL), 0.1)
    inp['ln_mix_b'] = nrm((DEPTH, D_MODEL), 0.02)
    inp['ln_ffn_g'] = 1.0 + nrm((DEPTH, D_MODEL), 0.1)
    inp['ln_ffn_b'] = nrm((DEPTH, D_MODEL), 0.02)
    return inp

def reference(x_prompt, x_sample, cache_nsa_kv, cache_nsa_win, state_lru_h, state_lru_conv, state_ssd,
              state_ssd_conv, state_gla, state_ffn_conv, page_table, w_in_even, w_out_even, nsa_cmp_w,
              lru_conv_w, lru_conv_b, lru_w_gates, lru_b_gates, lru_lambda, w_in_odd, w_out_odd, ssd_conv_w,
              ssd_conv_b, ssd_dt_bias, ssd_a_log, ssd_d, ssd_norm_w, gla_w_alpha, gla_b_alpha, gla_norm_w,
              ffn_w_up, ffn_conv_w, ffn_conv_b, ffn_w_down, ln_mix_g, ln_mix_b, ln_ffn_g, ln_ffn_b):
    p = dict(w_in_even=w_in_even, w_out_even=w_out_even, nsa_cmp_w=nsa_cmp_w, lru_conv_w=lru_conv_w,
             lru_conv_b=lru_conv_b, lru_w_gates=lru_w_gates, lru_b_gates=lru_b_gates, lru_lambda=lru_lambda,
             w_in_odd=w_in_odd, w_out_odd=w_out_odd, ssd_conv_w=ssd_conv_w, ssd_conv_b=ssd_conv_b,
             ssd_dt_bias=ssd_dt_bias, ssd_a_log=ssd_a_log, ssd_d=ssd_d, ssd_norm_w=ssd_norm_w,
             gla_w_alpha=gla_w_alpha, gla_b_alpha=gla_b_alpha, gla_norm_w=gla_norm_w, ffn_w_up=ffn_w_up,
             ffn_conv_w=ffn_conv_w, ffn_conv_b=ffn_conv_b, ffn_w_down=ffn_w_down, ln_mix_g=ln_mix_g,
             ln_mix_b=ln_mix_b, ln_ffn_g=ln_ffn_g, ln_ffn_b=ln_ffn_b)
    bp, tp = x_prompt.shape[0], x_prompt.shape[1]
    dtype = x_prompt.dtype

    def zeros(*shape):
        return jnp.zeros(shape, dtype)

    y_prompt, pr = trunk(
        x_prompt, lambda e: zeros(bp, 0, 4, NSA_KV_HEADS, HEAD_DIM),
        zeros(N_EVEN, bp, 0, 2, NSA_KV_HEADS, HEAD_DIM), min(WINDOW, tp),
        zeros(N_EVEN, bp, LRU_WIDTH), zeros(N_EVEN, bp, SHORT_CONV - 1, LRU_WIDTH),
        zeros(N_ODD, bp, SSD_HEADS, SSD_HEAD_DIM, SSD_STATE), zeros(N_ODD, bp, SHORT_CONV - 1, SSD_CONV_DIM),
        zeros(N_ODD, bp, GLA_HEADS, GLA_DK, GLA_DV), zeros(DEPTH, bp, FFN_CONV - 1, 2 * D_FF), p)
    bd = x_sample.shape[0]

    def past(e):
        return cache_nsa_kv[e][page_table].reshape(bd, -1, 4, NSA_KV_HEADS, HEAD_DIM)

    y_sample, sr = trunk(
        x_sample, past, cache_nsa_win, cache_nsa_win.shape[2], state_lru_h, state_lru_conv,
        state_ssd, state_ssd_conv, state_gla, state_ffn_conv, p)
    kv_p, win_p, lh_p, lc_p, ss_p, sc_p, g_p, f_p = pr
    kv_s, win_s, lh_s, lc_s, ss_s, sc_s, g_s, f_s = sr
    return (y_prompt, y_sample, kv_p, kv_s, win_p, win_s, lh_p, lh_s, lc_p, lc_s, ss_p, ss_s, sc_p, sc_s, g_p, g_s, f_p, f_s)


_drawn_inputs = setup_inputs


def setup_inputs(seed=0):
    import zlib

    import numpy as np

    out = dict(_drawn_inputs(seed))
    spreads = {}
    factors = {'nsa_cmp_w': 3.551, 'ssd_conv_b': 3.254, 'gla_norm_w': 4.692, 'ffn_conv_b': 8.0}
    for name, (base, spread) in spreads.items():
        noise = np.random.default_rng([zlib.crc32(name.encode()), seed]).standard_normal(out[name].shape)
        drawn = base * np.exp(spread * noise) if base else spread * noise
        out[name] = jnp.asarray(drawn.astype(out[name].dtype))
    for name, factor in factors.items():
        out[name] = (out[name] * factor).astype(out[name].dtype)
    return out
```

```python
from contextlib import ExitStack

import numpy as np
import concourse.bass as bass
from concourse import mybir

F32 = mybir.dt.float32
I32 = mybir.dt.int32
ALU = mybir.AluOpType
ACT = mybir.ActivationFunctionType
AX = mybir.AxisListType.X

P = 128
D = 1024
KD = D // P
TP, NB, TS = 512, 8, 8
NS = NB * TS
T = TP + NS
TT = 5
DH = 64
PAGES, PHYS = 4, 40
NEG = -1e30
LW = 512
DFF = 2816
FM = DFF // P
ALPHA = 4.0 ** 0.25
EPS = 1e-5
SCH = 128
GCH = 32
NH = 16


def tok(tt):
    n = P if tt < 4 else NS
    return slice(P * tt, P * tt + n), n


def constants():
    c = {}
    p = np.arange(P)
    c["ident"] = np.eye(P)
    c["ones"] = np.ones((P, P))
    inv = np.power(np.float32(500000.0), (-2.0 * np.arange(8, dtype=np.float32) / 16).astype(np.float32))
    pos = np.stack([(P * t + p) if t < 4 else (512 + p % TS) for t in range(TT)], 1).astype(np.float32)
    ang = (pos[:, :, None] * inv.astype(np.float32)).astype(np.float32).astype(np.float64)
    c["rope_c"] = np.concatenate([np.cos(ang), np.cos(ang)], -1)
    c["rope_s"] = np.concatenate([-np.sin(ang), np.sin(ang)], -1)
    c["causal"] = np.where(p[None, :] <= p[:, None], 0.0, NEG)
    n = np.arange(32)
    seen = np.stack([(16 * n[None, :] + 31 <= (P * t + p)[:, None]) & (n[None, :] < 31) for t in range(4)], 1)
    c["cmp_neg"] = np.where(seen, 0.0, NEG)
    c["cmp_01"] = seen * 1.0
    i = (P * np.arange(4)[None, :, None] + p[:, None, None]) - 16 * n[None, None, :]
    c["wc_lo"] = ((i >= 0) & (i < 16) & (n < 31)) * 1.0
    c["wc_hi"] = ((i >= 16) & (i < 32) & (n < 31)) * 1.0
    c["cmp_pad"] = np.broadcast_to(np.where(n < 31, 0.0, NEG), (P, 32))
    c["head4"] = (p[:, None] // 32 == np.arange(4)[None, :]) * 1.0
    b, j, t = p // 32, (p // 8) % 4, p % 8
    c["group"] = ((b[:, None] == b[None, :]) & (t[:, None] == t[None, :])) * 1.0
    kb, kt = np.arange(NS) // TS, np.arange(NS) % TS
    c["new_neg"] = np.stack([np.where((kb[None, :] == (4 * h + b)[:, None]) & (kt[None, :] <= t[:, None]), 0.0, NEG)
                             for h in range(2)], 1)
    c["win_neg"] = np.where(np.arange(8)[None, :] > t[:, None], 0.0, NEG)
    c["row_head"] = (j[:, None] == np.arange(4)[None, :]) * 1.0
    e = np.stack([(np.arange(NS)[:, None] == ((4 * h + b) * TS + t)[None, :]) for h in range(2)], 1) * 1.0
    c["expand"] = np.concatenate([e, np.zeros_like(e)], 0)
    c["blk_no"] = np.broadcast_to(np.arange(1.0, 7.0), (P, 6))
    col = np.arange(T)
    start = np.where(col < TP, col % SCH == 0, (col - TP) % TS == 0)
    c["ssd_keep"] = np.broadcast_to(1.0 - start, (P, T))
    start = np.where(col < TP, col % GCH == 0, (col - TP) % TS == 0)
    c["gla_keep"] = np.broadcast_to(1.0 - start, (P, T))
    c["upto"] = (p[:, None] <= p[None, :]) * 1.0
    s64 = ((kb[:, None] == kb[None, :]) & (kt[:, None] <= kt[None, :])) * 1.0
    c["upto_s"] = np.concatenate([s64, np.zeros_like(s64)], 0)
    c["upto_g"] = ((p[:, None] <= p[None, :]) & (p[:, None] // GCH == p[None, :] // GCH)) * 1.0
    c["of_b"] = np.concatenate([(kb[:, None] == np.arange(NB)[None, :]) * 1.0, np.zeros((64, NB))], 0)
    one = np.zeros((P, NH, P))
    for h in range(NH):
        one[h, h, :] = 1.0
    c["one_head"] = one
    two = np.zeros((P, 8, P))
    for k in range(8):
        two[2 * k, k, :64] = 1.0
        two[2 * k + 1, k, 64:] = 1.0
    c["two_heads"] = two
    return {k: np.ascontiguousarray(v, np.float32).reshape(P, -1) for k, v in c.items()}


EVEN_C = ["ident", "rope_c", "rope_s", "causal", "cmp_neg", "cmp_01", "wc_lo", "wc_hi", "cmp_pad", "head4",
          "group", "new_neg", "win_neg", "row_head", "expand", "blk_no"]
ODD_C = ["ident", "ones", "ssd_keep", "gla_keep", "upto", "upto_s", "upto_g", "of_b", "one_head", "two_heads"]


def pack(names):
    c = constants()
    return np.concatenate([c[n] for n in names], 1)


def unpack(tile, names):
    c, at, out = constants(), 0, {}
    for n in names:
        out[n] = tile[:, at:at + c[n].shape[1]]
        at += c[n].shape[1]
    return out


def split_free(ap, **dims):
    names = list(dims)
    return ap.rearrange(f"p ({' '.join(names)}) -> p {' '.join(names)}", **dims)


class Net:

    def __init__(self, nc, ctx, io):
        self.nc, self.ctx, self.io = nc, ctx, io
        self.n_sems = self.n_bufs = 0
        self.live = []
        self.stored, self.n_stored = nc.alloc_semaphore(name="stored"), 0
        self.ps = ctx.enter_context(nc.psum_tensor("ps", [P, 8, 512], F32))
        self.x = ctx.enter_context(self.buf("x", [P, KD, T]))
        self.ones = ctx.enter_context(self.buf("ones_t", [P, P]))

    def store(self, eng, dst, src):
        eng.dma_start(dst, src).then_inc(self.stored, 16)
        self.n_stored += 16

    def all_stored(self, eng):
        eng.wait_ge(self.stored, self.n_stored)

    def buf(self, name, shape, dtype=F32):
        self.n_bufs += 1
        return self.nc.sbuf_tensor(f"{name}_{self.n_bufs}", shape, dtype)

    def sem(self, name):
        self.n_sems += 1
        self.live.append(self.nc.alloc_semaphore(name=f"{name}_{self.n_sems}"))
        return self.live[-1]

    def recycle(self):
        self.nc.clear_and_free_semaphores(self.live)
        self.nc.all_engine_barrier()
        self.live = []

    def bank(self, b, parts=P):
        return self.ps[0:parts, b, :]


class Chain:

    def __init__(self, eng, sem):
        self.eng, self.sem, self.n = eng, sem, 0

    def __call__(self, ins):
        self.n += 1
        ins.then_inc(self.sem, 1)
        self.eng.wait_ge(self.sem, self.n)


def load_x(net):
    landed = net.sem("x_landed")
    with net.nc.Block() as block:
        @block.sync
        def _(sp):
            sp.dma_start(net.x[:], net.io["x"]).then_inc(landed, 16)
            sp.dma_start(net.ones[:], net.io["ones"]).then_inc(landed, 16)
            sp.wait_ge(landed, 32)


def even_project(net, qkv, gates, c):
    nc, io = net.nc, net.io
    NQ = [512, 512, 280]
    with ExitStack() as st:
        w = st.enter_context(net.buf("wq_ring", [P, 2, KD, 512]))
        ra = st.enter_context(net.buf("rope_a", [P, 4, 8, 16]))
        rb = st.enter_context(net.buf("rope_b", [P, 4, 8, 16]))
        w_landed = [net.sem("w_landed0"), net.sem("w_landed1")]
        chunk_done, prod, copied = net.sem("chunk_done"), net.sem("prod"), net.sem("copied")
        exp_done, order = net.sem("exp_done"), net.sem("order")
        with nc.Block() as block:
            @block.sync
            def _(sp):
                for i, n in enumerate(NQ):
                    if i >= 2:
                        sp.wait_ge(prod, TT * (i - 1))
                    sp.dma_start(w[:, i % 2, :, 0:n], io["w_even_tok"][:, :, 512 * i:512 * i + n]).then_inc(w_landed[i % 2], 16)

            @block.tensor
            def _(pe):
                u = 0
                for i, n in enumerate(NQ):
                    pe.wait_ge(w_landed[i % 2], 16 * (i // 2 + 1))
                    for tt in range(TT):
                        cols, m = tok(tt)
                        if u >= 4:
                            pe.wait_ge(copied, u - 3)
                        for k in range(KD):
                            mm = pe.matmul(net.ps[0:m, u % 4, 0:n], net.x[:, k, cols], w[:, i % 2, k, 0:n],
                                           start=(k == 0), stop=(k == KD - 1))
                        mm.then_inc(prod, 1)
                        u += 1

            @block.scalar
            def _(act):
                u = 0
                for i, n in enumerate(NQ):
                    for tt in range(TT):
                        _, m = tok(tt)
                        act.wait_ge(prod, u + 1)
                        act.activation(qkv[0:m, tt, 512 * i:512 * i + n], net.ps[0:m, u % 4, 0:n], ACT.Copy).then_inc(copied, 1)
                        u += 1
                act.wait_ge(copied, u)
                act.activation(gates[:, 0:4, :], qkv[:, 0:4, 1280:1304], ACT.Exp, scale=-1.0).then_inc(exp_done, 1)
                act.activation(gates[0:NS, 4, :], qkv[0:NS, 4, 1280:1304], ACT.Exp, scale=-1.0).then_inc(exp_done, 1)

            @block.vector
            def _(dve):
                link = Chain(dve, order)
                rc, rs = (split_free(c[n], t=TT, e=16) for n in ("rope_c", "rope_s"))

                def rope(parts, t0, nt, lo, heads):
                    x = qkv[0:parts, t0:t0 + nt, lo:lo + 64 * heads].rearrange("p t (h e) -> p t h e", e=64)
                    a, b = ra[0:parts, 0:nt, 0:heads, :], rb[0:parts, 0:nt, 0:heads, :]
                    cc = rc[0:parts, t0:t0 + nt, None, :].broadcast_to([parts, nt, heads, 16])
                    ss = rs[0:parts, t0:t0 + nt, None, :].broadcast_to([parts, nt, heads, 16])
                    dve.tensor_tensor(b[:, :, :, 0:8], x[:, :, :, 8:16], ss[:, :, :, 0:8], ALU.mult)
                    dve.tensor_tensor(b[:, :, :, 8:16], x[:, :, :, 0:8], ss[:, :, :, 8:16], ALU.mult)
                    link(dve.tensor_tensor(a, x[:, :, :, 0:16], cc, ALU.mult))
                    link(dve.tensor_tensor(x[:, :, :, 0:16], a, b, ALU.add))

                for parts, t0, nt in ((P, 0, 4), (NS, 4, 1)):
                    dve.wait_ge(copied, TT)
                    rope(parts, t0, nt, 0, 8)
                    dve.wait_ge(copied, 2 * TT)
                    rope(parts, t0, nt, 512, 2)
                    rope(parts, t0, nt, 768, 2)
                    dve.wait_ge(copied, 3 * TT)
                    rope(parts, t0, nt, 1024, 2)
                dve.wait_ge(exp_done, 2)
                for parts, g in ((P, gates[:, 0:4, :]), (NS, gates[0:NS, 4, :])):
                    link(dve.tensor_scalar(g, g, 1.0, None, ALU.add))
                    link(dve.reciprocal(g, g))


def even_rows_out(net, qkv, qT, kT, qTs, c):
    nc, io = net.nc, net.io
    turned, copied_q, copied_k = net.sem("turned"), net.sem("copied_q"), net.sem("copied_k")
    with nc.Block() as block:
        @block.sync
        def _(sp):
            n = 0
            for tt in range(4):
                net.store(sp, io["kv_p"][P * tt:P * tt + P, :], qkv[:, tt, 512:1024])
                net.store(sp, io["win_p"][P * tt:P * tt + P, :], qkv[:, tt, 1024:1280])
                n += 2
            net.store(sp, io["kv_s"], qkv[0:NS, 4, 512:1024])
            n += 1
            for b in range(NB):
                net.store(sp, io["win_s"][b, 504:512, :], qkv[TS * b:TS * b + TS, 4, 1024:1280])
                net.store(sp, io["win_s"][b, 0:504, :], io["win_tok"][b, 8:512, :])
                n += 2
            net.all_stored(sp)

        @block.tensor
        def _(pe):
            for tt in range(TT):
                _, m = tok(tt)
                if tt >= 2:
                    pe.wait_ge(copied_q, tt - 1)
                    pe.wait_ge(copied_k, tt - 1)
                for i, lo in enumerate([0, 128, 256, 384, 768, 1024]):
                    bank = (tt % 2) * 2 + (i >= 4)
                    mm = pe.transpose(net.ps[:, bank, (i % 4) * P:(i % 4) * P + m], qkv[0:m, tt, lo:lo + P], c["ident"][0:m, 0:m])
                mm.then_inc(turned, 1)

        @block.scalar
        def _(act):
            for tt in range(TT):
                cols, m = tok(tt)
                act.wait_ge(turned, tt + 1)
                src = split_free(net.bank((tt % 2) * 2), j=4, n=P)[:, :, 0:m]
                if tt == 4:
                    for j in range(4):
                        act.activation(qTs[:, :, j, :], src[:, j, :].rearrange("p (b t) -> p b t", t=TS), ACT.Copy, scale=DH ** -0.5)
                act.activation(qT[:, :, cols], src, ACT.Copy, scale=DH ** -0.5).then_inc(copied_q, 1)

        @block.vector
        def _(dve):
            for tt in range(TT):
                cols, m = tok(tt)
                dve.wait_ge(turned, tt + 1)
                dve.tensor_copy(kT[:, :, cols], split_free(net.bank((tt % 2) * 2 + 1), j=4, n=P)[:, 0:2, 0:m]).then_inc(copied_k, 1)


def compress_weights(net, wc, wv4, c, ce):
    nc = net.nc
    order = net.sem("order")
    landed = net.sem("landed")
    with nc.Block() as block:
        @block.sync
        def _(sp):
            sp.dma_start(ce[:], net.io["cmp_w"]).then_inc(landed, 16)

        @block.vector
        def _(dve):
            link = Chain(dve, order)
            dve.wait_ge(landed, 16)
            lo, hi = (split_free(c[n], t=4, n=32) for n in ("wc_lo", "wc_hi"))
            for q in range(4):
                link(dve.tensor_scalar(wc[:, q], lo, ce[:, q:q + 1], None, ALU.mult))
                link(dve.scalar_tensor_tensor(wc[:, q], hi, ce[:, 4 + q:5 + q], wc[:, q], ALU.mult, ALU.add))
            for i in range(4):
                dve.tensor_copy(wv4[:, :, :, i, :], wc[:, 2:4])


def prompt_compressed(net, qkv, gates, qT, wc, wv4, on, c):
    nc = net.nc
    with ExitStack() as st:
        sb = lambda n, s: st.enter_context(net.buf(n, s))
        ckT, cvd = sb("ckT", [P, 32]), sb("cvd", [P, 2, 4, DH])
        sc, mx, sm, pT = sb("sc", [P, 8, 32]), sb("mx", [P, 8]), sb("sm", [P, 8]), sb("pT", [P, 2, P])
        blocks, order, scored, centred = net.sem("blocks"), net.sem("order"), net.sem("scored"), net.sem("centred")
        exped, probs, turned, turned_in, summed = (net.sem(n) for n in ("exped", "probs", "turned", "turned_in", "summed"))
        kept = net.sem("kept")
        with nc.Block() as block:
            @block.tensor
            def _(pe):
                for h in range(2):
                    for tt in range(4):
                        pe.matmul(net.ps[64 * h:64 * h + 64, 0, 0:32], qkv[:, tt, 512 + 64 * h:576 + 64 * h], wc[:, h, tt, :],
                                  start=(tt == 0), stop=(tt == 3))
                for h in range(2):
                    for tt in range(4):
                        mm = pe.matmul(net.ps[:, 1, 64 * h:64 * h + 64], wv4[:, h, tt].rearrange("p i n -> p (i n)"),
                                       qkv[:, tt, 640 + 64 * h:704 + 64 * h], start=(tt == 0), stop=(tt == 3))
                mm.then_inc(blocks, 1)
                pe.wait_ge(kept, 1)
                for qt in range(4):
                    for h in range(2):
                        for j in range(4):
                            mm = pe.matmul(net.ps[:, 5 + h, 32 * j:32 * j + 32],
                                           qT[64 * h:64 * h + 64, j, P * qt:P * qt + P], ckT[64 * h:64 * h + 64, :], start=True, stop=True)
                    mm.then_inc(scored, 1)
                    pe.wait_ge(probs, qt + 1)
                    for h in range(2):
                        mm = pe.transpose(net.ps[:, 3, P * h:P * h + P], sc[:, 4 * h:4 * h + 4, :].rearrange("p j n -> p (j n)"), c["ident"])
                    mm.then_inc(turned, 1)
                    pe.wait_ge(turned_in, qt + 1)
                    for h in range(2):
                        mm = pe.matmul(net.ps[:, 4, 256 * h:256 * h + 256], pT[:, h, :], cvd[:, h].rearrange("p j d -> p (j d)"), start=True, stop=True)
                    mm.then_inc(summed, 1)

            @block.scalar
            def _(act):
                for qt in range(4):
                    act.wait_ge(centred, qt + 1)
                    act.activation(sc[:], sc[:], ACT.Exp).then_inc(exped, 1)
                    act.wait_ge(turned, qt + 1)
                    act.activation(pT[:], net.ps[:, 3, 0:256], ACT.Copy).then_inc(turned_in, 1)

            @block.vector
            def _(dve):
                link = Chain(dve, order)
                neg, keep = (split_free(c[n], t=4, n=32) for n in ("cmp_neg", "cmp_01"))
                dve.wait_ge(blocks, 1)
                dve.tensor_copy(ckT[:], net.ps[:, 0, 0:32])
                for h in range(2):
                    mm = dve.tensor_tensor(cvd[:, h], net.ps[:, 1, None, 64 * h:64 * h + 64].broadcast_to([P, 4, DH]),
                                           c["head4"][:, :, None].broadcast_to([P, 4, DH]), ALU.mult)
                mm.then_inc(kept, 1)
                g3 = gates.rearrange("p t (h j r) -> p t h j r", h=2, r=3)
                for qt in range(4):
                    s8 = net.ps[:, 5:7, 0:P].rearrange("p h (j n) -> p h j n", n=32)
                    dve.wait_ge(scored, qt + 1)
                    link(dve.tensor_tensor(sc[:].rearrange("p (h j) n -> p h j n", h=2), s8, neg[:, qt:qt + 1, None, :].broadcast_to([P, 2, 4, 32]), ALU.add))
                    link(dve.tensor_reduce(mx[:], sc[:], AX, ALU.max))
                    dve.tensor_tensor(sc[:], sc[:], mx[:, :, None].broadcast_to([P, 8, 32]), ALU.subtract).then_inc(centred, 1)
                    dve.wait_ge(exped, qt + 1)
                    link(dve.tensor_reduce(sm[:], sc[:], AX, ALU.add))
                    link(dve.reciprocal(sm[:], sm[:]))
                    link(dve.tensor_tensor(split_free(sm[:], h=2, j=4), split_free(sm[:], h=2, j=4), g3[:, qt, :, :, 0], ALU.mult))
                    link(dve.tensor_tensor(sc[:], sc[:], keep[:, qt:qt + 1, :].broadcast_to([P, 8, 32]), ALU.mult))
                    dve.tensor_tensor(sc[:], sc[:], sm[:, :, None].broadcast_to([P, 8, 32]), ALU.mult).then_inc(probs, 1)
                    dve.wait_ge(summed, qt + 1)
                    out = on[:, qt, :].rearrange("p (j h d) -> p h j d", j=4, h=2)
                    for h in range(2):
                        dve.tensor_copy(out[:, h], split_free(net.ps[:, 4, 256 * h:256 * h + 256], j=4, d=DH))


def prompt_attention(net, qkv, gates, qT, kT, on, c):
    nc = net.nc
    units = [(br, qt, j, h) for br in range(2) for qt in range(4) for j in range(4) for h in range(2)]
    N = len(units)
    with ExitStack() as st:
        sb = lambda n, s: st.enter_context(net.buf(n, s))
        probs, pT = sb("probs", [P, 2, 512]), sb("pT", [P, 2, 512])
        nmx, sums, tmp = sb("nmx", [P, 2]), sb("sums", [P, 2, 8]), sb("tmp", [P, 4, 2, DH])
        mx = sb("mxp", [P, 2])
        scored, maxed, exped, turned, turned_in, summed, added, order = (
            net.sem(n) for n in ("scored", "maxed", "exped", "turned", "turned_in", "summed", "added", "order"))
        with nc.Block() as block:
            @block.tensor
            def _(pe):
                def scores(u):
                    br, qt, j, h = units[u]
                    n = P * (qt + 1)
                    if u >= 2:
                        pe.wait_ge(exped, u - 1)
                    pe.matmul(net.ps[:, u % 2, 0:n], qT[64 * h:64 * h + 64, j, P * qt:P * qt + P],
                              kT[64 * h:64 * h + 64, br, 0:n], start=True, stop=True).then_inc(scored, 1)

                def turn(u):
                    br, qt, j, h = units[u]
                    pe.wait_ge(exped, u + 1)
                    if u >= 2:
                        pe.wait_ge(turned_in, u - 1)
                    for k in range(qt + 1):
                        mm = pe.transpose(net.ps[:, 2 + u % 2, P * k:P * k + P], probs[:, u % 2, P * k:P * k + P], c["ident"])
                    mm.then_inc(turned, 1)

                def weigh(u):
                    br, qt, j, h = units[u]
                    g = u // 8
                    pe.wait_ge(turned_in, u + 1)
                    if u % 8 == 0 and g >= 2:
                        pe.wait_ge(added, g - 1)
                    v0 = (896 if br == 0 else 1152) + 64 * h
                    for k in range(qt + 1):
                        mm = pe.matmul(net.ps[:, 4 + g % 2, 64 * (u % 8):64 * (u % 8) + 64], pT[:, u % 2, P * k:P * k + P],
                                       qkv[:, k, v0:v0 + 64], start=(k == 0), stop=(k == qt))
                    mm.then_inc(summed, 1)

                for i in range(N + 2):
                    if i < N:
                        scores(i)
                    if 1 <= i <= N:
                        turn(i - 1)
                    if i >= 2:
                        weigh(i - 2)

            @block.scalar
            def _(act):
                for i in range(N + 1):
                    if i < N:
                        br, qt, j, h = units[i]
                        n, g = P * (qt + 1), i // 8
                        act.wait_ge(maxed, i + 1)
                        if i >= 2:
                            act.wait_ge(turned, i - 1)
                        if i % 8 == 0 and g >= 2:
                            act.wait_ge(added, g - 1)
                        act.activation(probs[:, i % 2, 0:n], net.ps[:, i % 2, 0:n], ACT.Exp, bias=nmx[:, i % 2:i % 2 + 1],
                                       accum_out=sums[:, g % 2, i % 8:i % 8 + 1]).then_inc(exped, 1)
                    if i >= 1:
                        u = i - 1
                        n = P * (units[u][1] + 1)
                        act.wait_ge(turned, u + 1)
                        if u >= 2:
                            act.wait_ge(summed, u - 1)
                        act.activation(pT[:, u % 2, 0:n], net.ps[:, 2 + u % 2, 0:n], ACT.Copy).then_inc(turned_in, 1)

            @block.vector
            def _(dve):
                link = Chain(dve, order)
                g3 = gates.rearrange("p t (h j r) -> p t j h r", h=2, r=3)

                def add(g):
                    br, qt = units[8 * g][:2]
                    dve.wait_ge(summed, 8 * g + 8)
                    r = split_free(sums[:, g % 2, :], j=4, h=2)
                    link(dve.reciprocal(r, r))
                    link(dve.tensor_tensor(r, r, g3[:, qt, :, :, 1 + br], ALU.mult))
                    link(dve.tensor_tensor(tmp[:], net.ps[:, 4 + g % 2, :].rearrange("p (j h d) -> p j h d", j=4, h=2),
                                           r[:, :, :, None].broadcast_to([P, 4, 2, DH]), ALU.mult))
                    dve.tensor_tensor(on[:, qt, :], on[:, qt, :], tmp[:].rearrange("p j h d -> p (j h d)"), ALU.add).then_inc(added, 1)

                for u, (br, qt, j, h) in enumerate(units):
                    dve.wait_ge(scored, u + 1)
                    diag = net.ps[:, u % 2, P * qt:P * qt + P]
                    link(dve.tensor_tensor(diag, diag, c["causal"], ALU.add))
                    link(dve.tensor_reduce(mx[:, u % 2:u % 2 + 1], net.ps[:, u % 2, 0:P * qt + P], AX, ALU.max))
                    dve.tensor_scalar(nmx[:, u % 2:u % 2 + 1], mx[:, u % 2:u % 2 + 1], -1.0, None, ALU.mult).then_inc(maxed, 1)
                    if u >= 10 and u % 8 == 2:
                        add((u - 10) // 8)
                add(N // 8 - 1)


class Steps:

    def __init__(self, sem, names):
        self.sem, self.at = sem, {n: i + 1 for i, n in enumerate(names)}

    def after(self, eng, name):
        eng.wait_ge(self.sem, self.at[name])

    def done(self, ins):
        ins.then_inc(self.sem, 1)


def sample_attention(net, qkv, gates, kT, qTs, wc, cat, c):
    nc, io = net.nc, net.io
    names = []
    for half in range(2):
        names += [(half, "compressed"), (half, "kept")]
        for h in range(2):
            names += [(half, h, n) for n in ("c_scored", "c_centred", "c_exp", "c_probs", "c_turned", "c_pT", "c_out", "picked")]
            for br in range(2):
                names += [(half, h, br, n) for n in ("scored", "maxed", "exp", "turned", "pT", "out", "added")]
        names += [(half, "o_turned"), (half, "o_kept")]
    step = Steps(net.sem("steps_done"), names)
    with ExitStack() as st:
        sb = lambda n, s, d=F32: st.enter_context(net.buf(n, s, d))
        ids = sb("ids", [1, NB * PAGES], I32)
        kslc, kwin = sb("kslc", [P, 4, PAGES * P]), sb("kwin", [P, 4, 512])
        ptok, vwin = sb("ptok", [P, 4, PAGES, 3 * P]), sb("vwin", [P, 4, PAGES, P])
        ckT, cv = sb("ckTs", [P, 4, 32]), sb("cv", [32, 4, P])
        gx, grow = sb("gx", [P, 24]), sb("grow", [P, 2, 3])
        pc, imp = sb("pc", [P, 32]), sb("imp", [P, 8])
        cand, pick = sb("cand", [P, 6]), sb("pick", [P, 1])
        probs, pT = sb("probs", [P, T]), sb("pTs", [P, TT, P])
        nmx, row_sum, mx = sb("nmx", [P, 1]), sb("row_sum", [P, 1]), sb("mx1", [P, 1])
        so = sb("so", [P, 2, DH])
        ids_landed, past_landed, order = net.sem("ids_landed"), net.sem("past_landed"), net.sem("order")
        with nc.Block() as block:
            @block.sync
            def _(sp):
                sp.dma_start(ids[:], io["pages"]).then_inc(ids_landed, 16)
                sp.wait_ge(ids_landed, 16)
                for half in range(2):
                    if half:
                        step.after(sp, (0, "o_kept"))
                    for b in range(4):
                        for g in range(PAGES):
                            n = (4 * half + b) * PAGES + g
                            page = sp.value_load(ids[0:1, n:n + 1], min_val=0, max_val=PHYS - 1)
                            sp.dma_start(kslc[:, b, P * g:P * g + P], io["cache_kT"][bass.ds(page, 1), :, :].rearrange("a p t -> p (a t)")).then_inc(past_landed, 16)
                            sp.dma_start(ptok[:, b, g, :], io["cache_tok"][bass.ds(page, 1), :, :].rearrange("a p t -> p (a t)")).then_inc(past_landed, 16)
                        sp.dma_start(kwin[:, b, :], io["win_kT"][4 * half + b]).then_inc(past_landed, 16)
                        sp.dma_start(vwin[:, b], io["win_v"][4 * half + b]).then_inc(past_landed, 16)

            @block.tensor
            def _(pe):
                for half in range(2):
                    pe.wait_ge(past_landed, 16 * 40 * (half + 1))
                    if half:
                        step.after(pe, (0, "o_kept"))
                    for b in range(4):
                        for h in range(2):
                            for g in range(PAGES):
                                pe.matmul(net.ps[64 * h:64 * h + 64, 0, 32 * b:32 * b + 32], ptok[:, b, g, 64 * h:64 * h + 64],
                                          wc[:, h, g, :], start=(g == 0), stop=(g == 3))
                    for b in range(4):
                        for h in range(2):
                            for g in range(PAGES):
                                pe.matmul(net.ps[0:32, 1, P * b + 64 * h:P * b + 64 * h + 64], wc[:, 2 + h, g, :],
                                          ptok[:, b, g, P + 64 * h:P + 64 * h + 64], start=(g == 0), stop=(g == 3))
                    step.done(pe.matmul(net.ps[:, 2, 0:24], split_free(c["expand"], h=2, n=P)[0:NS, half, :], gates[0:NS, 4, :],
                                        start=True, stop=True))
                    step.after(pe, (half, "kept"))
                    for h in range(2):
                        rows = qTs[64 * h:64 * h + 64, 4 * half:4 * half + 4].rearrange("p b j t -> p (b j t)")
                        hp = slice(64 * h, 64 * h + 64)
                        if h:
                            step.after(pe, (half, 0, 1, "added"))
                        for b in range(4):
                            mm = pe.matmul(net.ps[32 * b:32 * b + 32, 0, 0:32], rows[:, 32 * b:32 * b + 32], ckT[hp, b, :], start=True, stop=True)
                        step.done(mm)
                        step.after(pe, (half, h, "c_probs"))
                        pe.matmul(net.ps[:, 1, 0:32], c["group"], pc[:], start=True, stop=True)
                        step.done(pe.transpose(net.ps[0:32, 2, 0:P], pc[:], c["ident"]))
                        step.after(pe, (half, h, "c_pT"))
                        for b in range(4):
                            mm = pe.matmul(net.ps[32 * b:32 * b + 32, 3, 0:64], pT[0:32, 0, 32 * b:32 * b + 32], cv[:, b, 64 * h:64 * h + 64], start=True, stop=True)
                        step.done(mm)
                        for br in range(2):
                            keys = (kslc, kwin)[br]
                            step.after(pe, (half, h, "picked") if br == 0 else (half, h, 0, "added"))
                            for b in range(4):
                                pe.matmul(net.ps[32 * b:32 * b + 32, 4, :], rows[:, 32 * b:32 * b + 32], keys[hp, b, :], start=True, stop=True)
                            step.done(pe.matmul(net.ps[:, 5, 0:NS], rows, kT[hp, br, TP:T], start=True, stop=True))
                            step.after(pe, (half, h, br, "exp"))
                            for g in range(PAGES):
                                pe.transpose(net.ps[:, 6, P * g:P * g + P], probs[:, P * g:P * g + P], c["ident"])
                            step.done(pe.transpose(net.ps[0:NS, 7, 0:P], probs[:, TP:T], c["ident"]))
                            step.after(pe, (half, h, br, "pT"))
                            for b in range(4):
                                out = net.ps[32 * b:32 * b + 32, 3, 0:64]
                                for g in range(PAGES):
                                    v = ptok[:, b, g, 2 * P + 64 * h:2 * P + 64 * h + 64] if br == 0 else vwin[:, b, g, 64 * h:64 * h + 64]
                                    pe.matmul(out, pT[:, g, 32 * b:32 * b + 32], v, start=(g == 0), stop=False)
                                v0 = (896 if br == 0 else 1152) + 64 * h
                                mm = pe.matmul(out, pT[0:NS, 4, 32 * b:32 * b + 32], qkv[0:NS, 4, v0:v0 + 64], start=False, stop=True)
                            step.done(mm)
                    step.after(pe, (half, 1, 1, "added"))
                    step.done(pe.transpose(net.ps[:, 0, 0:P], so[:].rearrange("p h d -> p (h d)"), c["ident"]))

            @block.scalar
            def _(act):
                for half in range(2):
                    for h in range(2):
                        step.after(act, (half, h, "c_centred"))
                        step.done(act.activation(pc[:], pc[:], ACT.Exp, accum_out=row_sum[:]))
                        step.after(act, (half, h, "c_turned"))
                        step.done(act.activation(pT[0:32, 0, :], net.ps[0:32, 2, 0:P], ACT.Copy))
                        for br in range(2):
                            step.after(act, (half, h, br, "maxed"))
                            step.done(act.activation(probs[:], net.ps[:, 4:6, :].rearrange("p a n -> p (a n)")[:, 0:T], ACT.Exp,
                                                     bias=nmx[:], accum_out=row_sum[:]))
                            step.after(act, (half, h, br, "turned"))
                            act.activation(pT[:, 0:4, :], split_free(net.bank(6), g=4, n=P), ACT.Copy)
                            step.done(act.activation(pT[0:NS, 4, :], net.ps[0:NS, 7, 0:P], ACT.Copy))
                    step.after(act, (half, "o_turned"))
                    o = split_free(net.ps[:, 0, 0:P], b=4, j=4, t=TS)
                    for j in range(4):
                        ins = act.activation(cat[:, j, TP + 32 * half:TP + 32 * half + 32].rearrange("p (b t) -> p b t", t=TS), o[:, :, j, :], ACT.Copy)
                    step.done(ins)

            @block.vector
            def _(dve):
                link = Chain(dve, order)
                neg_new = split_free(c["new_neg"], h=2, n=NS)
                for half in range(2):
                    step.after(dve, (half, "compressed"))
                    dve.tensor_copy(ckT[:], split_free(net.ps[:, 0, 0:P], b=4, n=32))
                    dve.tensor_copy(cv[:], split_free(net.ps[0:32, 1, :], b=4, n=P))
                    link(dve.tensor_tensor(split_free(gx[:], h=2, j=4, r=3), split_free(net.ps[:, 2, 0:24], h=2, j=4, r=3),
                                           c["row_head"][:, None, :, None].broadcast_to([P, 2, 4, 3]), ALU.mult))
                    step.done(dve.tensor_reduce(grow[:], gx[:].rearrange("p (h j r) -> p h r j", h=2, r=3), AX, ALU.add))
                    for h in range(2):
                        step.after(dve, (half, h, "c_scored"))
                        link(dve.tensor_tensor(pc[:], net.ps[:, 0, 0:32], c["cmp_pad"], ALU.add))
                        link(dve.tensor_reduce(mx[:], pc[:], AX, ALU.max))
                        step.done(dve.tensor_scalar(pc[:], pc[:], mx[:], None, ALU.subtract))
                        step.after(dve, (half, h, "c_exp"))
                        link(dve.reciprocal(row_sum[:], row_sum[:]))
                        step.done(dve.tensor_scalar(pc[:], pc[:], row_sum[:], None, ALU.mult))
                        step.after(dve, (half, h, "c_out"))
                        link(dve.tensor_scalar(so[:, h, :], net.ps[:, 3, 0:64], grow[:, h, 0:1], None, ALU.mult))
                        pg = split_free(net.ps[:, 1, 0:32], j=8, i=4)
                        link(dve.tensor_reduce(imp[:], pg[:, :, 0:3], AX, ALU.add))
                        link(dve.tensor_copy(probs[:, 0:32], net.ps[:, 1, 0:32]))
                        pg = split_free(probs[:, 0:32], j=8, i=4)
                        link(dve.scalar_tensor_tensor(cand[:], pg[:, 1:7, 3], 0.5, imp[:, 1:7], ALU.mult, ALU.add))
                        link(dve.scalar_tensor_tensor(cand[:], pg[:, 0:6, 3], 0.5, cand[:], ALU.mult, ALU.add))
                        link(dve.tensor_reduce(pick[:], cand[:], AX, ALU.min))
                        link(dve.tensor_scalar(cand[:], cand[:], pick[:], None, ALU.is_le))
                        link(dve.tensor_tensor(cand[:], cand[:], c["blk_no"], ALU.mult))
                        link(dve.tensor_reduce(pick[:], cand[:], AX, ALU.max))
                        step.done(dve.tensor_scalar(cand[:], c["blk_no"], pick[:], NEG, ALU.is_equal, ALU.mult))
                        for br in range(2):
                            step.after(dve, (half, h, br, "scored"))
                            if br == 0:
                                s = split_free(net.ps[:, 4, 64:448], j=6, n=64)
                                link(dve.tensor_tensor(s, s, cand[:, :, None].broadcast_to([P, 6, 64]), ALU.add))
                            else:
                                link(dve.tensor_tensor(net.ps[:, 4, 0:8], net.ps[:, 4, 0:8], c["win_neg"], ALU.add))
                            link(dve.tensor_tensor(net.ps[:, 5, 0:NS], net.ps[:, 5, 0:NS], neg_new[:, half, :], ALU.add))
                            link(dve.tensor_reduce(mx[:], net.ps[:, 4:6, :].rearrange("p a n -> p (a n)")[:, 0:T], AX, ALU.max))
                            step.done(dve.tensor_scalar(nmx[:], mx[:], -1.0, None, ALU.mult))
                            step.after(dve, (half, h, br, "out"))
                            link(dve.reciprocal(row_sum[:], row_sum[:]))
                            link(dve.tensor_tensor(row_sum[:], row_sum[:], grow[:, h, 1 + br:2 + br], ALU.mult))
                            step.done(dve.scalar_tensor_tensor(so[:, h, :], net.ps[:, 3, 0:64], row_sum[:], so[:, h, :], ALU.mult, ALU.add))


def turn_outputs(net, on, cat, c):
    turned, copied = net.sem("turned"), net.sem("copied")
    with net.nc.Block() as block:
        @block.tensor
        def _(pe):
            for qt in range(4):
                for j in range(4):
                    mm = pe.transpose(net.ps[:, qt, P * j:P * j + P], on[:, qt, P * j:P * j + P], c["ident"])
                mm.then_inc(turned, 1)

        @block.scalar
        def _(act):
            for qt in range(4):
                act.wait_ge(turned, qt + 1)
                act.activation(cat[:, 0:4, P * qt:P * qt + P], split_free(net.bank(qt), j=4, n=P), ACT.Copy).then_inc(copied, 1)


def products(net, pe, out_bank, w, x, kt, m=P):
    for lo, hi, b in ((0, TP, out_bank), (TP, T, out_bank + 1)):
        for k in range(kt):
            mm = pe.matmul(net.ps[0:m, b, 0:hi - lo], w[:, k, :], x[:, k, lo:hi], start=(k == 0), stop=(k == kt - 1))
    return mm


def both(net, b, m=P):
    return net.ps[0:m, b:b + 2, :].rearrange("p a n -> p (a n)")[:, 0:T]


def conv_cols(taps):
    h = taps - 1
    return h + TP + NB * (h + TS)


def conv_parts(buf, taps):
    h = taps - 1
    s = buf[:, h + TP:].rearrange("p (b n) -> p b n", n=h + TS)
    return buf[:, h:h + TP], s[:, :, h:], s[:, :, 0:h], buf[:, TP:TP + h], s[:, :, TS:]


def conv_out_parts(buf, taps):
    h = taps - 1
    s = buf[:, h + TP:]
    return buf[:, 0:TP], [s[:, (h + TS) * b:(h + TS) * b + TS] for b in range(NB)]


def tokens_of(buf, taps):
    h = taps - 1
    return buf[:, 0:TP], buf[:, h + TP:].rearrange("p (b n) -> p b n", n=h + TS)[:, :, 0:TS]


def tok3(ap):
    return ap[:, TP:T].rearrange("p (b t) -> p b t", t=TS)


def lru(net, cat):
    nc, io = net.nc, net.io
    CC = conv_cols(4)
    SC = TP + NB * (1 + TS)
    with ExitStack() as st:
        sb = lambda n, s: st.enter_context(net.buf(n, s))
        w = sb("w_ring", [P, 4, KD, P])
        hx, xc = sb("hx", [P, 4, CC]), sb("xc", [P, 4, CC])
        gg, wg = sb("gelu_g", [P, 4, T]), sb("wg", [P, 8, P])
        small = sb("small", [P, 4, 8])
        hist, h0 = sb("hist", [P, 4, NB, 3]), sb("h0", [P, 4, NB])
        rg, ig, la = sb("rg", [P, 2, T]), sb("ig", [P, 2, T]), sb("la", [P, 2, T])
        a, u, hh = sb("a", [P, 4, SC]), sb("u", [P, 4, SC]), sb("hh", [P, 4, SC])
        sp8, tmp4 = sb("sp8", [P, 4]), sb("tmp4", [P, 4, 4])
        tails = sb("tails", [P, 4, 27])
        hlast = sb("hlast", [P, 4, 9])
        w_landed = [net.sem(f"w_landed{i}") for i in range(4)]
        (small_landed, prod, copied, conved, gated, gates_out, stepped, gelued, order, act_order, sqrts, tanhs, halo, lam1, lam2, prep) = (
            net.sem(n) for n in ("small_landed", "prod", "copied", "conved", "gated", "gates_out", "stepped", "gelued", "order",
                                 "act_order", "sqrts", "tanhs", "halo", "lam1", "lam2", "prep"))
        with nc.Block() as block:
            @block.sync
            def _(sp):
                for dst, name in ((small, "lru_small"), (hist, "lru_hist"), (h0, "lru_h0"), (wg, "lru_wg")):
                    sp.dma_start(dst[:], io[name]).then_inc(small_landed, 16)
                for m in range(8):
                    if m >= 4:
                        sp.wait_ge(prod, m - 3)
                    sp.dma_start(w[:, m % 4], io["w_lru"][m]).then_inc(w_landed[m % 4], 16)

            @block.gpsimd
            def _(pool):
                pool.wait_ge(small_landed, 64)
                for i in range(4):
                    p_tok, s_tok, s_hist, _, _ = conv_parts(hx[:, i, :], 4)
                    pool.memset(hx[:, i, 0:3], 0.0)
                    pool.tensor_copy(s_hist, hist[:, i])
                    pool.memset(a[:, i, TP:].rearrange("p (b n) -> p b n", n=1 + TS)[:, :, 0:1], 0.0)
                    ins = pool.tensor_copy(u[:, i, TP:].rearrange("p (b n) -> p b n", n=1 + TS)[:, :, 0], h0[:, i])
                ins.then_inc(halo, 1)

            @block.tensor
            def _(pe):
                for m in range(8):
                    pe.wait_ge(w_landed[m % 4], 16 * (m // 4 + 1))
                    if m >= 2:
                        pe.wait_ge(copied, m - 1)
                    products(net, pe, 2 * (m % 2), w[:, m % 4], net.x, KD).then_inc(prod, 1)
                pe.wait_ge(small_landed, 64)
                for i in range(4):
                    pe.wait_ge(conved, i + 1)
                    if i:
                        pe.wait_ge(gates_out, i)
                    for g in range(2):
                        pe.matmul(net.ps[:, 4 + 2 * g, :], wg[:, 4 * g + i, :], xc[:, i, 0:TP], start=True, stop=True)
                        mm = pe.matmul(net.ps[:, 5 + 2 * g, 0:NS], wg[:, 4 * g + i, :], tokens_of(xc[:, i, :], 4)[1], start=True, stop=True)
                    mm.then_inc(gated, 1)

            @block.scalar
            def _(act):
                act.wait_ge(small_landed, 64)
                act.wait_ge(halo, 1)
                for m in range(8):
                    act.wait_ge(prod, m + 1)
                    b = 2 * (m % 2)
                    if m < 4:
                        p_tok, s_tok, *_ = conv_parts(hx[:, m, :], 4)
                        act.activation(p_tok, net.bank(b), ACT.Copy)
                        act.activation(s_tok, split_free(net.ps[:, b + 1, 0:NS], b=NB, t=TS), ACT.Copy).then_inc(copied, 1)
                    else:
                        act.activation(gg[:, m - 4, :], both(net, b), ACT.Gelu_apprx_tanh).then_inc(copied, 1)
                act.wait_ge(lam1, 1)
                act.activation(tmp4[:, 1, :], tmp4[:, 0, :], ACT.Exp, scale=-1.0).then_inc(lam2, 1)
                for i in range(4):
                    act.wait_ge(gated, i + 1)
                    if i >= 2:
                        act.wait_ge(stepped, i - 1)
                    act.activation(rg[:, i % 2, :], both(net, 4), ACT.Sigmoid, bias=small[:, i, 5:6])
                    act.activation(ig[:, i % 2, :], both(net, 6), ACT.Sigmoid, bias=small[:, i, 6:7]).then_inc(gates_out, 1)
                    act.wait_ge(prep, i + 1)
                    av = a[:, i, TP:].rearrange("p (b n) -> p b n", n=1 + TS)[:, :, 1:]
                    act.activation(a[:, i, 0:TP], la[:, i % 2, 0:TP], ACT.Exp)
                    act.activation(av, tok3(la[:, i % 2, :]), ACT.Exp)
                    act.activation(rg[:, i % 2, :], la[:, i % 2, :], ACT.Tanh).then_inc(tanhs, 1)
                    act.wait_ge(sqrts, 2 * i + 1)
                    act.activation(la[:, i % 2, :], rg[:, i % 2, :], ACT.Sqrt).then_inc(sqrts, 1)

            @block.vector
            def _(dve):
                link = Chain(dve, order)
                dve.wait_ge(small_landed, 64)
                lam = small[:, :, 7]
                link(dve.scalar_tensor_tensor(tmp4[:, 0, :], lam, -1.0, lam, ALU.mult, ALU.max))
                dve.tensor_scalar(tmp4[:, 2, :], lam, -1.0, 0.0, ALU.mult, ALU.max).then_inc(lam1, 1)
                for i in range(4):
                    dve.wait_ge(copied, i + 1)
                    n = CC - 3
                    link(dve.tensor_scalar(xc[:, i, 0:n], hx[:, i, 0:n], small[:, i, 0:1], small[:, i, 4:5], ALU.mult, ALU.add))
                    for k in range(1, 4):
                        ins = dve.scalar_tensor_tensor(xc[:, i, 0:n], hx[:, i, k:k + n], small[:, i, k:k + 1], xc[:, i, 0:n], ALU.mult, ALU.add)
                        if k < 3:
                            link(ins)
                        else:
                            ins.then_inc(conved, 1)
                    *_, p_tail, s_tail = conv_parts(hx[:, i, :], 4)
                    link(dve.tensor_copy(tails[:, i, 0:3], p_tail))
                    link(dve.tensor_copy(tails[:, i, 3:27].rearrange("p (b n) -> p b n", n=3), s_tail))
                dve.wait_ge(lam2, 1)
                log1p(dve, link, tmp4[:, 1, :], tmp4[:, 0, :], tmp4[:, 3, :], sp8[:])
                link(dve.tensor_tensor(sp8[:], sp8[:], tmp4[:, 2, :], ALU.add))
                link(dve.tensor_scalar(sp8[:], sp8[:], -8.0, None, ALU.mult))
                dve.wait_ge(conved, 4)
                for i in range(4):
                    xp, xs = tokens_of(xc[:, i, :], 4)
                    uv = u[:, i, TP:].rearrange("p (b n) -> p b n", n=1 + TS)[:, :, 1:]
                    dve.wait_ge(gates_out, i + 1)
                    dve.tensor_scalar(la[:, i % 2, :], rg[:, i % 2, :], sp8[:, i:i + 1], None, ALU.mult).then_inc(prep, 1)
                    dve.wait_ge(tanhs, i + 1)
                    th, t2 = rg[:, i % 2, :], ig[:, i % 2, :]
                    link(dve.tensor_scalar(la[:, i % 2, :], th, -1.0, 1.0, ALU.mult, ALU.add))
                    link(dve.reciprocal(la[:, i % 2, :], la[:, i % 2, :]))
                    dve.scalar_tensor_tensor(th, th, -2.0, la[:, i % 2, :], ALU.mult, ALU.mult).then_inc(sqrts, 1)
                    link(dve.tensor_tensor(u[:, i, 0:TP], t2[:, 0:TP], xp, ALU.mult))
                    link(dve.tensor_tensor(uv, tok3(t2), xs, ALU.mult))
                    dve.wait_ge(sqrts, 2 * i + 2)
                    link(dve.tensor_tensor(u[:, i, 0:TP], u[:, i, 0:TP], la[:, i % 2, 0:TP], ALU.mult))
                    link(dve.tensor_tensor(uv, uv, tok3(la[:, i % 2, :]), ALU.mult))
                    dve.tensor_tensor_scan(hh[:, i, :], a[:, i, :], u[:, i, :], 0.0, ALU.mult, ALU.add).then_inc(stepped, 1)
                    dve.wait_ge(stepped, i + 1)
                    hv = hh[:, i, TP:].rearrange("p (b n) -> p b n", n=1 + TS)
                    link(dve.tensor_copy(hlast[:, i, 0:1], hh[:, i, TP - 1:TP]))
                    link(dve.tensor_copy(hlast[:, i, 1:9], hv[:, :, TS]))
                    dve.wait_ge(copied, 5 + i)
                    link(dve.tensor_tensor(cat[:, 4 + i, 0:TP], hh[:, i, 0:TP], gg[:, i, 0:TP], ALU.mult))
                    link(dve.tensor_tensor(tok3(cat[:, 4 + i, :]), hv[:, :, 1:], tok3(gg[:, i, :]), ALU.mult))
        with nc.Block() as block:
            @block.sync
            def _(sp):
                net.store(sp, io["lru_tails"], tails[:])
                net.store(sp, io["lru_hlast"], hlast[:])
                net.all_stored(sp)


def log1p(dve, link, e, w, w2, out):
    link(dve.tensor_scalar(w2, e, 2.0, None, ALU.add))
    link(dve.reciprocal(w2, w2))
    link(dve.tensor_tensor(w, e, w2, ALU.mult))
    link(dve.tensor_tensor(w2, w, w, ALU.mult))
    link(dve.tensor_scalar(out, w2, 1.0 / 15, None, ALU.mult))
    for k in (13, 11, 9, 7, 5, 3):
        link(dve.scalar_tensor_tensor(out, out, 1.0 / k, w2, ALU.add, ALU.mult))
    link(dve.scalar_tensor_tensor(out, out, 1.0, w, ALU.add, ALU.mult))
    link(dve.tensor_scalar(out, out, 2.0, None, ALU.mult))


def project_and_norm(net, name, w_name, src, kt, ln_name, gb_index):
    nc, io = net.nc, net.io
    with ExitStack() as st:
        sb = lambda n, s: st.enter_context(net.buf(n, s))
        w = sb("w_ring", [P, 2, kt, P])
        gb = sb("ln_gb", [P, 2, KD])
        sq = sb("sq", [P, 2, T])
        w_landed = [net.sem("w_landed0"), net.sem("w_landed1")]
        gb_landed, prod, z_done, order = net.sem("gb_landed"), net.sem("prod"), net.sem("z_done"), net.sem("order")
        summed, centred, squared, var_done, rstd_done, root = (net.sem(n) for n in ("summed", "centred", "squared", "var_done", "rstd_done", "root"))
        mean, rstd = sb("mean", [P, T]), sb("rstd", [P, T])
        with nc.Block() as block:
            @block.sync
            def _(sp):
                sp.dma_start(gb[:], io[ln_name][gb_index]).then_inc(gb_landed, 16)
                for m in range(KD):
                    if m >= 2:
                        sp.wait_ge(prod, m - 1)
                    sp.dma_start(w[:, m % 2], io[w_name][m]).then_inc(w_landed[m % 2], 16)

            @block.tensor
            def _(pe):
                for m in range(KD):
                    pe.wait_ge(w_landed[m % 2], 16 * (m // 2 + 1))
                    if m >= 2:
                        pe.wait_ge(z_done, m - 1)
                    products(net, pe, 2 * (m % 2), w[:, m % 2], src, kt).then_inc(prod, 1)
                for k in range(KD):
                    pe.wait_ge(z_done, k + 1)
                    pe.matmul(net.ps[:, 4, :], net.ones[:], net.x[:, k, 0:TP], start=(k == 0), stop=(k == KD - 1), skip_group_check=True)
                    mm = pe.matmul(net.ps[:, 5, 0:NS], net.ones[:], net.x[:, k, TP:T], start=(k == 0), stop=(k == KD - 1), skip_group_check=True)
                mm.then_inc(summed, 1)
                for k in range(KD):
                    pe.wait_ge(squared, k + 1)
                    pe.matmul(net.ps[:, 6, :], net.ones[:], sq[:, k % 2, 0:TP], start=(k == 0), stop=(k == KD - 1), skip_group_check=True)
                    mm = pe.matmul(net.ps[:, 7, 0:NS], net.ones[:], sq[:, k % 2, TP:T], start=(k == 0), stop=(k == KD - 1), skip_group_check=True)
                    mm.then_inc(var_done, 1)

            @block.scalar
            def _(act):
                for k in range(KD):
                    act.wait_ge(centred, k + 1)
                    if k >= 2:
                        act.wait_ge(var_done, k - 1)
                    act.activation(sq[:, k % 2, :], net.x[:, k, :], ACT.Square).then_inc(squared, 1)
                act.wait_ge(root, 1)
                act.activation(rstd[:], rstd[:], ACT.Sqrt).then_inc(root, 1)

            @block.vector
            def _(dve):
                link = Chain(dve, order)
                for m in range(KD):
                    dve.wait_ge(prod, m + 1)
                    dve.scalar_tensor_tensor(net.x[:, m, :], net.x[:, m, :], ALPHA, both(net, 2 * (m % 2)), ALU.mult, ALU.add).then_inc(z_done, 1)
                dve.wait_ge(summed, 1)
                link(dve.tensor_scalar(mean[:], both(net, 4), 1.0 / D, None, ALU.mult))
                for k in range(KD):
                    dve.tensor_tensor(net.x[:, k, :], net.x[:, k, :], mean[:], ALU.subtract).then_inc(centred, 1)
                dve.wait_ge(var_done, KD)
                dve.tensor_scalar(rstd[:], both(net, 6), 1.0 / D, EPS, ALU.mult, ALU.add).then_inc(root, 1)
                dve.wait_ge(root, 2)
                link(dve.reciprocal(rstd[:], rstd[:]))
                dve.wait_ge(gb_landed, 16)
                for k in range(KD):
                    link(dve.tensor_tensor(net.x[:, k, :], net.x[:, k, :], rstd[:], ALU.mult))
                    link(dve.tensor_scalar(net.x[:, k, :], net.x[:, k, :], gb[:, 0, k:k + 1], gb[:, 1, k:k + 1], ALU.mult, ALU.add))


def ffn(net, layer):
    nc, io = net.nc, net.io
    CC = conv_cols(3)
    N = CC - 2
    with ExitStack() as st:
        sb = lambda n, s: st.enter_context(net.buf(n, s))
        g = sb("g", [P, FM, T])
        with ExitStack() as up:
            sb = lambda n, s: up.enter_context(net.buf(n, s))
            w = sb("w_ring", [P, 4, KD, P])
            ub, uc = sb("ub", [P, 4, CC]), sb("uc", [P, 4, CC])
            par = sb("ffn_par", [P, 2 * FM, 4])
            hist = sb("ffn_hist", [P, 2 * FM, NB, 2])
            tails = sb("ffn_tails", [P, 2 * FM, 18])
            w_landed = [net.sem(f"w_landed{i}") for i in range(4)]
            small_landed, halo, prod, copied, conved, gelued, order, made, tailed, zeroed = (
                net.sem(n) for n in ("small_landed", "halo", "prod", "copied", "conved", "gelued", "order", "made", "tailed", "zeroed"))
            with nc.Block() as block:
                @block.sync
                def _(sp):
                    sp.dma_start(par[:], io["ffn_par"][layer]).then_inc(small_landed, 16)
                    sp.dma_start(hist[:], io["ffn_hist"][layer]).then_inc(small_landed, 16)
                    for m in range(2 * FM):
                        if m >= 4:
                            sp.wait_ge(prod, m - 3)
                        sp.dma_start(w[:, m % 4], io["w_up"][layer, m]).then_inc(w_landed[m % 4], 16)

                @block.gpsimd
                def _(pool):
                    pool.memset(ub[:, :, 0:2], 0.0).then_inc(zeroed, 1)
                    pool.wait_ge(small_landed, 32)
                    for m in range(2 * FM + 4):
                        if m >= 4:
                            pool.wait_ge(copied, m - 3)
                            *_, p_tail, s_tail = conv_parts(ub[:, m % 4, :], 3)
                            pool.tensor_copy(tails[:, m - 4, 0:2], p_tail).then_inc(tailed, 1)
                            pool.tensor_copy(tails[:, m - 4, 2:18].rearrange("p (b n) -> p b n", n=2), s_tail).then_inc(tailed, 1)
                            pool.wait_ge(conved, m - 3)
                        if m < 2 * FM:
                            pool.tensor_copy(conv_parts(ub[:, m % 4, :], 3)[2], hist[:, m]).then_inc(halo, 1)

                @block.tensor
                def _(pe):
                    for m in range(2 * FM):
                        pe.wait_ge(w_landed[m % 4], 16 * (m // 4 + 1))
                        if m >= 4:
                            pe.wait_ge(copied, m - 3)
                        products(net, pe, 2 * (m % 4), w[:, m % 4], net.x, KD).then_inc(prod, 1)

                @block.scalar
                def _(act):
                    def gelu(m):
                        act.wait_ge(conved, m + 1)
                        act.activation(uc[:, m % 4, 0:N], uc[:, m % 4, 0:N], ACT.Gelu_apprx_tanh).then_inc(gelued, 1)

                    act.wait_ge(zeroed, 1)
                    for m in range(2 * FM):
                        p_tok, s_tok, *_ = conv_parts(ub[:, m % 4, :], 3)
                        act.wait_ge(prod, m + 1)
                        act.wait_ge(halo, m + 1)
                        act.activation(p_tok, net.bank(2 * (m % 4)), ACT.Copy)
                        act.activation(s_tok, split_free(net.ps[:, 2 * (m % 4) + 1, 0:NS], b=NB, t=TS), ACT.Copy).then_inc(copied, 1)
                        if m % 2 and m > 2:
                            gelu(m - 3)
                    gelu(2 * FM - 2)

                @block.vector
                def _(dve):
                    link = Chain(dve, order)

                    def conv(m):
                        s, x, y = m % 4, ub[:, m % 4, :], uc[:, m % 4, :]
                        dve.wait_ge(copied, m + 1)
                        if m >= 4:
                            dve.wait_ge(made, (m - 4) // 2 + 1)
                        link(dve.tensor_scalar(y[:, 0:N], x[:, 0:N], par[:, m, 0:1], par[:, m, 3:4], ALU.mult, ALU.add))
                        link(dve.scalar_tensor_tensor(y[:, 0:N], x[:, 1:1 + N], par[:, m, 1:2], y[:, 0:N], ALU.mult, ALU.add))
                        dve.scalar_tensor_tensor(y[:, 0:N], x[:, 2:2 + N], par[:, m, 2:3], y[:, 0:N], ALU.mult, ALU.add).then_inc(conved, 1)

                    def make(i):
                        gp, gs = tokens_of(uc[:, (2 * i) % 4, :], 3)
                        vp, vs = tokens_of(uc[:, (2 * i + 1) % 4, :], 3)
                        dve.wait_ge(gelued, i + 1)
                        dve.wait_ge(conved, 2 * i + 2)
                        dve.tensor_tensor(g[:, i, 0:TP], gp, vp, ALU.mult)
                        dve.tensor_tensor(tok3(g[:, i, :]), gs, vs, ALU.mult).then_inc(made, 1)

                    dve.wait_ge(small_landed, 32)
                    for i in range(FM):
                        conv(2 * i)
                        if i:
                            make(i - 1)
                        conv(2 * i + 1)
                    make(FM - 1)

            with nc.Block() as block:
                @block.sync
                def _(sp):
                    net.store(sp, io["ffn_tails"][layer], tails[:])
                    net.all_stored(sp)
        project_and_norm(net, "down", f"w_down{layer}", g, FM, "ln_ffn", layer)


def odd_mixer(net, cat):
    nc, io = net.nc, net.io
    CC = conv_cols(4)
    N = CC - 3
    with ExitStack() as st:
        sb = lambda n, s: st.enter_context(net.buf(n, s))
        cpk = sb("odd_consts", [P, pack(ODD_C).shape[1]])
        c = unpack(cpk, ODD_C)
        zt = sb("zt", [P, 8, T])
        xbc = sb("xbc", [P, 12, T])
        small = sb("odd_small", [P, 48])
        dtr = sb("dtr", [NH, T])
        with ExitStack() as gla_st:
            qk = cat
            vtok, ga = None, None
            vtok = gla_st.enter_context(net.buf("vtok", [P, TT, 512]))
            ga = gla_st.enter_context(net.buf("ga", [16, T]))
            odd_project(net, cpk, small, zt, xbc, dtr, ga, vtok, qk)
            gla(net, c, small, ga, vtok, qk)
        ssd(net, c, small, zt, xbc, dtr, cat)


def odd_project(net, cpk, small, zt, xbc, dtr, ga, vtok, qk):
    nc, io = net.nc, net.io
    CC = conv_cols(4)
    N = CC - 3
    M = 32
    with ExitStack() as st:
        sb = lambda n, s: st.enter_context(net.buf(n, s))
        w = sb("w_ring", [P, 4, KD, P])
        wv = w[:].rearrange("p s k m -> p (s k m)").rearrange("p (k n) -> p k n", k=KD)
        w16 = sb("w16", [P, KD, 32])
        ub = sb("ub", [P, 2, CC])
        uc = sb("uc", [P, 2, CC])
        par, hist, tails = sb("conv_par", [P, 12, 5]), sb("conv_hist", [P, 12, NB, 3]), sb("conv_tails", [P, 12, 27])
        w_landed = [net.sem(f"w_landed{i}") for i in range(4)]
        small_landed, prod, copied, conved, order, halo, silued, wv_landed = (
            net.sem(n) for n in ("small_landed", "prod", "copied", "conved", "order", "halo", "silued", "wv_landed"))
        with nc.Block() as block:
            @block.sync
            def _(sp):
                loads = ((par, "ssd_conv_par"), (hist, "ssd_hist"), (cpk, "odd_consts"), (small, "odd_small"), (w16, "w_odd16"))
                for dst, name in loads:
                    sp.dma_start(dst[:], io[name]).then_inc(small_landed, 16)
                for m in range(M):
                    if m >= 4:
                        sp.wait_ge(prod, m - 3)
                    sp.dma_start(w[:, m % 4], io["w_odd"][m]).then_inc(w_landed[m % 4], 16)
                sp.wait_ge(prod, M)
                sp.dma_start(wv, io["w_v"]).then_inc(wv_landed, 16)

            @block.tensor
            def _(pe):
                for m in range(M):
                    pe.wait_ge(w_landed[m % 4], 16 * (m // 4 + 1))
                    if m >= 2:
                        pe.wait_ge(copied, m - 1)
                    products(net, pe, 2 * (m % 2), w[:, m % 4], net.x, KD).then_inc(prod, 1)
                pe.wait_ge(small_landed, 80)
                for i in range(2):
                    products(net, pe, 4 + 2 * i, w16[:, :, 16 * i:16 * i + 16], net.x, KD, 16).then_inc(prod, 1)
                pe.wait_ge(wv_landed, 16)
                pe.wait_ge(copied, M)
                for tt in range(TT):
                    cols, m = tok(tt)
                    if tt >= 4:
                        pe.wait_ge(copied, M + 2 + tt - 3)
                    for k in range(KD):
                        mm = pe.matmul(net.ps[0:m, tt % 4, :], net.x[:, k, cols], wv[:, k, :], start=(k == 0), stop=(k == KD - 1))
                    mm.then_inc(prod, 1)

            @block.gpsimd
            def _(pool):
                pool.wait_ge(small_landed, 80)
                pool.memset(ub[:, :, 0:3], 0.0)
                for m in range(12):
                    if m >= 2:
                        pool.wait_ge(conved, 2 * (m - 1))
                    pool.tensor_copy(conv_parts(ub[:, m % 2, :], 4)[2], hist[:, m]).then_inc(halo, 1)

            @block.scalar
            def _(act):
                def silu_conv(m):
                    act.wait_ge(conved, 2 * m + 2)
                    yp, ys = tokens_of(uc[:, m % 2, :], 4)
                    act.activation(xbc[:, m, 0:TP], yp, ACT.Silu)
                    act.activation(tok3(xbc[:, m, :]), ys, ACT.Silu).then_inc(silued, 1)

                for m in range(M):
                    b = 2 * (m % 2)
                    act.wait_ge(prod, m + 1)
                    if m < 12:
                        act.wait_ge(halo, m + 1)
                        p_tok, s_tok, *_ = conv_parts(ub[:, m % 2, :], 4)
                        act.activation(p_tok, net.bank(b), ACT.Copy)
                        act.activation(s_tok, split_free(net.ps[:, b + 1, 0:NS], b=NB, t=TS), ACT.Copy).then_inc(copied, 1)
                        if m:
                            silu_conv(m - 1)
                        continue
                    if m == 12:
                        silu_conv(11)
                    if m < 20:
                        act.activation(zt[:, m - 12, :], both(net, b), ACT.Silu).then_inc(copied, 1)
                    elif m < 24:
                        act.activation(qk[:, 8 + m - 20, :], both(net, b), ACT.Silu).then_inc(copied, 1)
                    else:
                        act.activation(qk[:, m - 24, :], both(net, b), ACT.Copy, scale=P ** -0.5 if m < 28 else 1.0).then_inc(copied, 1)
                act.wait_ge(prod, M + 2)
                act.activation(dtr[:], both(net, 4, 16), ACT.Copy).then_inc(copied, 1)
                act.activation(ga[:], both(net, 6, 16), ACT.Copy).then_inc(copied, 1)
                for tt in range(TT):
                    _, m = tok(tt)
                    act.wait_ge(prod, M + 3 + tt)
                    act.activation(vtok[0:m, tt, :], net.ps[0:m, tt % 4, :], ACT.Copy).then_inc(copied, 1)

            @block.vector
            def _(dve):
                link = Chain(dve, order)
                dve.wait_ge(small_landed, 80)
                for m in range(12):
                    x, y = ub[:, m % 2, :], uc[:, m % 2, :]
                    dve.wait_ge(copied, m + 1)
                    if m >= 2:
                        dve.wait_ge(silued, m - 1)
                    link(dve.tensor_scalar(y[:, 0:N], x[:, 0:N], par[:, m, 0:1], par[:, m, 4:5], ALU.mult, ALU.add))
                    for k in range(1, 4):
                        ins = dve.scalar_tensor_tensor(y[:, 0:N], x[:, k:k + N], par[:, m, k:k + 1], y[:, 0:N], ALU.mult, ALU.add)
                        if k < 3:
                            link(ins)
                        else:
                            ins.then_inc(conved, 1)
                    *_, p_tail, s_tail = conv_parts(x, 4)
                    link(dve.tensor_copy(tails[:, m, 0:3], p_tail))
                    dve.tensor_copy(tails[:, m, 3:27].rearrange("p (b n) -> p b n", n=3), s_tail).then_inc(conved, 1)
        with nc.Block() as block:
            @block.sync
            def _(sp):
                net.store(sp, io["ssd_tails"], tails[:])
                net.all_stored(sp)


def gla(net, c, small, ga, vtok, qk):
    nc, io = net.nc, net.io
    H = 4
    NC = TP // GCH
    b_al = small[:, 36:40]
    with ExitStack() as st:
        sb = lambda n, s: st.enter_context(net.buf(n, s))
        la, cum, ke = sb("la", [P, H, T]), sb("cum", [P, H, T]), sb("ke", [P, H, T])
        dec = sb("dec", [P, H, NC + NB])
        wa = sb("w_alpha", [16, 512])
        kdt = sb("kdt", [P, TT, 512])
        kdm = sb("kdm", [NS, 2, 512])
        sp_, ss = sb("s_p", [P, H, P]), sb("s_s", [P, NB, H, P])
        att = sb("att", [P, 2, H, P])
        q, k, gg = qk[:, 0:4, :], qk[:, 4:8, :], qk[:, 8:12, :]
        o = la
        step = Steps(net.sem("steps_done"), ["alpha", "biased", "abs", "logs", "cum", "exp_up", "q_done", "exp_down",
                                             "k_done", "left", "exp_left", "kd_done", "turned", "kdt_done"])
        small_landed, order, act_order = net.sem("small_landed"), net.sem("order"), net.sem("act_order")
        state_landed = net.sem("state_landed")

        def ends(ap):
            return ap[:, :, GCH - 1:TP:GCH], ap[:, :, TP + TS - 1:T:TS]

        def chunks(ap):
            return (ap[:, :, 0:TP].rearrange("p h (c n) -> p h c n", n=GCH), ap[:, :, TP:T].rearrange("p h (c n) -> p h c n", n=TS))

        with nc.Block() as block:
            @block.sync
            def _(sp):
                sp.dma_start(wa[:], io["w_alpha"]).then_inc(small_landed, 16)
                sp.dma_start(ss[:], io["gla_s0"]).then_inc(state_landed, 16)
                sp.wait_ge(state_landed, 16)

            @block.tensor
            def _(pe):
                pe.wait_ge(small_landed, 16)
                for h in range(H):
                    pe.matmul(net.ps[:, 2 * h, :], wa[:, P * h:P * h + P], ga[:, 0:TP], start=True, stop=True)
                    mm = pe.matmul(net.ps[:, 2 * h + 1, 0:NS], wa[:, P * h:P * h + P], ga[:, TP:T], start=True, stop=True)
                step.done(mm)
                step.after(pe, "kd_done")
                for tt in range(TT):
                    cols, m = tok(tt)
                    for h in range(H):
                        mm = pe.transpose(net.ps[0:m, tt, P * h:P * h + P], k[:, h, cols], c["ident"])
                step.done(mm)

            @block.scalar
            def _(act):
                step.after(act, "alpha")
                for h in range(H):
                    ins = act.activation(la[:, h, :], both(net, 2 * h), ACT.Identity, bias=b_al[:, h:h + 1])
                step.done(ins)
                step.after(act, "abs")
                act.activation(cum[:], cum[:], ACT.Exp, scale=-1.0).then_inc(act_order, 1)
                act.wait_ge(act_order, 1)
                step.done(act.activation(cum[:], cum[:], ACT.Ln, bias=1.0))
                step.after(act, "cum")
                for e, d in zip(ends(cum), (dec[:, :, 0:NC], dec[:, :, NC:])):
                    act.activation(d, e, ACT.Exp, scale=1.0 / 16)
                step.done(act.activation(la[:], cum[:], ACT.Exp, scale=1.0 / 16))
                step.after(act, "q_done")
                step.done(act.activation(ke[:], cum[:], ACT.Exp, scale=-1.0 / 16))
                step.after(act, "left")
                step.done(act.activation(la[:], la[:], ACT.Exp, scale=1.0 / 16))
                step.after(act, "turned")
                for tt in range(TT):
                    _, m = tok(tt)
                    ins = act.activation(kdt[0:m, tt, :], net.ps[0:m, tt, :], ACT.Copy)
                step.done(ins)

            @block.vector
            def _(dve):
                link = Chain(dve, order)
                step.after(dve, "biased")
                step.done(dve.scalar_tensor_tensor(cum[:], la[:], -1.0, la[:], ALU.mult, ALU.max))
                step.after(dve, "logs")
                link(dve.scalar_tensor_tensor(la[:], la[:], 0.0, cum[:], ALU.min, ALU.subtract))
                for h in range(H):
                    ins = dve.tensor_tensor_scan(cum[:, h, :], c["gla_keep"], la[:, h, :], 0.0, ALU.mult, ALU.add)
                step.done(ins)
                step.after(dve, "exp_up")
                step.done(dve.tensor_tensor(q, q, la[:], ALU.mult))
                step.after(dve, "exp_down")
                step.done(dve.tensor_tensor(ke[:], ke[:], k, ALU.mult))
                step.after(dve, "k_done")
                for (x, e, y, n, w) in zip(chunks(cum), ends(cum), chunks(la), (NC, NB), (GCH, TS)):
                    for h in range(H):
                        ins = dve.tensor_tensor(y[:, h], e[:, h, :, None].broadcast_to([P, n, w]), x[:, h], ALU.subtract)
                step.done(ins)
                step.after(dve, "exp_left")
                step.done(dve.tensor_tensor(k, k, la[:], ALU.mult))

        scored, masked, o_done, o_kept, inter_done, kv_done, stepped, kdm_done, kv_used = (
            net.sem(n) for n in ("scored", "masked", "o_done", "o_kept", "inter_done", "kv_done", "stepped", "kdm_done", "kv_used"))
        zeroed, squared, normed, root, rms_used, order, made = (net.sem(n) for n in ("zeroed", "squared", "normed", "root", "rms_used", "order", "made"))
        A, O, KV = (0, 1), (2, 3), (4, 5)
        with nc.Block() as block:
            @block.tensor
            def _(pe):
                pe.wait_ge(zeroed, 1)
                n = 0
                for tt in range(TT):
                    cols, m = tok(tt)
                    if tt >= 2:
                        pe.wait_ge(masked, tt - 1)
                    for h in range(H):
                        mm = pe.matmul(net.ps[0:m, A[tt % 2], P * h:P * h + m], ke[:, h, cols], q[:, h, cols], start=True, stop=True)
                    mm.then_inc(scored, 1)
                    pe.wait_ge(masked, tt + 1)
                    if tt >= 2:
                        pe.wait_ge(o_kept, tt - 1)
                    for h in range(H):
                        pe.matmul(net.ps[:, O[tt % 2], P * h:P * h + m], vtok[0:m, tt, P * h:P * h + P], att[0:m, tt % 2, h, 0:m],
                                  start=(h == 0), stop=False, skip_group_check=True)
                    for ch in range(4 if tt < 4 else NB):
                        lo, w = (GCH * ch, GCH) if tt < 4 else (TS * ch, TS)
                        if n >= 2:
                            pe.wait_ge(kv_used, n - 1)
                        if tt == 4:
                            pe.wait_ge(kdm_done, ch + 1)
                        for h in range(H):
                            if tt < 4:
                                lhs, rhs = kdt[lo:lo + w, tt, P * h:P * h + P], vtok[lo:lo + w, tt, P * h:P * h + P]
                            else:
                                lhs, rhs = kdm[:, ch % 2, P * h:P * h + P], vtok[0:NS, 4, P * h:P * h + P]
                            mm = pe.matmul(net.ps[:, KV[n % 2], P * h:P * h + P], lhs, rhs, start=True, stop=True)
                        mm.then_inc(kv_done, 1)
                        if tt < 4:
                            pe.wait_ge(kv_used, n)
                        for h in range(H):
                            s = sp_[:, h, :] if tt < 4 else ss[:, ch, h, :]
                            mm = pe.matmul(net.ps[:, O[tt % 2], P * h + lo:P * h + lo + w], s, q[:, h, cols.start + lo:cols.start + lo + w],
                                           start=False, stop=(h == H - 1 and ch == (3 if tt < 4 else NB - 1)), skip_group_check=True)
                        mm.then_inc(inter_done, 1)
                        n += 1
                for h in range(H):
                    pe.wait_ge(squared, h + 1)
                    if h >= 2:
                        pe.wait_ge(rms_used, h - 1)
                    pe.matmul(net.ps[:, 6, :] if h % 2 else net.ps[:, 0, :], net.ones[:], ke[:, h, 0:TP], start=True, stop=True)
                    pe.matmul(net.ps[:, 7, 0:NS] if h % 2 else net.ps[:, 1, 0:NS], net.ones[:], ke[:, h, TP:T], start=True, stop=True).then_inc(normed, 1)

            @block.scalar
            def _(act):
                for tt in range(TT):
                    cols, m = tok(tt)
                    act.wait_ge(inter_done, 4 * (tt + 1) if tt < 4 else 16 + NB)
                    act.activation(o[:, :, cols], split_free(net.bank(O[tt % 2]), h=H, n=P)[:, :, 0:m], ACT.Copy).then_inc(o_kept, 1)
                act.wait_ge(o_kept, TT)
                for h in range(H):
                    act.activation(ke[:, h, :], o[:, h, :], ACT.Square).then_inc(squared, 1)
                for h in range(H):
                    act.wait_ge(rms_used, h + 1)
                    act.activation(cum[:, h, :], cum[:, h, :], ACT.Sqrt).then_inc(root, 1)

            @block.gpsimd
            def _(pool):
                for b in range(NB):
                    if b >= 2:
                        pool.wait_ge(kv_done, 16 + b - 1)
                    pool.tensor_scalar(kdm[:, b % 2, :], kdt[0:NS, 4, :], c["of_b"][0:NS, b:b + 1], 1.0, ALU.mult, ALU.mult).then_inc(kdm_done, 1)

            @block.vector
            def _(dve):
                link = Chain(dve, order)
                dve.memset(sp_[:], 0.0).then_inc(zeroed, 1)
                n = 0
                for tt in range(TT):
                    cols, m = tok(tt)
                    mask = (c["upto_g"] if tt < 4 else c["upto_s"])[0:m, None, 0:m].broadcast_to([m, H, m])
                    dve.wait_ge(scored, tt + 1)
                    dve.tensor_tensor(att[0:m, tt % 2, :, 0:m], split_free(net.ps[0:m, A[tt % 2], :], h=H, n=P)[:, :, 0:m], mask, ALU.mult).then_inc(masked, 1)
                    for ch in range(4 if tt < 4 else NB):
                        dve.wait_ge(kv_done, n + 1)
                        dve.wait_ge(inter_done, n + 1)
                        if n == 0:
                            dve.wait_ge(zeroed, 1)
                        elif tt < 4:
                            dve.wait_ge(kv_used, n)
                        for h in range(H):
                            s = sp_[:, h, :] if tt < 4 else ss[:, ch, h, :]
                            ins = dve.scalar_tensor_tensor(s, s, dec[:, h, n:n + 1], net.ps[:, KV[n % 2], P * h:P * h + P], ALU.mult, ALU.add)
                        ins.then_inc(kv_used, 1)
                        n += 1
                dve.wait_ge(squared, H)
                for h in range(H):
                    dve.wait_ge(normed, h + 1)
                    dve.tensor_scalar(cum[:, h, :], both(net, 6 if h % 2 else 0), 1.0 / P, EPS, ALU.mult, ALU.add).then_inc(rms_used, 1)
                for h in range(H):
                    dve.wait_ge(root, h + 1)
                    link(dve.reciprocal(cum[:, h, :], cum[:, h, :]))
                    link(dve.scalar_tensor_tensor(gg[:, h, :], gg[:, h, :], small[:, 35:36], o[:, h, :], ALU.mult, ALU.mult))
                    link(dve.tensor_tensor(gg[:, h, :], gg[:, h, :], cum[:, h, :], ALU.mult))

            @block.sync
            def _(sp):
                sp.wait_ge(kv_used, 16 + NB)
                net.store(sp, io["gla_s_p"], sp_[:])
                net.store(sp, io["gla_s_s"], ss[:])
                net.all_stored(sp)


def ssd(net, c, small, zt, xbc, dtr, cat):
    nc, io = net.nc, net.io
    NC = 4
    with ExitStack() as st:
        sb = lambda n, s: st.enter_context(net.buf(n, s))
        dt, cum, dtd, w, w2, e = (sb(n, [NH, T]) for n in ("dt", "cumA", "dtd", "w", "w2", "e"))
        na, al, diag = sb("na", [NH, 1]), sb("al", [NH, NC + NB]), sb("diag", [NH, NH, NC + NB])
        DL = sb("DL", [P, NH, NC + NB])
        per = sb("per_tok", [P, TT, 3, NH])
        EA = sb("EA", [P, 8, T])
        hs_p, hs_s = sb("hs_p", [P, 1024]), sb("hs_s", [P, NB, 1024])
        xdt, xdd, bt = sb("xdt", [P, 1024]), sb("xdd", [P, 1024]), sb("bt", [P, 2, P])
        btm = sb("btm", [NS, 2, 2, P])
        L = sb("L", [P, 2, 4, P])
        tmp = sb("tmp", [P, 4, P])
        names = ["biased", "e_done", "left", "exp_left", "diag_done", "DL_sum", "DL_done", "turned", "per_done"]
        names += [(j, n) for j in range(8) for n in ("EA_sum", "EA_done")]
        step = Steps(net.sem("steps_done"), names)
        order, act_order, state_landed = net.sem("order"), net.sem("act_order"), net.sem("state_landed")
        with nc.Block() as block:
            @block.sync
            def _(sp):
                sp.dma_start(hs_s[:], io["ssd_h0"]).then_inc(state_landed, 16)
                sp.wait_ge(state_landed, 16)

            @block.vector
            def _(dve):
                link = Chain(dve, order)
                link(dve.tensor_scalar(dtr[:], dtr[:], small[0:NH, 0:1], None, ALU.add))
                step.done(dve.scalar_tensor_tensor(e[:], dtr[:], -1.0, dtr[:], ALU.mult, ALU.max))
                step.after(dve, "e_done")
                log1p(dve, link, e[:], w[:], w2[:], dt[:])
                link(dve.scalar_tensor_tensor(dt[:], dtr[:], 0.0, dt[:], ALU.max, ALU.add))
                link(dve.tensor_scalar(w[:], dt[:], na[:], -1.0, ALU.mult, ALU.mult))
                link(dve.tensor_tensor_scan(cum[:], c["ssd_keep"][0:NH, :], w[:], 0.0, ALU.mult, ALU.add))
                link(dve.tensor_copy(al[:, 0:NC], cum[:, SCH - 1:TP:SCH]))
                link(dve.tensor_copy(al[:, NC:], cum[:, TP + TS - 1:T:TS]))
                dve.tensor_tensor(w2[:, 0:TP].rearrange("p (c n) -> p c n", n=SCH), al[:, 0:NC, None].broadcast_to([NH, NC, SCH]),
                                  cum[:, 0:TP].rearrange("p (c n) -> p c n", n=SCH), ALU.subtract)
                step.done(dve.tensor_tensor(tok3(w2[:]), al[:, NC:, None].broadcast_to([NH, NB, TS]), tok3(cum[:]), ALU.subtract))
                step.after(dve, "exp_left")
                dve.tensor_tensor(dtd[:], dt[:], w2[:], ALU.mult)
                step.done(dve.tensor_tensor(diag[:], c["ident"][0:NH, 0:NH, None].broadcast_to([NH, NH, NC + NB]),
                                            al[:, None, :].broadcast_to([NH, NH, NC + NB]), ALU.mult))
                step.after(dve, "turned")
                v = split_free(net.ps[:, 1, 0:240], t=TT, q=3, h=NH)
                dve.tensor_copy(per[:, 0:4], v[:, 0:4])
                step.done(dve.tensor_copy(per[0:NS, 4], v[0:NS, 4]))

            @block.scalar
            def _(act):
                act.activation(na[:], small[0:NH, 1:2], ACT.Exp)
                step.after(act, "biased")
                step.done(act.activation(e[:], e[:], ACT.Exp, scale=-1.0))
                step.after(act, "left")
                step.done(act.activation(w2[:], w2[:], ACT.Exp))
                step.after(act, "DL_sum")
                step.done(act.activation(DL[:].rearrange("p h c -> p (h c)"), net.ps[:, 0, 0:192], ACT.Exp))
                for j in range(8):
                    step.after(act, (j, "EA_sum"))
                    step.done(act.activation(EA[:, j, :], both(net, 2 + 2 * (j % 2)), ACT.Exp))

            @block.tensor
            def _(pe):
                step.after(pe, "diag_done")
                step.done(pe.matmul(net.ps[:, 0, 0:192], net.ones[0:NH, :], diag[:].rearrange("p h c -> p (h c)"), start=True, stop=True))
                step.after(pe, "DL_done")
                for tt in range(TT):
                    cols, m = tok(tt)
                    for i, src in enumerate((cum, dt, dtd)):
                        mm = pe.transpose(net.ps[0:m, 1, 48 * tt + 16 * i:48 * tt + 16 * i + 16], src[:, cols], c["ident"][0:NH, 0:NH])
                step.done(mm)
                for j in range(8):
                    step.after(pe, "per_done" if j == 0 else (j - 1, "EA_done"))
                    lhs, b = split_free(c["two_heads"], j=8, n=P)[0:NH, j, :], 2 + 2 * (j % 2)
                    pe.matmul(net.ps[:, b, :], lhs, cum[:, 0:TP], start=True, stop=True)
                    step.done(pe.matmul(net.ps[:, b + 1, 0:NS], lhs, cum[:, TP:T], start=True, stop=True))

        names = []
        for tt in range(TT):
            names += [(tt, n) for n in ("turned", "scaled", "b_kept", "cb", "cb_masked")]
            for g in range(2):
                for u in range(2):
                    names += [(tt, g, u, n) for n in ("decays", "clamped", "exp", "mixed", "y")]
                names += [(tt, g, "off"), (tt, g, "y_sum")]
            for g in range(2):
                names += [(tt, g, n) for n in ("kv", "state")] if tt < 4 else []
        for b in range(NB):
            names += [(4, "b", b, "masked")]
            for g in range(2):
                names += [(4, "b", b, g, "kv"), (4, "b", b, g, "state")]
        step2 = Steps(net.sem("steps_done"), names)
        zeroed, order = net.sem("zeroed"), net.sem("order")
        with nc.Block() as block:
            @block.tensor
            def _(pe):
                pe.wait_ge(zeroed, 1)
                for tt in range(TT):
                    cols, m = tok(tt)
                    if tt:
                        step2.after(pe, (tt - 1, 1, "state"))
                    for i in range(10):
                        mm = pe.transpose(net.ps[0:m, i // 4, (i % 4) * P:(i % 4) * P + P], xbc[:, i, cols], c["ident"])
                    step2.done(mm)
                    step2.after(pe, (tt, "b_kept"))
                    for g in range(2):
                        mm = pe.matmul(net.ps[0:m, 3, P * g:P * g + m], xbc[:, 8 + g, cols], xbc[:, 10 + g, cols], start=True, stop=True)
                    step2.done(mm)
                    for g in range(2):
                        for u in range(2):
                            step2.after(pe, (tt, "cb_masked") if (g, u) == (0, 0) else ((tt, 0, "y_sum") if u == 0 else (tt, g, 0, "y")))
                            for i in range(4):
                                hd = 8 * g + 4 * u + i
                                mm = pe.matmul(net.ps[0:m, 4, P * i:P * i + m], split_free(c["one_head"], h=NH, n=P)[0:NH, hd, 0:m], cum[:, cols],
                                               start=True, stop=True)
                            step2.done(mm)
                            step2.after(pe, (tt, g, u, "mixed"))
                            for i in range(4):
                                hd = 4 * u + i
                                lo = 64 * (hd % 2)
                                mm = pe.matmul(net.ps[lo:lo + 64, 6, P * (hd // 2):P * (hd // 2) + m], xdt[0:m, 512 * g + 64 * hd:512 * g + 64 * hd + 64],
                                               L[0:m, 1, i, 0:m], start=True, stop=True)
                            step2.done(mm)
                        for j in range(4):
                            f = 512 * g + P * j
                            if tt < 4:
                                mm = pe.matmul(net.ps[:, 7, P * j:P * j + P], hs_p[:, f:f + P], xbc[:, 10 + g, cols], start=True, stop=True)
                            else:
                                for b in range(NB):
                                    mm = pe.matmul(net.ps[:, 7, P * j + TS * b:P * j + TS * b + TS], hs_s[:, b, f:f + P],
                                                   xbc[:, 10 + g, TP + TS * b:TP + TS * b + TS], start=True, stop=True)
                        step2.done(mm)
                    if tt < 4:
                        for g in range(2):
                            step2.after(pe, (tt, 1, "y_sum") if g == 0 else (tt, 0, "state"))
                            step2.done(pe.matmul(net.ps[:, g, :], bt[0:m, g, :], xdd[0:m, 512 * g:512 * g + 512], start=True, stop=True))
                for b in range(NB):
                    for g in range(2):
                        step2.after(pe, (4, "b", b, "masked") if g == 0 else (4, "b", b, 0, "state"))
                        step2.done(pe.matmul(net.ps[:, g, :], btm[:, b % 2, g, :], xdd[0:NS, 512 * g:512 * g + 512], start=True, stop=True))

            @block.scalar
            def _(act):
                for tt in range(TT):
                    cols, m = tok(tt)
                    step2.after(act, (tt, "scaled"))
                    step2.done(act.activation(bt[0:m, :, :], split_free(net.ps[0:m, 2, 0:256], g=2, n=P), ACT.Copy))
                    for g in range(2):
                        for u in range(2):
                            step2.after(act, (tt, g, u, "clamped"))
                            step2.done(act.activation(L[0:m, 0, :, 0:m], L[0:m, 0, :, 0:m], ACT.Exp))

            @block.vector
            def _(dve):
                link = Chain(dve, order)
                dve.memset(hs_p[:], 0.0).then_inc(zeroed, 1)
                for tt in range(TT):
                    cols, m = tok(tt)
                    step2.after(dve, (tt, "turned"))
                    for g in range(2):
                        x = split_free(net.ps[0:m, g, :], h=8, n=64)
                        for q, dst in ((1, xdt), (2, xdd)):
                            ins = dve.tensor_tensor(split_free(dst[0:m, 512 * g:512 * g + 512], h=8, n=64), x,
                                                    per[0:m, tt, q, 8 * g:8 * g + 8, None].broadcast_to([m, 8, 64]), ALU.mult)
                    step2.done(ins)
                    step2.after(dve, (tt, "cb"))
                    cb = split_free(net.ps[0:m, 3, 0:256], g=2, n=P)[:, :, 0:m]
                    mask = (c["upto"] if tt < 4 else c["upto_s"])[0:m, None, 0:m].broadcast_to([m, 2, m])
                    step2.done(dve.tensor_tensor(cb, cb, mask, ALU.mult))
                    for g in range(2):
                        for u in range(2):
                            step2.after(dve, (tt, g, u, "decays"))
                            a0 = 8 * g + 4 * u
                            d = split_free(net.ps[0:m, 4, :], h=4, n=P)[:, :, 0:m]
                            link(dve.tensor_tensor(L[0:m, 0, :, 0:m], d, per[0:m, tt, 0, a0:a0 + 4, None].broadcast_to([m, 4, m]), ALU.subtract))
                            step2.done(dve.tensor_scalar(L[0:m, 0, :, 0:m], L[0:m, 0, :, 0:m], 0.0, None, ALU.min))
                            step2.after(dve, (tt, g, u, "exp"))
                            step2.done(dve.tensor_tensor(L[0:m, 1, :, 0:m], L[0:m, 0, :, 0:m], cb[:, g:g + 1, :].broadcast_to([m, 4, m]), ALU.mult))
                        step2.after(dve, (tt, g, "off"))
                        link(dve.tensor_tensor(tmp[:, :, 0:m], split_free(net.bank(7), j=4, n=P)[:, :, 0:m], EA[:, 4 * g:4 * g + 4, cols], ALU.mult))
                        step2.done(dve.tensor_tensor(cat[:, 4 * g:4 * g + 4, cols], split_free(net.bank(6), j=4, n=P)[:, :, 0:m], tmp[:, :, 0:m], ALU.add))
                    if tt < 4:
                        for g in range(2):
                            step2.after(dve, (tt, g, "kv"))
                            s = split_free(hs_p[:, 512 * g:512 * g + 512], h=8, n=64)
                            link(dve.tensor_tensor(s, s, DL[:, 8 * g:8 * g + 8, tt:tt + 1].broadcast_to([P, 8, 64]), ALU.mult))
                            step2.done(dve.tensor_tensor(hs_p[:, 512 * g:512 * g + 512], hs_p[:, 512 * g:512 * g + 512], net.ps[:, g, :], ALU.add))
                step2.after(dve, (4, 1, "y_sum"))
                for b in range(NB):
                    if b:
                        step2.after(dve, (4, "b", b - 1, 1, "state"))
                    step2.done(dve.tensor_scalar(btm[:, b % 2], bt[0:NS], c["of_b"][0:NS, b:b + 1], None, ALU.mult))
                    for g in range(2):
                        step2.after(dve, (4, "b", b, g, "kv"))
                        f = slice(512 * g, 512 * g + 512)
                        s = split_free(hs_s[:, b, f], h=8, n=64)
                        link(dve.tensor_tensor(s, s, DL[:, 8 * g:8 * g + 8, 4 + b:5 + b].broadcast_to([P, 8, 64]), ALU.mult))
                        step2.done(dve.tensor_tensor(hs_s[:, b, f], hs_s[:, b, f], net.ps[:, g, :], ALU.add))

            @block.sync
            def _(sp):
                step2.after(sp, (4, "b", NB - 1, 1, "state"))
                net.store(sp, io["ssd_s_p"], hs_p[:])
                net.store(sp, io["ssd_s_s"], hs_s[:])
                net.all_stored(sp)

        gated, squared, summed, root, order = (net.sem(n) for n in ("gated", "squared", "summed", "root", "order"))
        with nc.Block() as block:
            @block.vector
            def _(dve):
                link = Chain(dve, order)
                for j in range(8):
                    link(dve.scalar_tensor_tensor(cat[:, j, :], xbc[:, j, :], small[:, 2 + j:3 + j], cat[:, j, :], ALU.mult, ALU.add))
                    dve.tensor_tensor(cat[:, j, :], cat[:, j, :], zt[:, j, :], ALU.mult).then_inc(gated, 1)
                dve.wait_ge(summed, 8)
                r = xbc[:, 0, :]
                dve.tensor_scalar(r, both(net, 0), 1.0 / 1024, EPS, ALU.mult, ALU.add).then_inc(root, 1)
                dve.wait_ge(root, 2)
                link(dve.reciprocal(r, r))
                for j in range(8):
                    dve.scalar_tensor_tensor(cat[:, j, :], cat[:, j, :], small[:, 27 + j:28 + j], r, ALU.mult, ALU.mult)

            @block.scalar
            def _(act):
                for j in range(8):
                    act.wait_ge(gated, j + 1)
                    act.activation(zt[:, j, :], cat[:, j, :], ACT.Square).then_inc(squared, 1)
                act.wait_ge(root, 1)
                act.activation(xbc[:, 0, :], xbc[:, 0, :], ACT.Sqrt).then_inc(root, 1)

            @block.tensor
            def _(pe):
                for j in range(8):
                    pe.wait_ge(squared, j + 1)
                    pe.matmul(net.ps[:, 0, :], net.ones[:], zt[:, j, 0:TP], start=(j == 0), stop=(j == 7), skip_group_check=True)
                    pe.matmul(net.ps[:, 1, 0:NS], net.ones[:], zt[:, j, TP:T], start=(j == 0), stop=(j == 7), skip_group_check=True).then_inc(summed, 1)


def even_mixer(net, cat):
    nc = net.nc
    with ExitStack() as st:
        sb = lambda n, s: st.enter_context(net.buf(n, s))
        cpk = sb("even_consts", [P, pack(EVEN_C).shape[1]])
        c = unpack(cpk, EVEN_C)
        landed = net.sem("consts_landed")
        with nc.Block() as block:
            @block.sync
            def _(sp):
                sp.dma_start(cpk[:], net.io["even_consts"]).then_inc(landed, 16)
                sp.wait_ge(landed, 16)
        lru(net, cat)
        qkv, gates = sb("qkv", [P, TT, 1304]), sb("gates", [P, TT, 24])
        qT, kT = sb("qT", [P, 4, T]), sb("kT", [P, 2, T])
        qTs = sb("qTs", [P, NB, 4, TS])
        wc, ce, on = sb("wc", [P, 4, 4, 32]), sb("ce", [P, 8]), sb("on", [P, 4, 512])
        even_project(net, qkv, gates, c)
        even_rows_out(net, qkv, qT, kT, qTs, c)
        with net.buf("wv4", [P, 2, 4, 4, 32]) as wv4:
            compress_weights(net, wc, wv4, c, ce)
            prompt_compressed(net, qkv, gates, qT, wc, wv4, on, c)
        prompt_attention(net, qkv, gates, qT, kT, on, c)
        turn_outputs(net, on, cat, c)
        sample_attention(net, qkv, gates, kT, qTs, wc, cat, c)


def store_y(net):
    with net.nc.Block() as block:
        @block.sync
        def _(sp):
            net.store(sp, net.io["y"], net.x[:])
            net.all_stored(sp)


OUTS = {
    "y": [P, KD, T], "kv_p": [TP, 512], "kv_s": [NS, 512], "win_p": [TP, 256], "win_s": [NB, 512, 256],
    "lru_tails": [P, 4, 27], "lru_hlast": [P, 4, 9], "ffn_tails": [2, P, 2 * FM, 18], "ssd_tails": [P, 12, 27],
    "gla_s_p": [P, 4, P], "gla_s_s": [P, NB, 4, P], "ssd_s_p": [P, 1024], "ssd_s_s": [P, NB, 1024],
}


def trunk_kernel(nc, io):
    with ExitStack() as ctx:
        net = Net(nc, ctx, io)
        load_x(net)
        with net.buf("cat", [P, 12, T]) as cat:
            even_mixer(net, cat)
            project_and_norm(net, "mix0", "w_mix0", cat, 8, "ln_mix", 0)
        net.recycle()
        ffn(net, 0)
        net.recycle()
        with net.buf("cat1", [P, 12, T]) as cat:
            odd_mixer(net, cat)
            project_and_norm(net, "mix1", "w_mix1", cat, 12, "ln_mix", 1)
        net.recycle()
        ffn(net, 1)
        store_y(net)


def tiles(w, m=P):
    k = w.shape[0] // P
    return w.reshape(k, P, w.shape[1] // m, m).transpose(2, 1, 0, 3)


def rows(a, n):
    f = a.reshape(a.shape[:-1] + (n, P))
    return np.moveaxis(f, (-1, -2), (0, 1))


def lay_out(i):
    o = {}
    z = np.zeros
    x = np.concatenate([i["x_prompt"][0], i["x_sample"].reshape(NS, D)], 0)
    o["x"] = x.T.reshape(KD, P, T).transpose(1, 0, 2)
    o["ones"] = constants()["ones"]
    o["even_consts"] = pack(EVEN_C)
    o["odd_consts"] = pack(ODD_C)
    we = i["w_in_even"][0]
    wq = we[:, 0:512].reshape(D, 2, 4, DH).transpose(0, 2, 1, 3).reshape(D, 512)
    wt = np.concatenate([wq, we[:, 512:1304]], 1)
    o["w_even_tok"] = wt.reshape(KD, P, 1304).transpose(1, 0, 2)
    o["w_lru"] = tiles(we[:, 1304:])
    taps = i["lru_conv_w"][0]
    o["lru_small"] = rows(np.concatenate([taps, i["lru_conv_b"], i["lru_b_gates"][0], i["lru_lambda"]], 0), 4)
    o["lru_hist"] = rows(i["state_lru_conv"][0], 4)
    o["lru_h0"] = rows(i["state_lru_h"][0], 4)
    wg = z((2, 4, P, P), np.float32)
    g = i["lru_w_gates"][0]
    for t in range(4):
        wg[:, t, 0:64, 0:64] = g[:, 2 * t]
        wg[:, t, 64:, 64:] = g[:, 2 * t + 1]
    o["lru_wg"] = wg.reshape(8, P, P).transpose(1, 0, 2)
    cw = i["nsa_cmp_w"][0].reshape(2, 16, 4)
    o["cmp_w"] = np.concatenate([np.tile(cw[0], (8, 1)), np.tile(cw[1], (8, 1))], 1)
    ck = i["cache_nsa_kv"][0].reshape(PHYS, P, 4, P)
    o["cache_kT"] = ck[:, :, 2, :].transpose(0, 2, 1)
    o["cache_tok"] = ck[:, :, [0, 1, 3], :].reshape(PHYS, P, 3 * P)
    win = i["cache_nsa_win"][0].reshape(NB, 512, 2, P)
    o["win_tok"] = win.reshape(NB, 512, 256)
    o["win_kT"] = win[:, :, 0, :].transpose(0, 2, 1)
    o["win_v"] = win[:, :, 1, :].reshape(NB, 4, P, P).transpose(0, 2, 1, 3)
    o["pages"] = i["page_table"].reshape(1, NB * PAGES)
    wo = i["w_out_even"][0]
    wn = wo[0:512].reshape(2, 4, DH, D).transpose(1, 0, 2, 3).reshape(512, D)
    o["w_mix0"] = tiles(np.concatenate([wn, wo[512:]], 0))
    o["w_mix1"] = tiles(i["w_out_odd"][0])
    for n in ("mix", "ffn"):
        o[f"ln_{n}"] = np.stack([np.stack([rows(i[f"ln_{n}_{s}"][k], KD) for s in "gb"], 1) for k in range(2)])
    up, par, hist = [], [], []
    for k in range(2):
        pairs = lambda a: a.reshape(a.shape[:-1] + (2, FM, P)).swapaxes(-2, -3).reshape(a.shape)
        up.append(tiles(pairs(i["ffn_w_up"][k])))
        par.append(rows(pairs(np.concatenate([i["ffn_conv_w"][k], i["ffn_conv_b"][k][None]], 0)), 2 * FM))
        hist.append(rows(pairs(i["state_ffn_conv"][k]), 2 * FM))
        o[f"w_down{k}"] = tiles(i["ffn_w_down"][k])
    o["w_up"], o["ffn_par"], o["ffn_hist"] = np.stack(up), np.stack(par), np.stack(hist)
    w = i["w_in_odd"][0]
    zc, xc, dc, gq, gk, gv, gg, ga = np.split(w, np.cumsum([1024, 1536, 16, 512, 512, 512, 512]), 1)
    o["w_odd"] = tiles(np.concatenate([xc, zc, gg, gq, gk], 1))
    o["w_odd16"] = np.concatenate([dc, ga], 1).reshape(KD, P, 32).transpose(1, 0, 2)
    o["w_v"] = gv.reshape(KD, P, 512).transpose(1, 0, 2)
    o["ssd_conv_par"] = rows(np.concatenate([i["ssd_conv_w"][0], i["ssd_conv_b"]], 0), 12)
    o["ssd_hist"] = rows(i["state_ssd_conv"][0], 12)
    s = z((P, 48), np.float32)
    s[0:NH, 0], s[0:NH, 1] = i["ssd_dt_bias"][0], i["ssd_a_log"][0]
    s[:, 2:10] = np.repeat(i["ssd_d"][0], 64).reshape(8, P).T
    s[:, 27:35] = i["ssd_norm_w"][0].reshape(8, P).T
    s[:, 35] = i["gla_norm_w"][0]
    s[:, 36:40] = i["gla_b_alpha"][0].reshape(4, P).T
    o["odd_small"] = s
    o["w_alpha"] = i["gla_w_alpha"][0]
    o["gla_s0"] = i["state_gla"][0].transpose(2, 0, 1, 3)
    o["ssd_h0"] = i["state_ssd"][0].transpose(3, 0, 1, 2).reshape(P, NB, 1024)
    return {k: np.ascontiguousarray(v) for k, v in o.items()}


def undo(r):
    y = r["y"].transpose(2, 1, 0).reshape(T, D)
    back = lambda a: np.moveaxis(a, (0, 1), (-1, -2)).reshape(a.shape[2:] + (-1,))
    lt, lh, st = r["lru_tails"], r["lru_hlast"], r["ssd_tails"]
    sp = lambda a, n: a[:, :, n:].reshape(P, a.shape[1], NB, n)
    ft_p, ft_s = [], []
    for k in range(2):
        f = r["ffn_tails"][k]
        unpair = lambda a: a.reshape(a.shape[:-1] + (FM, 2, P)).swapaxes(-2, -3).reshape(a.shape)
        ft_p.append(unpair(back(f[:, :, 0:2])))
        ft_s.append(unpair(back(sp(f, 2))))
    gp, gs = r["gla_s_p"], r["gla_s_s"]
    hp, hs = r["ssd_s_p"], r["ssd_s_s"]
    return (
        y[None, :TP], y[TP:].reshape(NB, TS, D),
        r["kv_p"].reshape(1, 1, TP, 4, 2, DH), r["kv_s"].reshape(1, NB, TS, 4, 2, DH),
        r["win_p"].reshape(1, 1, TP, 2, 2, DH), r["win_s"].reshape(1, NB, 512, 2, 2, DH),
        back(lh[:, :, 0])[None, None], back(lh[:, :, 1:])[None],
        back(lt[:, :, 0:3])[None, None], back(sp(lt, 3))[None],
        hp.T.reshape(1, 1, NH, DH, P), hs.transpose(1, 2, 0).reshape(1, NB, NH, DH, P),
        back(st[:, :, 0:3])[None, None], back(sp(st, 3))[None],
        gp.transpose(1, 0, 2)[None, None], gs.transpose(1, 2, 0, 3)[None],
        np.stack(ft_p)[:, None], np.stack(ft_s),
    )


def kernel(**inputs):
    import concourse.bacc as bacc
    from concourse.bass_utils import run_bass_kernel_spmd

    nc = bacc.Bacc("TRN2", target_bir_lowering=False, num_devices=1)
    arrays = lay_out({k: np.asarray(v) for k, v in inputs.items()})
    io = {}
    for name, a in arrays.items():
        io[name] = nc.dram_tensor(f"in_{name}", a.shape, mybir.dt.from_np(a.dtype), kind="ExternalInput").ap()
    for name, shape in OUTS.items():
        io[name] = nc.dram_tensor(f"out_{name}", shape, F32, kind="ExternalOutput").ap()
    trunk_kernel(nc, io)
    r = run_bass_kernel_spmd(nc, [{f"in_{k}": v for k, v in arrays.items()}], core_ids=[0])
    got = {n: r.results[0][f"out_{n}"].reshape(s) for n, s in OUTS.items()}
    return tuple(np.ascontiguousarray(a) for a in undo(got))
```

```python
from contextlib import ExitStack

import numpy as np
import concourse.bass as bass
from concourse import mybir

F32 = mybir.dt.float32
I32 = mybir.dt.int32
F32R = mybir.dt.float32r
ALU = mybir.AluOpType
ACT = mybir.ActivationFunctionType
AX = mybir.AxisListType.X

P = 128
D = 1024
KD = D // P
TP, NB, TS = 512, 8, 8
NS = NB * TS
T = TP + NS
HT = T // 2
TT = 5
DH = 64
PAGES, PHYS = 4, 40
NEG = -1e30
LW = 512
DFF = 2816
FM = DFF // P
ALPHA = 4.0 ** 0.25
EPS = 1e-5
SCH = 128
GCH = 32
NH = 16


def tok(tt):
    n = P if tt < 4 else NS
    return slice(P * tt, P * tt + n), n


def constants():
    c = {}
    p = np.arange(P)
    c["ident"] = np.eye(P)
    c["ones"] = np.ones((P, P))
    inv = np.power(np.float32(500000.0), (-2.0 * np.arange(8, dtype=np.float32) / 16).astype(np.float32))
    pos = np.stack([(P * t + p) if t < 4 else (512 + p % TS) for t in range(TT)], 1).astype(np.float32)
    ang = (pos[:, :, None] * inv.astype(np.float32)).astype(np.float32).astype(np.float64)
    c["rope_c"] = np.concatenate([np.cos(ang), np.cos(ang)], -1)
    c["rope_s"] = np.concatenate([-np.sin(ang), np.sin(ang)], -1)
    c["causal"] = np.where(p[None, :] <= p[:, None], 0.0, NEG)
    n = np.arange(32)
    seen = np.stack([(16 * n[None, :] + 31 <= (P * t + p)[:, None]) & (n[None, :] < 31) for t in range(4)], 1)
    c["cmp_neg"] = np.where(seen, 0.0, NEG)
    c["cmp_01"] = seen * 1.0
    i = (P * np.arange(4)[None, :, None] + p[:, None, None]) - 16 * n[None, None, :]
    c["wc_lo"] = ((i >= 0) & (i < 16) & (n < 31)) * 1.0
    c["wc_hi"] = ((i >= 16) & (i < 32) & (n < 31)) * 1.0
    c["cmp_pad"] = np.broadcast_to(np.where(n < 31, 0.0, NEG), (P, 32))
    c["head4"] = (p[:, None] // 32 == np.arange(4)[None, :]) * 1.0
    b, j, t = p // 32, (p // 8) % 4, p % 8
    c["group"] = ((b[:, None] == b[None, :]) & (t[:, None] == t[None, :])) * 1.0
    kb, kt = np.arange(NS) // TS, np.arange(NS) % TS
    c["new_neg"] = np.stack([np.where((kb[None, :] == (4 * h + b)[:, None]) & (kt[None, :] <= t[:, None]), 0.0, NEG)
                             for h in range(2)], 1)
    c["win_neg"] = np.where(np.arange(8)[None, :] > t[:, None], 0.0, NEG)
    c["row_head"] = (j[:, None] == np.arange(4)[None, :]) * 1.0
    e = np.stack([(np.arange(NS)[:, None] == ((4 * h + b) * TS + t)[None, :]) for h in range(2)], 1) * 1.0
    c["expand"] = np.concatenate([e, np.zeros_like(e)], 0)
    c["blk_no"] = np.broadcast_to(np.arange(1.0, 7.0), (P, 6))
    col = np.arange(T)
    start = np.where(col < TP, col % SCH == 0, (col - TP) % TS == 0)
    c["ssd_keep"] = np.broadcast_to(1.0 - start, (P, T))
    start = np.where(col < TP, col % GCH == 0, (col - TP) % TS == 0)
    c["gla_keep"] = np.broadcast_to(1.0 - start, (P, T))
    c["upto"] = (p[:, None] <= p[None, :]) * 1.0
    s64 = ((kb[:, None] == kb[None, :]) & (kt[:, None] <= kt[None, :])) * 1.0
    c["upto_s"] = np.concatenate([s64, np.zeros_like(s64)], 0)
    c["upto_g"] = ((p[:, None] <= p[None, :]) & (p[:, None] // GCH == p[None, :] // GCH)) * 1.0
    c["of_b"] = np.concatenate([(kb[:, None] == np.arange(NB)[None, :]) * 1.0, np.zeros((64, NB))], 0)
    one = np.zeros((P, NH, P))
    for h in range(NH):
        one[h, h, :] = 1.0
    c["one_head"] = one
    two = np.zeros((P, 8, P))
    for k in range(8):
        two[2 * k, k, :64] = 1.0
        two[2 * k + 1, k, 64:] = 1.0
    c["two_heads"] = two
    return {k: np.ascontiguousarray(v, np.float32).reshape(P, -1) for k, v in c.items()}


EVEN_C = ["rope_c", "rope_s", "causal", "cmp_neg", "cmp_01", "wc_lo", "wc_hi", "cmp_pad", "head4",
          "group", "new_neg", "win_neg", "row_head", "expand", "blk_no"]
ODD_C = ["ssd_keep", "gla_keep", "upto", "upto_s", "upto_g", "of_b", "one_head", "two_heads"]


def pack(names):
    c = constants()
    return np.concatenate([c[n] for n in names], 1)


def unpack(tile, names):
    c, at, out = constants(), 0, {}
    for n in names:
        out[n] = tile[:, at:at + c[n].shape[1]]
        at += c[n].shape[1]
    return out


def split_free(ap, **dims):
    names = list(dims)
    return ap.rearrange(f"p ({' '.join(names)}) -> p {' '.join(names)}", **dims)


class Net:

    def __init__(self, nc, ctx, io):
        self.nc, self.ctx, self.io = nc, ctx, io
        self.n_sems = self.n_bufs = 0
        self.live = []
        self.stored, self.n_stored = nc.alloc_semaphore(name="stored"), 0
        self.ps = ctx.enter_context(nc.psum_tensor("ps", [P, 8, 512], F32))
        self.x = ctx.enter_context(self.buf("x", [P, KD, T]))
        self.xh = self.xl = None
        self.gb = ctx.enter_context(self.buf("ln_gb", [P, 2, KD]))
        self.rstd = ctx.enter_context(self.buf("rstd", [P, T]))
        self.ones = ctx.enter_context(self.buf("ones_t", [P, P]))
        self.ident = ctx.enter_context(self.buf("ident_t", [P, P]))

    def store(self, eng, dst, src):
        eng.dma_start(dst, src).then_inc(self.stored, 16)
        self.n_stored += 16

    def all_stored(self, eng):
        eng.wait_ge(self.stored, self.n_stored)

    def buf(self, name, shape, dtype=F32):
        self.n_bufs += 1
        return self.nc.sbuf_tensor(f"{name}_{self.n_bufs}", shape, dtype)

    def sem(self, name):
        self.n_sems += 1
        self.live.append(self.nc.alloc_semaphore(name=f"{name}_{self.n_sems}"))
        return self.live[-1]

    def recycle(self):
        self.nc.clear_and_free_semaphores(self.live)
        self.nc.all_engine_barrier()
        self.live = []

    def high(self, k):
        return self.xh[:, k, :]

    def low(self, k):
        return self.xl[:, k, :]

    def bank(self, b, parts=P):
        return self.ps[0:parts, b, :]


class Chain:

    def __init__(self, eng, sem):
        self.eng, self.sem, self.n = eng, sem, 0

    def __call__(self, ins):
        self.n += 1
        ins.then_inc(self.sem, 1)
        self.eng.wait_ge(self.sem, self.n)


def load_x(net):
    landed = net.sem("x_landed")
    with net.nc.Block() as block:
        @block.sync
        def _(sp):
            sp.dma_start(net.x[:], net.io["x"]).then_inc(landed, 16)
            sp.dma_start(net.ones[:], net.io["ones"]).then_inc(landed, 16)
            sp.dma_start(net.ident[:], net.io["ident"]).then_inc(landed, 16)
            sp.wait_ge(landed, 48)


def even_project(net, qkv, gates, c):
    nc, io = net.nc, net.io
    NQ = [512, 512, 280]
    with ExitStack() as st:
        w = st.enter_context(net.buf("wq_ring", [P, 2, KD, 512]))
        ra = st.enter_context(net.buf("rope_a", [P, 4, 8, 16]))
        rb = st.enter_context(net.buf("rope_b", [P, 4, 8, 16]))
        w_landed = [net.sem("w_landed0"), net.sem("w_landed1")]
        chunk_done, prod, copied = net.sem("chunk_done"), net.sem("prod"), net.sem("copied")
        exp_done, order = net.sem("exp_done"), net.sem("order")
        with nc.Block() as block:
            @block.sync
            def _(sp):
                for i, n in enumerate(NQ):
                    if i >= 2:
                        sp.wait_ge(prod, TT * (i - 1))
                    sp.dma_start(w[:, i % 2, :, 0:n], io["w_even_tok"][:, :, 512 * i:512 * i + n]).then_inc(w_landed[i % 2], 16)

            @block.tensor
            def _(pe):
                u = 0
                for i, n in enumerate(NQ):
                    pe.wait_ge(w_landed[i % 2], 16 * (i // 2 + 1))
                    for tt in range(TT):
                        cols, m = tok(tt)
                        if u >= 4:
                            pe.wait_ge(copied, u - 3)
                        for k in range(KD):
                            mm = pe.matmul(net.ps[0:m, u % 4, 0:n], net.x[:, k, cols], w[:, i % 2, k, 0:n],
                                           start=(k == 0), stop=(k == KD - 1))
                        mm.then_inc(prod, 1)
                        u += 1

            @block.scalar
            def _(act):
                u = 0
                for i, n in enumerate(NQ):
                    for tt in range(TT):
                        _, m = tok(tt)
                        act.wait_ge(prod, u + 1)
                        act.activation(qkv[0:m, tt, 512 * i:512 * i + n], net.ps[0:m, u % 4, 0:n], ACT.Copy).then_inc(copied, 1)
                        u += 1
                act.wait_ge(copied, u)
                act.activation(gates[:, 0:4, :], qkv[:, 0:4, 1280:1304], ACT.Exp, scale=-1.0).then_inc(exp_done, 1)
                act.activation(gates[0:NS, 4, :], qkv[0:NS, 4, 1280:1304], ACT.Exp, scale=-1.0).then_inc(exp_done, 1)

            @block.vector
            def _(dve):
                link = Chain(dve, order)
                rc, rs = (split_free(c[n], t=TT, e=16) for n in ("rope_c", "rope_s"))

                def rope(parts, t0, nt, lo, heads):
                    x = qkv[0:parts, t0:t0 + nt, lo:lo + 64 * heads].rearrange("p t (h e) -> p t h e", e=64)
                    a, b = ra[0:parts, 0:nt, 0:heads, :], rb[0:parts, 0:nt, 0:heads, :]
                    cc = rc[0:parts, t0:t0 + nt, None, :].broadcast_to([parts, nt, heads, 16])
                    ss = rs[0:parts, t0:t0 + nt, None, :].broadcast_to([parts, nt, heads, 16])
                    dve.tensor_tensor(b[:, :, :, 0:8], x[:, :, :, 8:16], ss[:, :, :, 0:8], ALU.mult)
                    dve.tensor_tensor(b[:, :, :, 8:16], x[:, :, :, 0:8], ss[:, :, :, 8:16], ALU.mult)
                    link(dve.tensor_tensor(a, x[:, :, :, 0:16], cc, ALU.mult))
                    link(dve.tensor_tensor(x[:, :, :, 0:16], a, b, ALU.add))

                for parts, t0, nt in ((P, 0, 4), (NS, 4, 1)):
                    dve.wait_ge(copied, TT)
                    rope(parts, t0, nt, 0, 8)
                    dve.wait_ge(copied, 2 * TT)
                    rope(parts, t0, nt, 512, 2)
                    rope(parts, t0, nt, 768, 2)
                    dve.wait_ge(copied, 3 * TT)
                    rope(parts, t0, nt, 1024, 2)
                dve.wait_ge(exp_done, 2)
                for parts, g in ((P, gates[:, 0:4, :]), (NS, gates[0:NS, 4, :])):
                    link(dve.tensor_scalar(g, g, 1.0, None, ALU.add))
                    link(dve.reciprocal(g, g))


def even_rows_out(net, qkv, qT, kT, qTs, c):
    nc, io = net.nc, net.io
    turned, copied_q, copied_k = net.sem("turned"), net.sem("copied_q"), net.sem("copied_k")
    with nc.Block() as block:
        @block.sync
        def _(sp):
            n = 0
            for tt in range(4):
                net.store(sp, io["kv_p"][P * tt:P * tt + P, :], qkv[:, tt, 512:1024])
                net.store(sp, io["win_p"][P * tt:P * tt + P, :], qkv[:, tt, 1024:1280])
                n += 2
            net.store(sp, io["kv_s"], qkv[0:NS, 4, 512:1024])
            n += 1
            for b in range(NB):
                net.store(sp, io["win_s"][b, 504:512, :], qkv[TS * b:TS * b + TS, 4, 1024:1280])
                net.store(sp, io["win_s"][b, 0:504, :], io["win_tok"][b, 8:512, :])
                n += 2
            net.all_stored(sp)

        @block.tensor
        def _(pe):
            for tt in range(TT):
                _, m = tok(tt)
                if tt >= 2:
                    pe.wait_ge(copied_q, tt - 1)
                    pe.wait_ge(copied_k, tt - 1)
                for i, lo in enumerate([0, 128, 256, 384, 768, 1024]):
                    bank = (tt % 2) * 2 + (i >= 4)
                    mm = pe.transpose(net.ps[:, bank, (i % 4) * P:(i % 4) * P + m], qkv[0:m, tt, lo:lo + P], net.ident[0:m, 0:m])
                mm.then_inc(turned, 1)

        @block.scalar
        def _(act):
            for tt in range(TT):
                cols, m = tok(tt)
                act.wait_ge(turned, tt + 1)
                src = split_free(net.bank((tt % 2) * 2), j=4, n=P)[:, :, 0:m]
                if tt == 4:
                    for j in range(4):
                        act.activation(qTs[:, :, j, :], src[:, j, :].rearrange("p (b t) -> p b t", t=TS), ACT.Copy, scale=DH ** -0.5)
                act.activation(qT[:, :, cols], src, ACT.Copy, scale=DH ** -0.5).then_inc(copied_q, 1)

        @block.vector
        def _(dve):
            for tt in range(TT):
                cols, m = tok(tt)
                dve.wait_ge(turned, tt + 1)
                dve.tensor_copy(kT[:, :, cols], split_free(net.bank((tt % 2) * 2 + 1), j=4, n=P)[:, 0:2, 0:m]).then_inc(copied_k, 1)


def compress_weights(net, wc, wv4, c, ce):
    nc = net.nc
    order = net.sem("order")
    landed = net.sem("landed")
    with nc.Block() as block:
        @block.sync
        def _(sp):
            sp.dma_start(ce[:], net.io["cmp_w"]).then_inc(landed, 16)

        @block.vector
        def _(dve):
            link = Chain(dve, order)
            dve.wait_ge(landed, 16)
            lo, hi = (split_free(c[n], t=4, n=32) for n in ("wc_lo", "wc_hi"))
            for q in range(4):
                link(dve.tensor_scalar(wc[:, q], lo, ce[:, q:q + 1], None, ALU.mult))
                link(dve.scalar_tensor_tensor(wc[:, q], hi, ce[:, 4 + q:5 + q], wc[:, q], ALU.mult, ALU.add))
            for i in range(4):
                dve.tensor_copy(wv4[:, :, :, i, :], wc[:, 2:4])


def prompt_compressed(net, qkv, gates, qT, wc, wv4, on, c):
    nc = net.nc
    with ExitStack() as st:
        sb = lambda n, s: st.enter_context(net.buf(n, s))
        ckT, cvd = sb("ckT", [P, 32]), sb("cvd", [P, 2, 4, DH])
        sc, mx, sm, pT = sb("sc", [P, 8, 32]), sb("mx", [P, 8]), sb("sm", [P, 8]), sb("pT", [P, 2, P])
        blocks, order, scored, centred = net.sem("blocks"), net.sem("order"), net.sem("scored"), net.sem("centred")
        exped, probs, turned, turned_in, summed = (net.sem(n) for n in ("exped", "probs", "turned", "turned_in", "summed"))
        kept = net.sem("kept")
        with nc.Block() as block:
            @block.tensor
            def _(pe):
                for h in range(2):
                    for tt in range(4):
                        pe.matmul(net.ps[64 * h:64 * h + 64, 0, 0:32], qkv[:, tt, 512 + 64 * h:576 + 64 * h], wc[:, h, tt, :],
                                  start=(tt == 0), stop=(tt == 3))
                for h in range(2):
                    for tt in range(4):
                        mm = pe.matmul(net.ps[:, 1, 64 * h:64 * h + 64], wv4[:, h, tt].rearrange("p i n -> p (i n)"),
                                       qkv[:, tt, 640 + 64 * h:704 + 64 * h], start=(tt == 0), stop=(tt == 3))
                mm.then_inc(blocks, 1)
                pe.wait_ge(kept, 1)
                for qt in range(4):
                    for h in range(2):
                        for j in range(4):
                            mm = pe.matmul(net.ps[:, 5 + h, 32 * j:32 * j + 32],
                                           qT[64 * h:64 * h + 64, j, P * qt:P * qt + P], ckT[64 * h:64 * h + 64, :], start=True, stop=True)
                    mm.then_inc(scored, 1)
                    pe.wait_ge(probs, qt + 1)
                    for h in range(2):
                        mm = pe.transpose(net.ps[:, 3, P * h:P * h + P], sc[:, 4 * h:4 * h + 4, :].rearrange("p j n -> p (j n)"), net.ident[:])
                    mm.then_inc(turned, 1)
                    pe.wait_ge(turned_in, qt + 1)
                    for h in range(2):
                        mm = pe.matmul(net.ps[:, 4, 256 * h:256 * h + 256], pT[:, h, :], cvd[:, h].rearrange("p j d -> p (j d)"), start=True, stop=True)
                    mm.then_inc(summed, 1)

            @block.scalar
            def _(act):
                for qt in range(4):
                    act.wait_ge(centred, qt + 1)
                    act.activation(sc[:], sc[:], ACT.Exp).then_inc(exped, 1)
                    act.wait_ge(turned, qt + 1)
                    act.activation(pT[:], net.ps[:, 3, 0:256], ACT.Copy).then_inc(turned_in, 1)

            @block.vector
            def _(dve):
                link = Chain(dve, order)
                neg, keep = (split_free(c[n], t=4, n=32) for n in ("cmp_neg", "cmp_01"))
                dve.wait_ge(blocks, 1)
                dve.tensor_copy(ckT[:], net.ps[:, 0, 0:32])
                for h in range(2):
                    mm = dve.tensor_tensor(cvd[:, h], net.ps[:, 1, None, 64 * h:64 * h + 64].broadcast_to([P, 4, DH]),
                                           c["head4"][:, :, None].broadcast_to([P, 4, DH]), ALU.mult)
                mm.then_inc(kept, 1)
                g3 = gates.rearrange("p t (h j r) -> p t h j r", h=2, r=3)
                for qt in range(4):
                    s8 = net.ps[:, 5:7, 0:P].rearrange("p h (j n) -> p h j n", n=32)
                    dve.wait_ge(scored, qt + 1)
                    link(dve.tensor_tensor(sc[:].rearrange("p (h j) n -> p h j n", h=2), s8, neg[:, qt:qt + 1, None, :].broadcast_to([P, 2, 4, 32]), ALU.add))
                    link(dve.tensor_reduce(mx[:], sc[:], AX, ALU.max))
                    dve.tensor_tensor(sc[:], sc[:], mx[:, :, None].broadcast_to([P, 8, 32]), ALU.subtract).then_inc(centred, 1)
                    dve.wait_ge(exped, qt + 1)
                    link(dve.tensor_reduce(sm[:], sc[:], AX, ALU.add))
                    link(dve.reciprocal(sm[:], sm[:]))
                    link(dve.tensor_tensor(split_free(sm[:], h=2, j=4), split_free(sm[:], h=2, j=4), g3[:, qt, :, :, 0], ALU.mult))
                    link(dve.tensor_tensor(sc[:], sc[:], keep[:, qt:qt + 1, :].broadcast_to([P, 8, 32]), ALU.mult))
                    dve.tensor_tensor(sc[:], sc[:], sm[:, :, None].broadcast_to([P, 8, 32]), ALU.mult).then_inc(probs, 1)
                    dve.wait_ge(summed, qt + 1)
                    out = on[:, qt, :].rearrange("p (j h d) -> p h j d", j=4, h=2)
                    for h in range(2):
                        dve.tensor_copy(out[:, h], split_free(net.ps[:, 4, 256 * h:256 * h + 256], j=4, d=DH))


def prompt_attention(net, qkv, gates, qT, kT, on, c):
    nc = net.nc
    units = [(br, qt, j, h) for br in range(2) for qt in range(4) for j in range(4) for h in range(2)]
    N = len(units)
    with ExitStack() as st:
        sb = lambda n, s: st.enter_context(net.buf(n, s))
        probs, pT = sb("probs", [P, 2, 512]), sb("pT", [P, 2, 512])
        nmx, sums, tmp = sb("nmx", [P, 2]), sb("sums", [P, 2, 8]), sb("tmp", [P, 4, 2, DH])
        mx = sb("mxp", [P, 2])
        scored, maxed, exped, turned, turned_in, summed, added, order = (
            net.sem(n) for n in ("scored", "maxed", "exped", "turned", "turned_in", "summed", "added", "order"))
        with nc.Block() as block:
            @block.tensor
            def _(pe):
                def scores(u):
                    br, qt, j, h = units[u]
                    n = P * (qt + 1)
                    if u >= 2:
                        pe.wait_ge(exped, u - 1)
                    pe.matmul(net.ps[:, u % 2, 0:n], qT[64 * h:64 * h + 64, j, P * qt:P * qt + P],
                              kT[64 * h:64 * h + 64, br, 0:n], start=True, stop=True).then_inc(scored, 1)

                def turn(u):
                    br, qt, j, h = units[u]
                    pe.wait_ge(exped, u + 1)
                    if u >= 2:
                        pe.wait_ge(turned_in, u - 1)
                    for k in range(qt + 1):
                        mm = pe.transpose(net.ps[:, 2 + u % 2, P * k:P * k + P], probs[:, u % 2, P * k:P * k + P], net.ident[:])
                    mm.then_inc(turned, 1)

                def weigh(u):
                    br, qt, j, h = units[u]
                    g = u // 8
                    pe.wait_ge(turned_in, u + 1)
                    if u % 8 == 0 and g >= 2:
                        pe.wait_ge(added, g - 1)
                    v0 = (896 if br == 0 else 1152) + 64 * h
                    for k in range(qt + 1):
                        mm = pe.matmul(net.ps[:, 4 + g % 2, 64 * (u % 8):64 * (u % 8) + 64], pT[:, u % 2, P * k:P * k + P],
                                       qkv[:, k, v0:v0 + 64], start=(k == 0), stop=(k == qt))
                    mm.then_inc(summed, 1)

                for i in range(N + 2):
                    if i < N:
                        scores(i)
                    if 1 <= i <= N:
                        turn(i - 1)
                    if i >= 2:
                        weigh(i - 2)

            @block.scalar
            def _(act):
                for i in range(N + 1):
                    if i < N:
                        br, qt, j, h = units[i]
                        n, g = P * (qt + 1), i // 8
                        act.wait_ge(maxed, i + 1)
                        if i >= 2:
                            act.wait_ge(turned, i - 1)
                        if i % 8 == 0 and g >= 2:
                            act.wait_ge(added, g - 1)
                        act.activation(probs[:, i % 2, 0:n], net.ps[:, i % 2, 0:n], ACT.Exp, bias=nmx[:, i % 2:i % 2 + 1],
                                       accum_out=sums[:, g % 2, i % 8:i % 8 + 1]).then_inc(exped, 1)
                    if i >= 1:
                        u = i - 1
                        n = P * (units[u][1] + 1)
                        act.wait_ge(turned, u + 1)
                        if u >= 2:
                            act.wait_ge(summed, u - 1)
                        act.activation(pT[:, u % 2, 0:n], net.ps[:, 2 + u % 2, 0:n], ACT.Copy).then_inc(turned_in, 1)

            @block.vector
            def _(dve):
                link = Chain(dve, order)
                g3 = gates.rearrange("p t (h j r) -> p t j h r", h=2, r=3)

                def add(g):
                    br, qt = units[8 * g][:2]
                    dve.wait_ge(summed, 8 * g + 8)
                    r = split_free(sums[:, g % 2, :], j=4, h=2)
                    link(dve.reciprocal(r, r))
                    link(dve.tensor_tensor(r, r, g3[:, qt, :, :, 1 + br], ALU.mult))
                    link(dve.tensor_tensor(tmp[:], net.ps[:, 4 + g % 2, :].rearrange("p (j h d) -> p j h d", j=4, h=2),
                                           r[:, :, :, None].broadcast_to([P, 4, 2, DH]), ALU.mult))
                    dve.tensor_tensor(on[:, qt, :], on[:, qt, :], tmp[:].rearrange("p j h d -> p (j h d)"), ALU.add).then_inc(added, 1)

                for u, (br, qt, j, h) in enumerate(units):
                    dve.wait_ge(scored, u + 1)
                    diag = net.ps[:, u % 2, P * qt:P * qt + P]
                    link(dve.tensor_tensor(diag, diag, c["causal"], ALU.add))
                    link(dve.tensor_reduce(mx[:, u % 2:u % 2 + 1], net.ps[:, u % 2, 0:P * qt + P], AX, ALU.max))
                    dve.tensor_scalar(nmx[:, u % 2:u % 2 + 1], mx[:, u % 2:u % 2 + 1], -1.0, None, ALU.mult).then_inc(maxed, 1)
                    if u >= 10 and u % 8 == 2:
                        add((u - 10) // 8)
                add(N // 8 - 1)


class Steps:

    def __init__(self, sem, names):
        self.sem, self.at = sem, {n: i + 1 for i, n in enumerate(names)}

    def after(self, eng, name):
        eng.wait_ge(self.sem, self.at[name])

    def done(self, ins):
        ins.then_inc(self.sem, 1)


def sample_attention(net, qkv, gates, kT, qTs, wc, cat, c):
    nc, io = net.nc, net.io
    names = []
    for half in range(2):
        names += [(half, "compressed"), (half, "kept")]
        for h in range(2):
            names += [(half, h, n) for n in ("c_scored", "c_centred", "c_exp", "c_probs", "c_turned", "c_pT", "c_out", "picked")]
            for br in range(2):
                names += [(half, h, br, n) for n in ("scored", "maxed", "exp", "turned", "pT", "out", "added")]
        names += [(half, "o_turned"), (half, "o_kept")]
    step = Steps(net.sem("steps_done"), names)
    with ExitStack() as st:
        sb = lambda n, s, d=F32: st.enter_context(net.buf(n, s, d))
        ids = sb("ids", [1, NB * PAGES], I32)
        kslc, kwin = sb("kslc", [P, 4, PAGES * P]), sb("kwin", [P, 4, 512])
        ptok, vwin = sb("ptok", [P, 4, PAGES, 3 * P]), sb("vwin", [P, 4, PAGES, P])
        ckT, cv = sb("ckTs", [P, 4, 32]), sb("cv", [32, 4, P])
        gx, grow = sb("gx", [P, 24]), sb("grow", [P, 2, 3])
        pc, imp = sb("pc", [P, 32]), sb("imp", [P, 8])
        cand, pick = sb("cand", [P, 6]), sb("pick", [P, 1])
        probs, pT = sb("probs", [P, T]), sb("pTs", [P, TT, P])
        nmx, row_sum, mx = sb("nmx", [P, 1]), sb("row_sum", [P, 1]), sb("mx1", [P, 1])
        so = sb("so", [P, 2, DH])
        ids_landed, past_landed, order = net.sem("ids_landed"), net.sem("past_landed"), net.sem("order")
        with nc.Block() as block:
            @block.sync
            def _(sp):
                sp.dma_start(ids[:], io["pages"]).then_inc(ids_landed, 16)
                sp.wait_ge(ids_landed, 16)
                for half in range(2):
                    if half:
                        step.after(sp, (0, "o_kept"))
                    for b in range(4):
                        for g in range(PAGES):
                            n = (4 * half + b) * PAGES + g
                            page = sp.value_load(ids[0:1, n:n + 1], min_val=0, max_val=PHYS - 1)
                            sp.dma_start(kslc[:, b, P * g:P * g + P], io["cache_kT"][bass.ds(page, 1), :, :].rearrange("a p t -> p (a t)")).then_inc(past_landed, 16)
                            sp.dma_start(ptok[:, b, g, :], io["cache_tok"][bass.ds(page, 1), :, :].rearrange("a p t -> p (a t)")).then_inc(past_landed, 16)
                        sp.dma_start(kwin[:, b, :], io["win_kT"][4 * half + b]).then_inc(past_landed, 16)
                        sp.dma_start(vwin[:, b], io["win_v"][4 * half + b]).then_inc(past_landed, 16)

            @block.tensor
            def _(pe):
                for half in range(2):
                    pe.wait_ge(past_landed, 16 * 40 * (half + 1))
                    if half:
                        step.after(pe, (0, "o_kept"))
                    for b in range(4):
                        for h in range(2):
                            for g in range(PAGES):
                                pe.matmul(net.ps[64 * h:64 * h + 64, 0, 32 * b:32 * b + 32], ptok[:, b, g, 64 * h:64 * h + 64],
                                          wc[:, h, g, :], start=(g == 0), stop=(g == 3))
                    for b in range(4):
                        for h in range(2):
                            for g in range(PAGES):
                                pe.matmul(net.ps[0:32, 1, P * b + 64 * h:P * b + 64 * h + 64], wc[:, 2 + h, g, :],
                                          ptok[:, b, g, P + 64 * h:P + 64 * h + 64], start=(g == 0), stop=(g == 3))
                    step.done(pe.matmul(net.ps[:, 2, 0:24], split_free(c["expand"], h=2, n=P)[0:NS, half, :], gates[0:NS, 4, :],
                                        start=True, stop=True))
                    step.after(pe, (half, "kept"))
                    for h in range(2):
                        rows = qTs[64 * h:64 * h + 64, 4 * half:4 * half + 4].rearrange("p b j t -> p (b j t)")
                        hp = slice(64 * h, 64 * h + 64)
                        if h:
                            step.after(pe, (half, 0, 1, "added"))
                        for b in range(4):
                            mm = pe.matmul(net.ps[32 * b:32 * b + 32, 0, 0:32], rows[:, 32 * b:32 * b + 32], ckT[hp, b, :], start=True, stop=True)
                        step.done(mm)
                        step.after(pe, (half, h, "c_probs"))
                        pe.matmul(net.ps[:, 1, 0:32], c["group"], pc[:], start=True, stop=True)
                        step.done(pe.transpose(net.ps[0:32, 2, 0:P], pc[:], net.ident[:]))
                        step.after(pe, (half, h, "c_pT"))
                        for b in range(4):
                            mm = pe.matmul(net.ps[32 * b:32 * b + 32, 3, 0:64], pT[0:32, 0, 32 * b:32 * b + 32], cv[:, b, 64 * h:64 * h + 64], start=True, stop=True)
                        step.done(mm)
                        for br in range(2):
                            keys = (kslc, kwin)[br]
                            step.after(pe, (half, h, "picked") if br == 0 else (half, h, 0, "added"))
                            for b in range(4):
                                pe.matmul(net.ps[32 * b:32 * b + 32, 4, :], rows[:, 32 * b:32 * b + 32], keys[hp, b, :], start=True, stop=True)
                            step.done(pe.matmul(net.ps[:, 5, 0:NS], rows, kT[hp, br, TP:T], start=True, stop=True))
                            step.after(pe, (half, h, br, "exp"))
                            for g in range(PAGES):
                                pe.transpose(net.ps[:, 6, P * g:P * g + P], probs[:, P * g:P * g + P], net.ident[:])
                            step.done(pe.transpose(net.ps[0:NS, 7, 0:P], probs[:, TP:T], net.ident[:]))
                            step.after(pe, (half, h, br, "pT"))
                            for b in range(4):
                                out = net.ps[32 * b:32 * b + 32, 3, 0:64]
                                for g in range(PAGES):
                                    v = ptok[:, b, g, 2 * P + 64 * h:2 * P + 64 * h + 64] if br == 0 else vwin[:, b, g, 64 * h:64 * h + 64]
                                    pe.matmul(out, pT[:, g, 32 * b:32 * b + 32], v, start=(g == 0), stop=False)
                                v0 = (896 if br == 0 else 1152) + 64 * h
                                mm = pe.matmul(out, pT[0:NS, 4, 32 * b:32 * b + 32], qkv[0:NS, 4, v0:v0 + 64], start=False, stop=True)
                            step.done(mm)
                    step.after(pe, (half, 1, 1, "added"))
                    step.done(pe.transpose(net.ps[:, 0, 0:P], so[:].rearrange("p h d -> p (h d)"), net.ident[:]))

            @block.scalar
            def _(act):
                for half in range(2):
                    for h in range(2):
                        step.after(act, (half, h, "c_centred"))
                        step.done(act.activation(pc[:], pc[:], ACT.Exp, accum_out=row_sum[:]))
                        step.after(act, (half, h, "c_turned"))
                        step.done(act.activation(pT[0:32, 0, :], net.ps[0:32, 2, 0:P], ACT.Copy))
                        for br in range(2):
                            step.after(act, (half, h, br, "maxed"))
                            step.done(act.activation(probs[:], net.ps[:, 4:6, :].rearrange("p a n -> p (a n)")[:, 0:T], ACT.Exp,
                                                     bias=nmx[:], accum_out=row_sum[:]))
                            step.after(act, (half, h, br, "turned"))
                            act.activation(pT[:, 0:4, :], split_free(net.bank(6), g=4, n=P), ACT.Copy)
                            step.done(act.activation(pT[0:NS, 4, :], net.ps[0:NS, 7, 0:P], ACT.Copy))
                    step.after(act, (half, "o_turned"))
                    o = split_free(net.ps[:, 0, 0:P], b=4, j=4, t=TS)
                    for j in range(4):
                        ins = act.activation(cat[:, j, TP + 32 * half:TP + 32 * half + 32].rearrange("p (b t) -> p b t", t=TS), o[:, :, j, :], ACT.Copy)
                    step.done(ins)

            @block.vector
            def _(dve):
                link = Chain(dve, order)
                neg_new = split_free(c["new_neg"], h=2, n=NS)
                for half in range(2):
                    step.after(dve, (half, "compressed"))
                    dve.tensor_copy(ckT[:], split_free(net.ps[:, 0, 0:P], b=4, n=32))
                    dve.tensor_copy(cv[:], split_free(net.ps[0:32, 1, :], b=4, n=P))
                    link(dve.tensor_tensor(split_free(gx[:], h=2, j=4, r=3), split_free(net.ps[:, 2, 0:24], h=2, j=4, r=3),
                                           c["row_head"][:, None, :, None].broadcast_to([P, 2, 4, 3]), ALU.mult))
                    step.done(dve.tensor_reduce(grow[:], gx[:].rearrange("p (h j r) -> p h r j", h=2, r=3), AX, ALU.add))
                    for h in range(2):
                        step.after(dve, (half, h, "c_scored"))
                        link(dve.tensor_tensor(pc[:], net.ps[:, 0, 0:32], c["cmp_pad"], ALU.add))
                        link(dve.tensor_reduce(mx[:], pc[:], AX, ALU.max))
                        step.done(dve.tensor_scalar(pc[:], pc[:], mx[:], None, ALU.subtract))
                        step.after(dve, (half, h, "c_exp"))
                        link(dve.reciprocal(row_sum[:], row_sum[:]))
                        step.done(dve.tensor_scalar(pc[:], pc[:], row_sum[:], None, ALU.mult))
                        step.after(dve, (half, h, "c_out"))
                        link(dve.tensor_scalar(so[:, h, :], net.ps[:, 3, 0:64], grow[:, h, 0:1], None, ALU.mult))
                        pg = split_free(net.ps[:, 1, 0:32], j=8, i=4)
                        link(dve.tensor_reduce(imp[:], pg[:, :, 0:3], AX, ALU.add))
                        link(dve.tensor_copy(probs[:, 0:32], net.ps[:, 1, 0:32]))
                        pg = split_free(probs[:, 0:32], j=8, i=4)
                        link(dve.scalar_tensor_tensor(cand[:], pg[:, 1:7, 3], 0.5, imp[:, 1:7], ALU.mult, ALU.add))
                        link(dve.scalar_tensor_tensor(cand[:], pg[:, 0:6, 3], 0.5, cand[:], ALU.mult, ALU.add))
                        link(dve.tensor_reduce(pick[:], cand[:], AX, ALU.min))
                        link(dve.tensor_scalar(cand[:], cand[:], pick[:], None, ALU.is_le))
                        link(dve.tensor_tensor(cand[:], cand[:], c["blk_no"], ALU.mult))
                        link(dve.tensor_reduce(pick[:], cand[:], AX, ALU.max))
                        step.done(dve.tensor_scalar(cand[:], c["blk_no"], pick[:], NEG, ALU.is_equal, ALU.mult))
                        for br in range(2):
                            step.after(dve, (half, h, br, "scored"))
                            if br == 0:
                                s = split_free(net.ps[:, 4, 64:448], j=6, n=64)
                                link(dve.tensor_tensor(s, s, cand[:, :, None].broadcast_to([P, 6, 64]), ALU.add))
                            else:
                                link(dve.tensor_tensor(net.ps[:, 4, 0:8], net.ps[:, 4, 0:8], c["win_neg"], ALU.add))
                            link(dve.tensor_tensor(net.ps[:, 5, 0:NS], net.ps[:, 5, 0:NS], neg_new[:, half, :], ALU.add))
                            link(dve.tensor_reduce(mx[:], net.ps[:, 4:6, :].rearrange("p a n -> p (a n)")[:, 0:T], AX, ALU.max))
                            step.done(dve.tensor_scalar(nmx[:], mx[:], -1.0, None, ALU.mult))
                            step.after(dve, (half, h, br, "out"))
                            link(dve.reciprocal(row_sum[:], row_sum[:]))
                            link(dve.tensor_tensor(row_sum[:], row_sum[:], grow[:, h, 1 + br:2 + br], ALU.mult))
                            step.done(dve.scalar_tensor_tensor(so[:, h, :], net.ps[:, 3, 0:64], row_sum[:], so[:, h, :], ALU.mult, ALU.add))


def turn_outputs(net, on, cat, c):
    turned, copied = net.sem("turned"), net.sem("copied")
    with net.nc.Block() as block:
        @block.tensor
        def _(pe):
            for qt in range(4):
                for j in range(4):
                    mm = pe.transpose(net.ps[:, qt, P * j:P * j + P], on[:, qt, P * j:P * j + P], net.ident[:])
                mm.then_inc(turned, 1)

        @block.scalar
        def _(act):
            for qt in range(4):
                act.wait_ge(turned, qt + 1)
                act.activation(cat[:, 0:4, P * qt:P * qt + P], split_free(net.bank(qt), j=4, n=P), ACT.Copy).then_inc(copied, 1)


def products(net, pe, out_bank, w, x, kt, m=P):
    for a in range(2):
        for k in range(kt):
            mm = pe.matmul(net.ps[0:m, out_bank + a, 0:HT], w[:, k, :], x[:, k, HT * a:HT * a + HT], start=(k == 0), stop=(k == kt - 1))
    return mm


class SplitWeights:

    def __init__(self, net, st, w_dram, n_tiles, kt, slots=3):
        self.net, self.w_dram, self.slots = net, w_dram, slots
        self.per = -(-kt // 8)
        size = -(-kt // self.per)
        self.chunks = [(m, k0, min(size, kt - k0)) for m in range(n_tiles) for k0 in range(0, kt, size)]
        self.kt = kt
        self.raws = 2
        self.raw = st.enter_context(net.buf("w_raw", [P, self.raws, size, P]))
        self.high = st.enter_context(net.buf("w_high", [P, slots, size, P], F32R))
        self.low = st.enter_context(net.buf("w_low", [P, slots, size, P], F32R))
        self.landed = [net.sem(f"w_landed{i}") for i in range(self.raws)]
        self.high_done, self.low_done, self.used = net.sem("w_high_done"), net.sem("w_low_done"), net.sem("w_used")

    def load(self, sp, i):
        m, k0, n = self.chunks[i]
        r = i % self.raws
        if i >= self.raws:
            sp.wait_ge(self.low_done, i - self.raws + 1)
        sp.dma_start(self.raw[:, r, 0:n, :], self.w_dram[m, :, k0:k0 + n, :]).then_inc(self.landed[r], 16)

    def split_high(self, act, i):
        s, r, n = i % self.slots, i % self.raws, self.chunks[i][2]
        act.wait_ge(self.landed[r], 16 * (i // self.raws + 1))
        if i >= self.slots:
            act.wait_ge(self.used, i - self.slots + 1)
        act.activation(self.high[:, s, 0:n, :], self.raw[:, r, 0:n, :], ACT.Copy).then_inc(self.high_done, 1)

    def split_low(self, dve, i):
        s, r, n = i % self.slots, i % self.raws, self.chunks[i][2]
        dve.wait_ge(self.high_done, i + 1)
        dve.tensor_tensor(self.low[:, s, 0:n, :], self.raw[:, r, 0:n, :], self.high[:, s, 0:n, :].bitcast(F32), ALU.subtract).then_inc(self.low_done, 1)

    def ahead(self, m=None):
        lo, hi = (0, self.slots) if m is None else (self.slots + m * self.per, self.slots + (m + 1) * self.per)
        return range(min(lo, len(self.chunks)), min(hi, len(self.chunks)))

    def multiply(self, pe, m, out_bank, high, low, ready=None):
        for i in range(m * self.per, (m + 1) * self.per):
            _, k0, n = self.chunks[i]
            s = i % self.slots
            pe.wait_ge(self.low_done, i + 1)
            for k in range(n):
                if ready is not None and m == 0:
                    ready(pe, k0 + k)
                for a in range(2):
                    cols = slice(HT * a, HT * a + HT)
                    out = self.net.ps[:, out_bank + a, 0:HT]
                    first, last = k0 + k == 0, k0 + k == self.kt - 1
                    pe.matmul(out, self.high[:, s, k, :], high(k0 + k)[:, cols], start=first, stop=False)
                    pe.matmul(out, self.high[:, s, k, :], low(k0 + k)[:, cols], start=False, stop=False)
                    mm = pe.matmul(out, self.low[:, s, k, :], high(k0 + k)[:, cols], start=False, stop=last)
            mm.then_inc(self.used, 1)

    def product_out(self, eng, m):
        eng.wait_ge(self.used, (m + 1) * self.per)


class Split:

    def __init__(self, net, src, high, low):
        self.src, self.high, self.low = src, high, low
        self.high_done, self.low_done = net.sem("x_high_done"), net.sem("x_low_done")

    def split_high(self, act, k):
        act.activation(self.high(k), self.src(k), ACT.Copy).then_inc(self.high_done, 1)

    def split_low(self, dve, k):
        dve.wait_ge(self.high_done, k + 1)
        dve.tensor_tensor(self.low(k), self.src(k), self.high(k).bitcast(F32), ALU.subtract).then_inc(self.low_done, 1)

    def ready(self, pe, k):
        pe.wait_ge(self.low_done, k + 1)


class FinishX:

    def __init__(self, net, st, norm=True):
        self.net, self.norm, self.splits = net, norm, st is not None
        if self.splits:
            net.xh = st.enter_context(net.buf("x_high", [P, KD, T], F32R))
            net.xl = st.enter_context(net.buf("x_low", [P, KD, T], F32R))
        self.split = Split(net, lambda k: net.x[:, k, :], lambda k: net.xh[:, k, :], lambda k: net.xl[:, k, :])
        self.x_done, self.order = net.sem("x_done"), net.sem("x_order")

    def on_vector(self, dve):
        net, link = self.net, Chain(dve, self.order)
        for k in range(KD + 1):
            if k < KD and self.norm:
                link(dve.tensor_tensor(net.x[:, k, :], net.x[:, k, :], net.rstd[:], ALU.mult))
                dve.tensor_scalar(net.x[:, k, :], net.x[:, k, :], net.gb[:, 0, k:k + 1], net.gb[:, 1, k:k + 1], ALU.mult, ALU.add).then_inc(self.x_done, 1)
            if k and self.splits:
                self.split.split_low(dve, k - 1)

    def on_scalar(self, act):
        for k in range(KD):
            if self.norm:
                act.wait_ge(self.x_done, k + 1)
            self.split.split_high(act, k)

    def ready(self, pe, k):
        self.split.ready(pe, k)


def both(net, b, m=P):
    return net.ps[0:m, b:b + 2, 0:HT]


def wide(net, b, m=P):
    return net.ps[0:m, b:b + 2, :].rearrange("p a n -> p (a n)")[:, 0:T]


def halves(ap):
    return ap.rearrange("p (a n) -> p a n", a=2)


def copy_to_conv(act, net, b, p_tok, s_tok):
    act.activation(p_tok[:, 0:HT], net.ps[:, b, 0:HT], ACT.Copy)
    act.activation(p_tok[:, HT:TP], net.ps[:, b + 1, 0:TP - HT], ACT.Copy)
    return act.activation(s_tok, split_free(net.ps[:, b + 1, TP - HT:HT], b=NB, t=TS), ACT.Copy)


def conv_cols(taps):
    h = taps - 1
    return h + TP + NB * (h + TS)


def conv_parts(buf, taps):
    h = taps - 1
    s = buf[:, h + TP:].rearrange("p (b n) -> p b n", n=h + TS)
    return buf[:, h:h + TP], s[:, :, h:], s[:, :, 0:h], buf[:, TP:TP + h], s[:, :, TS:]


def conv_out_parts(buf, taps):
    h = taps - 1
    s = buf[:, h + TP:]
    return buf[:, 0:TP], [s[:, (h + TS) * b:(h + TS) * b + TS] for b in range(NB)]


def tokens_of(buf, taps):
    h = taps - 1
    return buf[:, 0:TP], buf[:, h + TP:].rearrange("p (b n) -> p b n", n=h + TS)[:, :, 0:TS]


def tok3(ap):
    return ap[:, TP:T].rearrange("p (b t) -> p b t", t=TS)


def lru(net, cat):
    nc, io = net.nc, net.io
    CC = conv_cols(4)
    SC = TP + NB * (1 + TS)
    with ExitStack() as st:
        sb = lambda n, s: st.enter_context(net.buf(n, s))
        wt = SplitWeights(net, st, io["w_lru"], 8, KD)
        fin = FinishX(net, st, norm=False)
        hx, xc = sb("hx", [P, 4, CC]), sb("xc", [P, 4, CC])
        gg, wg = sb("gelu_g", [P, 4, T]), sb("wg", [P, 8, P])
        small = sb("small", [P, 4, 8])
        hist, h0 = sb("hist", [P, 4, NB, 3]), sb("h0", [P, 4, NB])
        rg, ig, la = sb("rg", [P, 2, T]), sb("ig", [P, 2, T]), sb("la", [P, 2, T])
        a, u, hh = sb("a", [P, 4, SC]), sb("u", [P, 4, SC]), sb("hh", [P, 4, SC])
        sp8, tmp4 = sb("sp8", [P, 4]), sb("tmp4", [P, 4, 4])
        tails = sb("tails", [P, 4, 27])
        hlast = sb("hlast", [P, 4, 9])
        (small_landed, copied, conved, gated, gates_out, stepped, gelued, order, act_order, sqrts, tanhs, halo, lam1, lam2, prep) = (
            net.sem(n) for n in ("small_landed", "copied", "conved", "gated", "gates_out", "stepped", "gelued", "order",
                                 "act_order", "sqrts", "tanhs", "halo", "lam1", "lam2", "prep"))
        with nc.Block() as block:
            @block.sync
            def _(sp):
                for dst, name in ((small, "lru_small"), (hist, "lru_hist"), (h0, "lru_h0"), (wg, "lru_wg")):
                    sp.dma_start(dst[:], io[name]).then_inc(small_landed, 16)
                for m in range(8):
                    wt.load(sp, m)

            @block.gpsimd
            def _(pool):
                pool.wait_ge(small_landed, 64)
                for i in range(4):
                    p_tok, s_tok, s_hist, _, _ = conv_parts(hx[:, i, :], 4)
                    pool.memset(hx[:, i, 0:3], 0.0)
                    pool.tensor_copy(s_hist, hist[:, i])
                    pool.memset(a[:, i, TP:].rearrange("p (b n) -> p b n", n=1 + TS)[:, :, 0:1], 0.0)
                    ins = pool.tensor_copy(u[:, i, TP:].rearrange("p (b n) -> p b n", n=1 + TS)[:, :, 0], h0[:, i])
                ins.then_inc(halo, 1)

            @block.tensor
            def _(pe):
                for m in range(8):
                    if m >= 2:
                        pe.wait_ge(copied, m - 1)
                    wt.multiply(pe, m, 2 * (m % 2), net.high, net.low, fin.ready)
                pe.wait_ge(small_landed, 64)
                for i in range(4):
                    pe.wait_ge(conved, i + 1)
                    if i:
                        pe.wait_ge(gates_out, i)
                    for g in range(2):
                        pe.matmul(net.ps[:, 4 + 2 * g, :], wg[:, 4 * g + i, :], xc[:, i, 0:TP], start=True, stop=True)
                        mm = pe.matmul(net.ps[:, 5 + 2 * g, 0:NS], wg[:, 4 * g + i, :], tokens_of(xc[:, i, :], 4)[1], start=True, stop=True)
                    mm.then_inc(gated, 1)

            @block.scalar
            def _(act):
                wt.split_high(act, 0)
                fin.on_scalar(act)
                for i in wt.ahead()[1:]:
                    wt.split_high(act, i)
                act.wait_ge(small_landed, 64)
                act.wait_ge(halo, 1)
                for m in range(8):
                    wt.product_out(act, m)
                    b = 2 * (m % 2)
                    if m < 4:
                        p_tok, s_tok, *_ = conv_parts(hx[:, m, :], 4)
                        copy_to_conv(act, net, b, p_tok, s_tok).then_inc(copied, 1)
                    else:
                        act.activation(halves(gg[:, m - 4, :]), both(net, b), ACT.Gelu_apprx_tanh).then_inc(copied, 1)
                    for i in wt.ahead(m):
                        wt.split_high(act, i)
                act.wait_ge(lam1, 1)
                act.activation(tmp4[:, 1, :], tmp4[:, 0, :], ACT.Exp, scale=-1.0).then_inc(lam2, 1)
                for i in range(4):
                    act.wait_ge(gated, i + 1)
                    if i >= 2:
                        act.wait_ge(stepped, i - 1)
                    act.activation(rg[:, i % 2, :], wide(net, 4), ACT.Sigmoid, bias=small[:, i, 5:6])
                    act.activation(ig[:, i % 2, :], wide(net, 6), ACT.Sigmoid, bias=small[:, i, 6:7]).then_inc(gates_out, 1)
                    act.wait_ge(prep, i + 1)
                    av = a[:, i, TP:].rearrange("p (b n) -> p b n", n=1 + TS)[:, :, 1:]
                    act.activation(a[:, i, 0:TP], la[:, i % 2, 0:TP], ACT.Exp)
                    act.activation(av, tok3(la[:, i % 2, :]), ACT.Exp)
                    act.activation(rg[:, i % 2, :], la[:, i % 2, :], ACT.Tanh).then_inc(tanhs, 1)
                    act.wait_ge(sqrts, 2 * i + 1)
                    act.activation(la[:, i % 2, :], rg[:, i % 2, :], ACT.Sqrt).then_inc(sqrts, 1)

            @block.vector
            def _(dve):
                link = Chain(dve, order)
                wt.split_low(dve, 0)
                fin.on_vector(dve)
                for i in wt.ahead()[1:]:
                    wt.split_low(dve, i)
                dve.wait_ge(small_landed, 64)
                lam = small[:, :, 7]
                link(dve.scalar_tensor_tensor(tmp4[:, 0, :], lam, -1.0, lam, ALU.mult, ALU.max))
                dve.tensor_scalar(tmp4[:, 2, :], lam, -1.0, 0.0, ALU.mult, ALU.max).then_inc(lam1, 1)
                for i in range(4):
                    dve.wait_ge(copied, i + 1)
                    n = CC - 3
                    link(dve.tensor_scalar(xc[:, i, 0:n], hx[:, i, 0:n], small[:, i, 0:1], small[:, i, 4:5], ALU.mult, ALU.add))
                    for k in range(1, 4):
                        ins = dve.scalar_tensor_tensor(xc[:, i, 0:n], hx[:, i, k:k + n], small[:, i, k:k + 1], xc[:, i, 0:n], ALU.mult, ALU.add)
                        if k < 3:
                            link(ins)
                        else:
                            ins.then_inc(conved, 1)
                    *_, p_tail, s_tail = conv_parts(hx[:, i, :], 4)
                    link(dve.tensor_copy(tails[:, i, 0:3], p_tail))
                    link(dve.tensor_copy(tails[:, i, 3:27].rearrange("p (b n) -> p b n", n=3), s_tail))
                    for i in wt.ahead(i):
                        wt.split_low(dve, i)
                for m in range(4, 8):
                    for i in wt.ahead(m):
                        wt.split_low(dve, i)
                dve.wait_ge(lam2, 1)
                log1p(dve, link, tmp4[:, 1, :], tmp4[:, 0, :], tmp4[:, 3, :], sp8[:])
                link(dve.tensor_tensor(sp8[:], sp8[:], tmp4[:, 2, :], ALU.add))
                link(dve.tensor_scalar(sp8[:], sp8[:], -8.0, None, ALU.mult))
                dve.wait_ge(conved, 4)
                for i in range(4):
                    xp, xs = tokens_of(xc[:, i, :], 4)
                    uv = u[:, i, TP:].rearrange("p (b n) -> p b n", n=1 + TS)[:, :, 1:]
                    dve.wait_ge(gates_out, i + 1)
                    dve.tensor_scalar(la[:, i % 2, :], rg[:, i % 2, :], sp8[:, i:i + 1], None, ALU.mult).then_inc(prep, 1)
                    dve.wait_ge(tanhs, i + 1)
                    th, t2 = rg[:, i % 2, :], ig[:, i % 2, :]
                    link(dve.tensor_scalar(la[:, i % 2, :], th, -1.0, 1.0, ALU.mult, ALU.add))
                    link(dve.reciprocal(la[:, i % 2, :], la[:, i % 2, :]))
                    dve.scalar_tensor_tensor(th, th, -2.0, la[:, i % 2, :], ALU.mult, ALU.mult).then_inc(sqrts, 1)
                    link(dve.tensor_tensor(u[:, i, 0:TP], t2[:, 0:TP], xp, ALU.mult))
                    link(dve.tensor_tensor(uv, tok3(t2), xs, ALU.mult))
                    dve.wait_ge(sqrts, 2 * i + 2)
                    link(dve.tensor_tensor(u[:, i, 0:TP], u[:, i, 0:TP], la[:, i % 2, 0:TP], ALU.mult))
                    link(dve.tensor_tensor(uv, uv, tok3(la[:, i % 2, :]), ALU.mult))
                    dve.tensor_tensor_scan(hh[:, i, :], a[:, i, :], u[:, i, :], 0.0, ALU.mult, ALU.add).then_inc(stepped, 1)
                    dve.wait_ge(stepped, i + 1)
                    hv = hh[:, i, TP:].rearrange("p (b n) -> p b n", n=1 + TS)
                    link(dve.tensor_copy(hlast[:, i, 0:1], hh[:, i, TP - 1:TP]))
                    link(dve.tensor_copy(hlast[:, i, 1:9], hv[:, :, TS]))
                    dve.wait_ge(copied, 5 + i)
                    link(dve.tensor_tensor(cat[:, 4 + i, 0:TP], hh[:, i, 0:TP], gg[:, i, 0:TP], ALU.mult))
                    link(dve.tensor_tensor(tok3(cat[:, 4 + i, :]), hv[:, :, 1:], tok3(gg[:, i, :]), ALU.mult))
        with nc.Block() as block:
            @block.sync
            def _(sp):
                net.store(sp, io["lru_tails"], tails[:])
                net.store(sp, io["lru_hlast"], hlast[:])
                net.all_stored(sp)


def log1p(dve, link, e, w, w2, out):
    link(dve.tensor_scalar(w2, e, 2.0, None, ALU.add))
    link(dve.reciprocal(w2, w2))
    link(dve.tensor_tensor(w, e, w2, ALU.mult))
    link(dve.tensor_tensor(w2, w, w, ALU.mult))
    link(dve.tensor_scalar(out, w2, 1.0 / 15, None, ALU.mult))
    for k in (13, 11, 9, 7, 5, 3):
        link(dve.scalar_tensor_tensor(out, out, 1.0 / k, w2, ALU.add, ALU.mult))
    link(dve.scalar_tensor_tensor(out, out, 1.0, w, ALU.add, ALU.mult))
    link(dve.tensor_scalar(out, out, 2.0, None, ALU.mult))


def project_and_norm(net, w_dram, kt, high, low, src, ln_name, layer):
    nc, io = net.nc, net.io
    with ExitStack() as st:
        sb = lambda n, s: st.enter_context(net.buf(n, s))
        wt = SplitWeights(net, st, w_dram, KD, kt, slots=4 if kt > 16 else 3)
        parts = Split(net, src, high, low) if src else None
        sq, mean = sb("sq", [P, 2, T]), sb("mean", [P, T])
        gb_landed, z_done, order = net.sem("gb_landed"), net.sem("z_done"), net.sem("order")
        summed, centred, squared, var_done, root = (net.sem(n) for n in ("summed", "centred", "squared", "var_done", "root"))
        with nc.Block() as block:
            @block.sync
            def _(sp):
                sp.dma_start(net.gb[:], io[ln_name][layer]).then_inc(gb_landed, 16)
                for i in range(len(wt.chunks)):
                    wt.load(sp, i)
                sp.wait_ge(gb_landed, 16)

            @block.tensor
            def _(pe):
                def sum_of(k):
                    pe.wait_ge(z_done, k + 1)
                    for a in range(2):
                        mm = pe.matmul(net.ps[:, 4 + a, 0:HT], net.ones[:], net.x[:, k, HT * a:HT * a + HT], start=(k == 0), stop=(k == KD - 1), skip_group_check=True)
                    return mm

                for m in range(KD):
                    if m >= 2:
                        pe.wait_ge(z_done, m - 1)
                    wt.multiply(pe, m, 2 * (m % 2), high, low, parts.ready if parts else None)
                    if m:
                        sum_of(m - 1)
                sum_of(KD - 1).then_inc(summed, 1)
                for k in range(KD):
                    pe.wait_ge(squared, k + 1)
                    for a in range(2):
                        mm = pe.matmul(net.ps[:, 6 + a, 0:HT], net.ones[:], sq[:, k % 2, HT * a:HT * a + HT], start=(k == 0), stop=(k == KD - 1), skip_group_check=True)
                    mm.then_inc(var_done, 1)

            @block.scalar
            def _(act):
                wt.split_high(act, 0)
                if parts:
                    for k in range(kt):
                        parts.split_high(act, k)
                for i in range(1, len(wt.chunks)):
                    wt.split_high(act, i)
                for k in range(KD):
                    act.wait_ge(centred, k + 1)
                    if k >= 2:
                        act.wait_ge(var_done, k - 1)
                    act.activation(sq[:, k % 2, :], net.x[:, k, :], ACT.Square).then_inc(squared, 1)
                act.wait_ge(root, 1)
                act.activation(net.rstd[:], net.rstd[:], ACT.Sqrt).then_inc(root, 1)

            @block.vector
            def _(dve):
                link = Chain(dve, order)
                wt.split_low(dve, 0)
                if parts:
                    for k in range(kt):
                        parts.split_low(dve, k)
                for i in wt.ahead()[1:]:
                    wt.split_low(dve, i)
                for m in range(KD):
                    wt.product_out(dve, m)
                    dve.scalar_tensor_tensor(halves(net.x[:, m, :]), halves(net.x[:, m, :]), ALPHA, both(net, 2 * (m % 2)), ALU.mult, ALU.add).then_inc(z_done, 1)
                    for i in wt.ahead(m):
                        wt.split_low(dve, i)
                dve.wait_ge(summed, 1)
                link(dve.tensor_scalar(halves(mean[:]), both(net, 4), 1.0 / D, None, ALU.mult))
                for k in range(KD):
                    dve.tensor_tensor(net.x[:, k, :], net.x[:, k, :], mean[:], ALU.subtract).then_inc(centred, 1)
                dve.wait_ge(var_done, KD)
                dve.tensor_scalar(halves(net.rstd[:]), both(net, 6), 1.0 / D, EPS, ALU.mult, ALU.add).then_inc(root, 1)
                dve.wait_ge(root, 2)
                link(dve.reciprocal(net.rstd[:], net.rstd[:]))


def mix_and_norm(net, cat, kt, layer):
    with net.buf("cat_high", [P, kt, T], F32R) as high, net.buf("cat_low", [P, kt, T], F32R) as low:
        project_and_norm(net, net.io[f"w_mix{layer}"], kt, lambda k: high[:, k, :], lambda k: low[:, k, :],
                         lambda k: cat[:, k, :], "ln_mix", layer)


def ffn(net, layer):
    nc, io = net.nc, net.io
    CC = conv_cols(3)
    N = CC - 2
    with ExitStack() as st:
        sb = lambda n, s: st.enter_context(net.buf(n, s))
        gh = st.enter_context(net.buf("g_high", [P, FM, T], F32R))
        gl = st.enter_context(net.buf("g_low", [P, FM, T], F32R))
        with ExitStack() as up:
            sb = lambda n, s: up.enter_context(net.buf(n, s))
            wt = SplitWeights(net, up, io["w_up"][layer], 2 * FM, KD)
            fin = FinishX(net, up)
            ub, uc = sb("ub", [P, 2, CC]), sb("uc", [P, 4, CC])
            par = sb("ffn_par", [P, 2 * FM, 4])
            tails = sb("ffn_tails", [P, 2 * FM, 18])
            hist = tails[:, :, 2:18].rearrange("p m (b n) -> p m b n", n=2)
            small_landed, halo, copied, conved, gelued, order, made, g_high, tailed, zeroed, g_low = (
                net.sem(n) for n in ("small_landed", "halo", "copied", "conved", "gelued", "order", "made", "g_high_done", "tailed", "zeroed", "g_low_done"))
            with nc.Block() as block:
                @block.sync
                def _(sp):
                    sp.dma_start(par[:], io["ffn_par"][layer]).then_inc(small_landed, 16)
                    sp.dma_start(tails[:], io["ffn_hist"][layer]).then_inc(small_landed, 16)
                    for m in range(2 * FM):
                        wt.load(sp, m)

                @block.gpsimd
                def _(pool):
                    pool.memset(ub[:, :, 0:2], 0.0).then_inc(zeroed, 1)
                    pool.wait_ge(small_landed, 32)
                    for m in range(2 * FM + 2):
                        if m >= 2:
                            pool.wait_ge(copied, m - 1)
                            *_, p_tail, s_tail = conv_parts(ub[:, m % 2, :], 3)
                            pool.tensor_copy(tails[:, m - 2, 0:2], p_tail).then_inc(tailed, 1)
                            pool.tensor_copy(tails[:, m - 2, 2:18].rearrange("p (b n) -> p b n", n=2), s_tail).then_inc(tailed, 1)
                            pool.wait_ge(conved, m - 1)
                        if m < 2 * FM:
                            pool.tensor_copy(conv_parts(ub[:, m % 2, :], 3)[2], hist[:, m]).then_inc(halo, 1)

                @block.tensor
                def _(pe):
                    for m in range(2 * FM):
                        if m >= 4:
                            pe.wait_ge(copied, m - 3)
                        wt.multiply(pe, m, 2 * (m % 4), net.high, net.low, fin.ready)

                @block.scalar
                def _(act):
                    def gelu(i):
                        act.wait_ge(conved, 2 * i + 1)
                        u = uc[:, (2 * i) % 4, 0:N]
                        act.activation(u, u, ACT.Gelu_apprx_tanh).then_inc(gelued, 1)

                    def high(i):
                        act.wait_ge(made, i + 1)
                        gp, gs = tokens_of(uc[:, (2 * i) % 4, :], 3)
                        act.activation(gh[:, i, 0:TP], gp, ACT.Copy)
                        act.activation(tok3(gh[:, i, :]), gs, ACT.Copy).then_inc(g_high, 1)

                    wt.split_high(act, 0)
                    fin.on_scalar(act)
                    for i in wt.ahead()[1:]:
                        wt.split_high(act, i)
                    act.wait_ge(zeroed, 1)
                    for m in range(2 * FM):
                        p_tok, s_tok, *_ = conv_parts(ub[:, m % 2, :], 3)
                        wt.product_out(act, m)
                        act.wait_ge(halo, m + 1)
                        copy_to_conv(act, net, 2 * (m % 4), p_tok, s_tok).then_inc(copied, 1)
                        for i in wt.ahead(m):
                            wt.split_high(act, i)
                        if m % 2 == 0 and m >= 2:
                            gelu(m // 2 - 1)
                        if m % 2 and m >= 3:
                            high((m + 1) // 2 - 2)
                    gelu(FM - 1)
                    high(FM - 1)

                @block.vector
                def _(dve):
                    link = Chain(dve, order)

                    def conv(m):
                        x, y = ub[:, m % 2, :], uc[:, m % 4, :]
                        dve.wait_ge(copied, m + 1)
                        if m % 2 == 0 and m >= 4:
                            dve.wait_ge(g_low, m // 2 - 1)
                        link(dve.tensor_scalar(y[:, 0:N], x[:, 0:N], par[:, m, 0:1], par[:, m, 3:4], ALU.mult, ALU.add))
                        link(dve.scalar_tensor_tensor(y[:, 0:N], x[:, 1:1 + N], par[:, m, 1:2], y[:, 0:N], ALU.mult, ALU.add))
                        dve.scalar_tensor_tensor(y[:, 0:N], x[:, 2:2 + N], par[:, m, 2:3], y[:, 0:N], ALU.mult, ALU.add).then_inc(conved, 1)
                        for i in wt.ahead(m):
                            wt.split_low(dve, i)

                    def make(i):
                        u = uc[:, (2 * i) % 4, 0:N]
                        dve.wait_ge(gelued, i + 1)
                        dve.wait_ge(conved, 2 * i + 2)
                        dve.tensor_tensor(u, u, uc[:, (2 * i + 1) % 4, 0:N], ALU.mult).then_inc(made, 1)

                    def low(i):
                        gp, gs = tokens_of(uc[:, (2 * i) % 4, :], 3)
                        dve.wait_ge(g_high, i + 1)
                        dve.tensor_tensor(gl[:, i, 0:TP], gp, gh[:, i, 0:TP].bitcast(F32), ALU.subtract)
                        dve.tensor_tensor(tok3(gl[:, i, :]), gs, tok3(gh[:, i, :]).bitcast(F32), ALU.subtract).then_inc(g_low, 1)

                    wt.split_low(dve, 0)
                    fin.on_vector(dve)
                    for i in wt.ahead()[1:]:
                        wt.split_low(dve, i)
                    dve.wait_ge(small_landed, 32)
                    for i in range(FM):
                        if i >= 2:
                            low(i - 2)
                        conv(2 * i)
                        if i:
                            make(i - 1)
                        conv(2 * i + 1)
                    low(FM - 2)
                    make(FM - 1)
                    low(FM - 1)

            with nc.Block() as block:
                @block.sync
                def _(sp):
                    net.store(sp, io["ffn_tails"][layer], tails[:])
                    net.all_stored(sp)
        project_and_norm(net, io[f"w_down{layer}"], FM, lambda k: gh[:, k, :], lambda k: gl[:, k, :], None, "ln_ffn", layer)


def odd_mixer(net, cat):
    nc, io = net.nc, net.io
    CC = conv_cols(4)
    N = CC - 3
    with ExitStack() as st:
        sb = lambda n, s: st.enter_context(net.buf(n, s))
        cpk = sb("odd_consts", [P, pack(ODD_C).shape[1]])
        c = unpack(cpk, ODD_C)
        zt = sb("zt", [P, 8, T])
        xbc = sb("xbc", [P, 12, T])
        small = sb("odd_small", [P, 48])
        dtr = sb("dtr", [NH, T])
        with ExitStack() as gla_st:
            qk = cat
            vtok, ga = None, None
            vtok = gla_st.enter_context(net.buf("vtok", [P, TT, 512]))
            ga = gla_st.enter_context(net.buf("ga", [16, T]))
            odd_project(net, cpk, small, zt, xbc, dtr, ga, vtok, qk)
            gla(net, c, small, ga, vtok, qk)
        ssd(net, c, small, zt, xbc, dtr, cat)


def odd_project(net, cpk, small, zt, xbc, dtr, ga, vtok, qk):
    nc, io = net.nc, net.io
    CC = conv_cols(4)
    N = CC - 3
    M = 36
    with ExitStack() as st:
        sb = lambda n, s: st.enter_context(net.buf(n, s))
        wt = SplitWeights(net, st, io["w_odd"], M, KD)
        fin = FinishX(net, st)
        w16 = sb("w16", [P, KD, 32])
        ub = sb("ub", [P, 2, CC])
        uc = sb("uc", [P, 2, CC])
        par, hist, tails = sb("conv_par", [P, 12, 5]), sb("conv_hist", [P, 12, NB, 3]), sb("conv_tails", [P, 12, 27])
        vbuf = ub[:, :, 0:T]
        small_landed, prod, copied, conved, order, halo, silued, v_turned, v_kept = (
            net.sem(n) for n in ("small_landed", "prod", "copied", "conved", "order", "halo", "silued", "v_turned", "v_kept"))
        with nc.Block() as block:
            @block.sync
            def _(sp):
                loads = ((par, "ssd_conv_par"), (hist, "ssd_hist"), (cpk, "odd_consts"), (small, "odd_small"), (w16, "w_odd16"))
                for dst, name in loads:
                    sp.dma_start(dst[:], io[name]).then_inc(small_landed, 16)
                for m in range(M):
                    wt.load(sp, m)

            @block.tensor
            def _(pe):
                def turn_v(i):
                    b = 4 + 2 * (i % 2)
                    pe.wait_ge(copied, 32 + i + 1)
                    if i >= 2:
                        pe.wait_ge(v_kept, i - 1)
                    for tt in range(TT):
                        cols, m = tok(tt)
                        out = net.ps[0:m, b, P * tt:P * tt + P] if tt < 4 else net.ps[0:m, b + 1, 0:P]
                        mm = pe.transpose(out, vbuf[:, i % 2, cols], net.ident[:])
                    mm.then_inc(v_turned, 1)

                for m in range(M):
                    if m >= 2:
                        pe.wait_ge(copied, m - 1)
                    wt.multiply(pe, m, 2 * (m % 2), net.high, net.low, fin.ready)
                    if m > 32:
                        turn_v(m - 33)
                turn_v(3)
                pe.wait_ge(small_landed, 80)
                pe.wait_ge(copied, M)
                for i in range(2):
                    products(net, pe, 2 * i, w16[:, :, 16 * i:16 * i + 16], net.x, KD, 16).then_inc(prod, 1)

            @block.gpsimd
            def _(pool):
                pool.wait_ge(small_landed, 80)
                pool.memset(ub[:, :, 0:3], 0.0)
                for m in range(12):
                    if m >= 2:
                        pool.wait_ge(conved, 2 * (m - 1))
                    pool.tensor_copy(conv_parts(ub[:, m % 2, :], 4)[2], hist[:, m]).then_inc(halo, 1)

            @block.scalar
            def _(act):
                def silu_conv(m):
                    act.wait_ge(conved, 2 * m + 2)
                    yp, ys = tokens_of(uc[:, m % 2, :], 4)
                    act.activation(xbc[:, m, 0:TP], yp, ACT.Silu)
                    act.activation(tok3(xbc[:, m, :]), ys, ACT.Silu).then_inc(silued, 1)

                wt.split_high(act, 0)
                fin.on_scalar(act)
                for i in wt.ahead()[1:]:
                    wt.split_high(act, i)
                for m in range(M):
                    b = 2 * (m % 2)
                    wt.product_out(act, m)
                    for i in wt.ahead(m):
                        wt.split_high(act, i)
                    if m < 12:
                        act.wait_ge(halo, m + 1)
                        p_tok, s_tok, *_ = conv_parts(ub[:, m % 2, :], 4)
                        copy_to_conv(act, net, b, p_tok, s_tok).then_inc(copied, 1)
                        if m:
                            silu_conv(m - 1)
                        continue
                    if m == 12:
                        silu_conv(11)
                    if m < 20:
                        act.activation(halves(zt[:, m - 12, :]), both(net, b), ACT.Silu).then_inc(copied, 1)
                    elif m < 24:
                        act.activation(halves(qk[:, 8 + m - 20, :]), both(net, b), ACT.Silu).then_inc(copied, 1)
                    elif m >= 32:
                        if m >= 34:
                            act.wait_ge(v_turned, m - 33)
                        act.activation(halves(vbuf[:, m % 2, :]), both(net, b), ACT.Copy).then_inc(copied, 1)
                    else:
                        act.activation(halves(qk[:, m - 24, :]), both(net, b), ACT.Copy, scale=P ** -0.5 if m < 28 else 1.0).then_inc(copied, 1)
                for i, dst in enumerate((dtr, ga)):
                    act.wait_ge(prod, i + 1)
                    act.activation(halves(dst[:]), both(net, 2 * i, 16), ACT.Copy)

            @block.vector
            def _(dve):
                link = Chain(dve, order)
                wt.split_low(dve, 0)
                fin.on_vector(dve)
                for i in wt.ahead()[1:]:
                    wt.split_low(dve, i)
                dve.wait_ge(small_landed, 80)
                for m in range(12):
                    x, y = ub[:, m % 2, :], uc[:, m % 2, :]
                    dve.wait_ge(copied, m + 1)
                    if m >= 2:
                        dve.wait_ge(silued, m - 1)
                    link(dve.tensor_scalar(y[:, 0:N], x[:, 0:N], par[:, m, 0:1], par[:, m, 4:5], ALU.mult, ALU.add))
                    for k in range(1, 4):
                        ins = dve.scalar_tensor_tensor(y[:, 0:N], x[:, k:k + N], par[:, m, k:k + 1], y[:, 0:N], ALU.mult, ALU.add)
                        if k < 3:
                            link(ins)
                        else:
                            ins.then_inc(conved, 1)
                    *_, p_tail, s_tail = conv_parts(x, 4)
                    link(dve.tensor_copy(tails[:, m, 0:3], p_tail))
                    dve.tensor_copy(tails[:, m, 3:27].rearrange("p (b n) -> p b n", n=3), s_tail).then_inc(conved, 1)
                    for i in wt.ahead(m):
                        wt.split_low(dve, i)
                for m in range(12, M):
                    for i in wt.ahead(m):
                        wt.split_low(dve, i)
                for i in range(4):
                    b = 4 + 2 * (i % 2)
                    dve.wait_ge(v_turned, i + 1)
                    dve.tensor_copy(vtok[:, 0:4, P * i:P * i + P], split_free(net.bank(b), t=4, n=P))
                    dve.tensor_copy(vtok[0:NS, 4, P * i:P * i + P], net.ps[0:NS, b + 1, 0:P]).then_inc(v_kept, 1)
        with nc.Block() as block:
            @block.sync
            def _(sp):
                net.store(sp, io["ssd_tails"], tails[:])
                net.all_stored(sp)


def gla(net, c, small, ga, vtok, qk):
    nc, io = net.nc, net.io
    H = 4
    NC = TP // GCH
    b_al = small[:, 36:40]
    with ExitStack() as st:
        sb = lambda n, s: st.enter_context(net.buf(n, s))
        la, cum, ke = sb("la", [P, H, T]), sb("cum", [P, H, T]), sb("ke", [P, H, T])
        dec = sb("dec", [P, H, NC + NB])
        wa = sb("w_alpha", [16, 512])
        kdt = sb("kdt", [P, TT, 512])
        kdm = sb("kdm", [NS, 2, 512])
        sp_, ss = sb("s_p", [P, H, P]), sb("s_s", [P, NB, H, P])
        att = sb("att", [P, 2, H, P])
        q, k, gg = qk[:, 0:4, :], qk[:, 4:8, :], qk[:, 8:12, :]
        o = la
        step = Steps(net.sem("steps_done"), ["alpha", "biased", "abs", "logs", "cum", "exp_up", "q_done", "exp_down",
                                             "k_done", "left", "exp_left", "kd_done", "turned", "kdt_done"])
        small_landed, order, act_order = net.sem("small_landed"), net.sem("order"), net.sem("act_order")
        state_landed = net.sem("state_landed")

        def ends(ap):
            return ap[:, :, GCH - 1:TP:GCH], ap[:, :, TP + TS - 1:T:TS]

        def chunks(ap):
            return (ap[:, :, 0:TP].rearrange("p h (c n) -> p h c n", n=GCH), ap[:, :, TP:T].rearrange("p h (c n) -> p h c n", n=TS))

        with nc.Block() as block:
            @block.sync
            def _(sp):
                sp.dma_start(wa[:], io["w_alpha"]).then_inc(small_landed, 16)
                sp.dma_start(ss[:], io["gla_s0"]).then_inc(state_landed, 16)
                sp.wait_ge(state_landed, 16)

            @block.tensor
            def _(pe):
                pe.wait_ge(small_landed, 16)
                for h in range(H):
                    for a in range(2):
                        mm = pe.matmul(net.ps[:, 2 * h + a, 0:HT], wa[:, P * h:P * h + P], ga[:, HT * a:HT * a + HT], start=True, stop=True)
                step.done(mm)
                step.after(pe, "kd_done")
                for tt in range(TT):
                    cols, m = tok(tt)
                    for h in range(H):
                        mm = pe.transpose(net.ps[0:m, tt, P * h:P * h + P], k[:, h, cols], net.ident[:])
                step.done(mm)

            @block.scalar
            def _(act):
                step.after(act, "alpha")
                for h in range(H):
                    ins = act.activation(halves(la[:, h, :]), both(net, 2 * h), ACT.Identity, bias=b_al[:, h:h + 1])
                step.done(ins)
                step.after(act, "abs")
                act.activation(cum[:], cum[:], ACT.Exp, scale=-1.0).then_inc(act_order, 1)
                act.wait_ge(act_order, 1)
                step.done(act.activation(cum[:], cum[:], ACT.Ln, bias=1.0))
                step.after(act, "cum")
                for e, d in zip(ends(cum), (dec[:, :, 0:NC], dec[:, :, NC:])):
                    act.activation(d, e, ACT.Exp, scale=1.0 / 16)
                step.done(act.activation(la[:], cum[:], ACT.Exp, scale=1.0 / 16))
                step.after(act, "q_done")
                step.done(act.activation(ke[:], cum[:], ACT.Exp, scale=-1.0 / 16))
                step.after(act, "left")
                step.done(act.activation(la[:], la[:], ACT.Exp, scale=1.0 / 16))
                step.after(act, "turned")
                for tt in range(TT):
                    _, m = tok(tt)
                    ins = act.activation(kdt[0:m, tt, :], net.ps[0:m, tt, :], ACT.Copy)
                step.done(ins)

            @block.vector
            def _(dve):
                link = Chain(dve, order)
                step.after(dve, "biased")
                step.done(dve.scalar_tensor_tensor(cum[:], la[:], -1.0, la[:], ALU.mult, ALU.max))
                step.after(dve, "logs")
                link(dve.scalar_tensor_tensor(la[:], la[:], 0.0, cum[:], ALU.min, ALU.subtract))
                for h in range(H):
                    ins = dve.tensor_tensor_scan(cum[:, h, :], c["gla_keep"], la[:, h, :], 0.0, ALU.mult, ALU.add)
                step.done(ins)
                step.after(dve, "exp_up")
                step.done(dve.tensor_tensor(q, q, la[:], ALU.mult))
                step.after(dve, "exp_down")
                step.done(dve.tensor_tensor(ke[:], ke[:], k, ALU.mult))
                step.after(dve, "k_done")
                for (x, e, y, n, w) in zip(chunks(cum), ends(cum), chunks(la), (NC, NB), (GCH, TS)):
                    for h in range(H):
                        ins = dve.tensor_tensor(y[:, h], e[:, h, :, None].broadcast_to([P, n, w]), x[:, h], ALU.subtract)
                step.done(ins)
                step.after(dve, "exp_left")
                step.done(dve.tensor_tensor(k, k, la[:], ALU.mult))

        scored, masked, o_done, o_kept, inter_done, kv_done, stepped, kdm_done, kv_used = (
            net.sem(n) for n in ("scored", "masked", "o_done", "o_kept", "inter_done", "kv_done", "stepped", "kdm_done", "kv_used"))
        zeroed, squared, normed, root, rms_used, order, made = (net.sem(n) for n in ("zeroed", "squared", "normed", "root", "rms_used", "order", "made"))
        A, O, KV = (0, 1), (2, 3), (4, 5)
        with nc.Block() as block:
            @block.tensor
            def _(pe):
                pe.wait_ge(zeroed, 1)
                n = 0
                for tt in range(TT):
                    cols, m = tok(tt)
                    if tt >= 2:
                        pe.wait_ge(masked, tt - 1)
                    for h in range(H):
                        mm = pe.matmul(net.ps[0:m, A[tt % 2], P * h:P * h + m], ke[:, h, cols], q[:, h, cols], start=True, stop=True)
                    mm.then_inc(scored, 1)
                    pe.wait_ge(masked, tt + 1)
                    if tt >= 2:
                        pe.wait_ge(o_kept, tt - 1)
                    for h in range(H):
                        pe.matmul(net.ps[:, O[tt % 2], P * h:P * h + m], vtok[0:m, tt, P * h:P * h + P], att[0:m, tt % 2, h, 0:m],
                                  start=(h == 0), stop=False, skip_group_check=True)
                    for ch in range(4 if tt < 4 else NB):
                        lo, w = (GCH * ch, GCH) if tt < 4 else (TS * ch, TS)
                        if n >= 2:
                            pe.wait_ge(kv_used, n - 1)
                        if tt == 4:
                            pe.wait_ge(kdm_done, ch + 1)
                        for h in range(H):
                            if tt < 4:
                                lhs, rhs = kdt[lo:lo + w, tt, P * h:P * h + P], vtok[lo:lo + w, tt, P * h:P * h + P]
                            else:
                                lhs, rhs = kdm[:, ch % 2, P * h:P * h + P], vtok[0:NS, 4, P * h:P * h + P]
                            mm = pe.matmul(net.ps[:, KV[n % 2], P * h:P * h + P], lhs, rhs, start=True, stop=True)
                        mm.then_inc(kv_done, 1)
                        if tt < 4:
                            pe.wait_ge(kv_used, n)
                        for h in range(H):
                            s = sp_[:, h, :] if tt < 4 else ss[:, ch, h, :]
                            mm = pe.matmul(net.ps[:, O[tt % 2], P * h + lo:P * h + lo + w], s, q[:, h, cols.start + lo:cols.start + lo + w],
                                           start=False, stop=(h == H - 1 and ch == (3 if tt < 4 else NB - 1)), skip_group_check=True)
                        mm.then_inc(inter_done, 1)
                        n += 1
                for h in range(H):
                    pe.wait_ge(squared, h + 1)
                    if h >= 2:
                        pe.wait_ge(rms_used, h - 1)
                    for a in range(2):
                        mm = pe.matmul(net.ps[:, (6 if h % 2 else 0) + a, 0:HT], net.ones[:], ke[:, h, HT * a:HT * a + HT], start=True, stop=True)
                    mm.then_inc(normed, 1)

            @block.scalar
            def _(act):
                for tt in range(TT):
                    cols, m = tok(tt)
                    act.wait_ge(inter_done, 4 * (tt + 1) if tt < 4 else 16 + NB)
                    act.activation(o[:, :, cols], split_free(net.bank(O[tt % 2]), h=H, n=P)[:, :, 0:m], ACT.Copy).then_inc(o_kept, 1)
                act.wait_ge(o_kept, TT)
                for h in range(H):
                    act.activation(ke[:, h, :], o[:, h, :], ACT.Square).then_inc(squared, 1)
                for h in range(H):
                    act.wait_ge(rms_used, h + 1)
                    act.activation(cum[:, h, :], cum[:, h, :], ACT.Sqrt).then_inc(root, 1)

            @block.gpsimd
            def _(pool):
                for b in range(NB):
                    if b >= 2:
                        pool.wait_ge(kv_done, 16 + b - 1)
                    pool.tensor_scalar(kdm[:, b % 2, :], kdt[0:NS, 4, :], c["of_b"][0:NS, b:b + 1], 1.0, ALU.mult, ALU.mult).then_inc(kdm_done, 1)

            @block.vector
            def _(dve):
                link = Chain(dve, order)
                dve.memset(sp_[:], 0.0).then_inc(zeroed, 1)
                n = 0
                for tt in range(TT):
                    cols, m = tok(tt)
                    mask = (c["upto_g"] if tt < 4 else c["upto_s"])[0:m, None, 0:m].broadcast_to([m, H, m])
                    dve.wait_ge(scored, tt + 1)
                    dve.tensor_tensor(att[0:m, tt % 2, :, 0:m], split_free(net.ps[0:m, A[tt % 2], :], h=H, n=P)[:, :, 0:m], mask, ALU.mult).then_inc(masked, 1)
                    for ch in range(4 if tt < 4 else NB):
                        dve.wait_ge(kv_done, n + 1)
                        dve.wait_ge(inter_done, n + 1)
                        if n == 0:
                            dve.wait_ge(zeroed, 1)
                        elif tt < 4:
                            dve.wait_ge(kv_used, n)
                        for h in range(H):
                            s = sp_[:, h, :] if tt < 4 else ss[:, ch, h, :]
                            ins = dve.scalar_tensor_tensor(s, s, dec[:, h, n:n + 1], net.ps[:, KV[n % 2], P * h:P * h + P], ALU.mult, ALU.add)
                        ins.then_inc(kv_used, 1)
                        n += 1
                dve.wait_ge(squared, H)
                for h in range(H):
                    dve.wait_ge(normed, h + 1)
                    dve.tensor_scalar(halves(cum[:, h, :]), both(net, 6 if h % 2 else 0), 1.0 / P, EPS, ALU.mult, ALU.add).then_inc(rms_used, 1)
                for h in range(H):
                    dve.wait_ge(root, h + 1)
                    link(dve.reciprocal(cum[:, h, :], cum[:, h, :]))
                    link(dve.scalar_tensor_tensor(gg[:, h, :], gg[:, h, :], small[:, 35:36], o[:, h, :], ALU.mult, ALU.mult))
                    link(dve.tensor_tensor(gg[:, h, :], gg[:, h, :], cum[:, h, :], ALU.mult))

            @block.sync
            def _(sp):
                sp.wait_ge(kv_used, 16 + NB)
                net.store(sp, io["gla_s_p"], sp_[:])
                net.store(sp, io["gla_s_s"], ss[:])
                net.all_stored(sp)


def ssd_chunks(net, c, xbc, cum, per, DL, hs_p, hs_s, cat):
    nc, io = net.nc, net.io
    TILE = [4, 0, 1, 2, 3]
    SLOTS = 4 * TT
    XS, BCB, D, Y, OFF, KV = 0, 2, (3, 4), 5, 7, (1, 6)
    kv_at = {s: [] for s in range(SLOTS)}
    kv_no, n_kv = {}, 0
    for s in range(4, SLOTS):
        n, q = divmod(s, 4)
        for key in ([("p", n, q - 2)] if q >= 2 else []) + [("s", (s - 4) // 2, s % 2)]:
            kv_at[s].append((n_kv, key))
            kv_no[key] = n_kv
            n_kv += 1
    with ExitStack() as st:
        sb = lambda n, s: st.enter_context(net.buf(n, s))
        xdt, xdd, xdd_s = sb("xdt", [P, 2, 1024]), sb("xdd", [P, 2, 1024]), sb("xdd_s", [NS, 1024])
        bt, cbm, btm = sb("bt", [P, 2, 2, P]), sb("cbm", [P, 2, 2, P]), sb("btm", [NS, NB, 2, P])
        L = sb("L", [P, 3, 4, P])
        (zeroed, order, decays, clamped, exped, mixed, y_done, y_summed, off_done, xs_turned, xdt_done, xdd_done, bcb_done,
         b_kept, cb_kept, btm_done, hp_decayed, hs_decayed, kv_done, kv_used) = (net.sem(n) for n in (
             "zeroed", "order", "decays", "clamped", "exped", "mixed", "y_done", "y_summed", "off_done", "xs_turned", "xdt_done",
             "xdd_done", "bcb_done", "b_kept", "cb_kept", "btm_done", "hp_decayed", "hs_decayed", "kv_done", "kv_used"))
        with nc.Block() as block:
            @block.tensor
            def _(pe):
                def sum_decays(s):
                    n, q = divmod(s, 4)
                    cols, m = tok(TILE[n])
                    if s >= 2:
                        pe.wait_ge(clamped, s - 1)
                    for i in range(4):
                        mm = pe.matmul(net.ps[0:m, D[s % 2], P * i:P * i + m], split_free(c["one_head"], h=NH, n=P)[0:NH, 4 * q + i, 0:m],
                                       cum[:, cols], start=True, stop=True)
                    mm.then_inc(decays, 1)

                def turn_xs(n, g):
                    cols, m = tok(TILE[n])
                    if n or g:
                        pe.wait_ge(xdt_done, 2 * n + g)
                    for i in range(4):
                        mm = pe.transpose(net.ps[0:m, XS, P * i:P * i + P], xbc[:, 4 * g + i, cols], net.ident[:])
                    mm.then_inc(xs_turned, 1)

                def turn_b(n):
                    cols, m = tok(TILE[n])
                    if n:
                        pe.wait_ge(b_kept, n)
                        pe.wait_ge(cb_kept, n)
                    for g in range(2):
                        pe.transpose(net.ps[0:m, BCB, P * g:P * g + P], xbc[:, 8 + g, cols], net.ident[:])
                    for g in range(2):
                        mm = pe.matmul(net.ps[0:m, BCB, 256 + P * g:256 + P * g + m], xbc[:, 8 + g, cols], xbc[:, 10 + g, cols], start=True, stop=True)
                    mm.then_inc(bcb_done, 1)

                def from_state(n, g):
                    cols, m = tok(TILE[n])
                    pe.wait_ge(y_summed, 2 * n + g)
                    if n > 1:
                        pe.wait_ge(kv_used, kv_no["p", n - 1, g] + 1)
                    else:
                        pe.wait_ge(zeroed, 1)
                    for j in range(4):
                        f = 512 * g + P * j
                        mm = pe.matmul(net.ps[:, OFF, P * j:P * j + P], hs_p[:, f:f + P], xbc[:, 10 + g, cols], start=True, stop=True)
                    mm.then_inc(off_done, 1)

                def new_state(no, key):
                    kind, i, g = key
                    if no >= 2:
                        pe.wait_ge(kv_used, no - 1)
                    if kind == "p":
                        pe.wait_ge(b_kept, i + 1)
                        pe.wait_ge(xdd_done, 2 * i + g + 1)
                        lhs, rhs = bt[:, i % 2, g, :], xdd[:, i % 2, 512 * g:512 * g + 512]
                    else:
                        pe.wait_ge(btm_done, i + 1)
                        pe.wait_ge(xdd_done, 2)
                        lhs, rhs = btm[:, i, g, :], xdd_s[:, 512 * g:512 * g + 512]
                    pe.matmul(net.ps[:, KV[no % 2], :], lhs, rhs, start=True, stop=True).then_inc(kv_done, 1)

                sum_decays(0)
                turn_xs(0, 0)
                turn_b(0)
                turn_xs(0, 1)
                for s in range(SLOTS):
                    n, q = divmod(s, 4)
                    g = q // 2
                    cols, m = tok(TILE[n])
                    if s + 1 < SLOTS:
                        sum_decays(s + 1)
                    if n + 1 < TT:
                        if q == 1:
                            turn_b(n + 1)
                        elif q in (0, 2):
                            turn_xs(n + 1, g)
                    if n and q % 2:
                        from_state(n, g)
                    if q % 2 == 0 and 2 * n + g:
                        pe.wait_ge(y_summed, 2 * n + g)
                    pe.wait_ge(mixed, s + 1)
                    for i in range(4):
                        hd = 4 * q + i
                        lo, at = 64 * (hd % 2), P * (hd % 8 // 2)
                        mm = pe.matmul(net.ps[lo:lo + 64, Y, at:at + m], xdt[0:m, n % 2, 64 * hd:64 * hd + 64], L[0:m, s % 3, i, 0:m], start=True, stop=True)
                    mm.then_inc(y_done, 1)
                    for no, key in kv_at[s]:
                        new_state(no, key)

            @block.scalar
            def _(act):
                def keep_b(n):
                    _, m = tok(TILE[n])
                    act.wait_ge(bcb_done, n + 1)
                    if n == 2:
                        act.wait_ge(btm_done, NB)
                    elif n > 2:
                        act.wait_ge(kv_done, kv_no["p", n - 2, 1] + 1)
                    act.activation(bt[0:m, n % 2, :, :], split_free(net.ps[0:m, BCB, 0:256], g=2, n=P), ACT.Copy).then_inc(b_kept, 1)

                keep_b(0)
                for s in range(SLOTS):
                    n, q = divmod(s, 4)
                    _, m = tok(TILE[n])
                    act.wait_ge(clamped, s + 1)
                    act.activation(L[0:m, s % 3, :, 0:m], L[0:m, s % 3, :, 0:m], ACT.Exp).then_inc(exped, 1)
                    if q == 2 and n + 1 < TT:
                        keep_b(n + 1)

            @block.gpsimd
            def _(pool):
                def leave(n, g):
                    _, m = tok(TILE[n])
                    dst = xdd[0:m, n % 2] if n else xdd_s
                    pool.wait_ge(xdt_done, 2 * n + g + 1)
                    if n > 2:
                        pool.wait_ge(kv_done, kv_no["p", n - 2, g] + 1)
                    pool.tensor_tensor(split_free(dst[:, 512 * g:512 * g + 512], h=8, n=64), split_free(xdt[0:m, n % 2, 512 * g:512 * g + 512], h=8, n=64),
                                       per[0:m, TILE[n], 2, 8 * g:8 * g + 8, None].broadcast_to([m, 8, 64]), ALU.mult).then_inc(xdd_done, 1)

                def decay(s, hs, at, heads):
                    hs = split_free(hs, h=heads, n=64)
                    return pool.tensor_tensor(hs, hs, DL[:, s:s + heads, at:at + 1].broadcast_to([P, heads, 64]), ALU.mult)

                leave(0, 0)
                leave(0, 1)
                pool.wait_ge(b_kept, 1)
                for b in range(NB):
                    pool.tensor_scalar(btm[:, b].rearrange("p g n -> p (g n)"), bt[0:NS, 0].rearrange("p g n -> p (g n)"), c["of_b"][0:NS, b:b + 1], 1.0,
                                       ALU.mult, ALU.mult).then_inc(btm_done, 1)
                b = 0
                for s in range(SLOTS):
                    n, q = divmod(s, 4)
                    if q % 2:
                        if n:
                            pool.wait_ge(off_done, 2 * (n - 1) + q // 2 + 1)
                            decay(8 * (q // 2), hs_p[:, 512 * (q // 2):512 * (q // 2) + 512], TILE[n], 8).then_inc(hp_decayed, 1)
                        if n + 1 < TT:
                            leave(n + 1, q // 2)
                    if b < NB and (s in (1, 2) or (n and q % 2 == 0)):
                        decay(0, hs_s[:, b, :], 4 + b, NH).then_inc(hs_decayed, 1)
                        b += 1

            @block.vector
            def _(dve):
                link = Chain(dve, order)

                def clamp(s):
                    n, q = divmod(s, 4)
                    _, m = tok(TILE[n])
                    dve.wait_ge(decays, s + 1)
                    if s >= 3:
                        dve.wait_ge(y_done, s - 2)
                    for i in range(4):
                        ins = dve.tensor_scalar(L[0:m, s % 3, i, 0:m], net.ps[0:m, D[s % 2], P * i:P * i + m],
                                                per[0:m, TILE[n], 0, 4 * q + i:4 * q + i + 1], 0.0, ALU.subtract, ALU.min)
                    ins.then_inc(clamped, 1)

                def scale_xs(n, g):
                    _, m = tok(TILE[n])
                    dve.wait_ge(xs_turned, 2 * n + g + 1)
                    if n > 1:
                        dve.wait_ge(y_done, 4 * (n - 1))
                    if n > 1:
                        dve.wait_ge(xdd_done, 2 * (n - 1))
                    dve.tensor_tensor(split_free(xdt[0:m, n % 2, 512 * g:512 * g + 512], h=8, n=64), split_free(net.ps[0:m, XS, :], h=8, n=64),
                                      per[0:m, TILE[n], 1, 8 * g:8 * g + 8, None].broadcast_to([m, 8, 64]), ALU.mult).then_inc(xdt_done, 1)

                def mask_cb(n):
                    _, m = tok(TILE[n])
                    mask = (c["upto"] if n else c["upto_s"])[0:m, None, 0:m].broadcast_to([m, 2, m])
                    dve.wait_ge(b_kept, n + 1)
                    dve.tensor_tensor(cbm[0:m, n % 2, :, 0:m], split_free(net.ps[0:m, BCB, 256:512], g=2, n=P)[:, :, 0:m], mask, ALU.mult).then_inc(cb_kept, 1)

                def sum_y(n, g):
                    cols, m = tok(TILE[n])
                    y = split_free(net.bank(Y), j=4, n=P)[:, :, 0:m]
                    out = cat[:, 4 * g:4 * g + 4, cols]
                    if n:
                        dve.wait_ge(off_done, 2 * (n - 1) + g + 1)
                        link(dve.tensor_tensor(out, split_free(net.bank(OFF), j=4, n=P), out, ALU.mult))
                    dve.wait_ge(y_done, 4 * n + 2 * g + 2)
                    dve.tensor_tensor(out, y, out, ALU.add).then_inc(y_summed, 1)

                def add_states(s):
                    for no, (kind, i, g) in kv_at[s]:
                        if kind == "p":
                            dve.wait_ge(hp_decayed, 2 * (i - 1) + g + 1)
                            h = hs_p[:, 512 * g:512 * g + 512]
                        else:
                            dve.wait_ge(hs_decayed, i + 1)
                            h = hs_s[:, i, 512 * g:512 * g + 512]
                        dve.wait_ge(kv_done, no + 1)
                        dve.tensor_tensor(h, h, net.ps[:, KV[no % 2], :], ALU.add).then_inc(kv_used, 1)

                dve.memset(hs_p[:], 0.0).then_inc(zeroed, 1)
                clamp(0)
                scale_xs(0, 0)
                mask_cb(0)
                scale_xs(0, 1)
                for s in range(SLOTS):
                    n, q = divmod(s, 4)
                    _, m = tok(TILE[n])
                    if s and q % 2 == 0:
                        sum_y(*divmod(s // 2 - 1, 2))
                    if s:
                        add_states(s - 1)
                    if s + 1 < SLOTS:
                        clamp(s + 1)
                    dve.wait_ge(exped, s + 1)
                    dve.wait_ge(cb_kept, n + 1)
                    l = L[0:m, s % 3, :, 0:m]
                    dve.tensor_tensor(l, l, cbm[0:m, n % 2, q // 2:q // 2 + 1, 0:m].broadcast_to([m, 4, m]), ALU.mult).then_inc(mixed, 1)
                    if n + 1 < TT:
                        if q == 2:
                            mask_cb(n + 1)
                        elif q % 2:
                            scale_xs(n + 1, q // 2)
                sum_y(TT - 1, 1)
                add_states(SLOTS - 1)

            @block.sync
            def _(sp):
                sp.wait_ge(kv_used, n_kv)
                net.store(sp, io["ssd_s_p"], hs_p[:])
                net.store(sp, io["ssd_s_s"], hs_s[:])
                net.all_stored(sp)


def ssd(net, c, small, zt, xbc, dtr, cat):
    nc, io = net.nc, net.io
    NC = 4
    with ExitStack() as st:
        sb = lambda n, s: st.enter_context(net.buf(n, s))
        cum = sb("cumA", [NH, T])
        DL = sb("DL", [P, NH, NC + NB])
        per = sb("per_tok", [P, TT, 3, NH])
        EA = cat[:, 0:8, :]
        hs_p, hs_s = sb("hs_p", [P, 1024]), sb("hs_s", [P, NB, 1024])
        prep = st.enter_context(ExitStack())
        ps_ = lambda n, s: prep.enter_context(net.buf(n, s))
        dt, w, w2, e = (ps_(n, [NH, T]) for n in ("dt", "w", "w2", "e"))
        na, al, diag = ps_("na", [NH, 1]), ps_("al", [NH, NC + NB]), ps_("diag", [NH, NH, NC + NB])
        names = ["biased", "e_done", "left", "exp_left", "diag_done", "DL_sum", "DL_done", "turned", "per_done"]
        names += [(j, n) for j in range(8) for n in ("EA_sum", "EA_done")]
        step = Steps(net.sem("steps_done"), names)
        order, act_order, state_landed, off_s_done = net.sem("order"), net.sem("act_order"), net.sem("state_landed"), net.sem("off_s_done")
        with nc.Block() as block:
            @block.sync
            def _(sp):
                sp.dma_start(hs_s[:], io["ssd_h0"]).then_inc(state_landed, 16)
                sp.wait_ge(state_landed, 16)

            @block.vector
            def _(dve):
                link = Chain(dve, order)
                link(dve.tensor_scalar(dtr[:], dtr[:], small[0:NH, 0:1], None, ALU.add))
                step.done(dve.scalar_tensor_tensor(e[:], dtr[:], -1.0, dtr[:], ALU.mult, ALU.max))
                step.after(dve, "e_done")
                log1p(dve, link, e[:], w[:], w2[:], dt[:])
                link(dve.scalar_tensor_tensor(dt[:], dtr[:], 0.0, dt[:], ALU.max, ALU.add))
                link(dve.tensor_scalar(w[:], dt[:], na[:], -1.0, ALU.mult, ALU.mult))
                link(dve.tensor_tensor_scan(cum[:], c["ssd_keep"][0:NH, :], w[:], 0.0, ALU.mult, ALU.add))
                link(dve.tensor_copy(al[:, 0:NC], cum[:, SCH - 1:TP:SCH]))
                link(dve.tensor_copy(al[:, NC:], cum[:, TP + TS - 1:T:TS]))
                dve.tensor_tensor(w2[:, 0:TP].rearrange("p (c n) -> p c n", n=SCH), al[:, 0:NC, None].broadcast_to([NH, NC, SCH]),
                                  cum[:, 0:TP].rearrange("p (c n) -> p c n", n=SCH), ALU.subtract)
                step.done(dve.tensor_tensor(tok3(w2[:]), al[:, NC:, None].broadcast_to([NH, NB, TS]), tok3(cum[:]), ALU.subtract))
                step.after(dve, "exp_left")
                step.done(dve.tensor_tensor(diag[:], net.ident[0:NH, 0:NH, None].broadcast_to([NH, NH, NC + NB]),
                                            al[:, None, :].broadcast_to([NH, NH, NC + NB]), ALU.mult))
                step.after(dve, "turned")
                v = split_free(net.ps[:, 1, 0:240], t=TT, q=3, h=NH)
                dve.tensor_copy(per[:, 0:4], v[:, 0:4])
                step.done(dve.tensor_copy(per[0:NS, 4], v[0:NS, 4]))
                step.after(dve, (7, "EA_done"))
                dve.wait_ge(off_s_done, 1)
                dve.tensor_tensor(EA[:, :, TP:T], split_free(net.bank(7), j=8, n=NS), EA[:, :, TP:T], ALU.mult)

            @block.scalar
            def _(act):
                act.activation(na[:], small[0:NH, 1:2], ACT.Exp)
                step.after(act, "biased")
                step.done(act.activation(e[:], e[:], ACT.Exp, scale=-1.0))
                step.after(act, "left")
                step.done(act.activation(w2[:], w2[:], ACT.Exp))
                step.after(act, "DL_sum")
                step.done(act.activation(DL[:].rearrange("p h c -> p (h c)"), net.ps[:, 0, 0:192], ACT.Exp))
                for j in range(8):
                    step.after(act, (j, "EA_sum"))
                    step.done(act.activation(halves(EA[:, j, :]), both(net, 2 + 2 * (j % 2)), ACT.Exp))

            @block.tensor
            def _(pe):
                step.after(pe, "diag_done")
                step.done(pe.matmul(net.ps[:, 0, 0:192], net.ones[0:NH, :], diag[:].rearrange("p h c -> p (h c)"), start=True, stop=True))
                step.after(pe, "DL_done")
                for tt in range(TT):
                    cols, m = tok(tt)
                    for i, src in enumerate((cum, dt, w2)):
                        mm = pe.transpose(net.ps[0:m, 1, 48 * tt + 16 * i:48 * tt + 16 * i + 16], src[:, cols], net.ident[0:NH, 0:NH])
                step.done(mm)
                pe.wait_ge(state_landed, 16)
                for j in range(8):
                    step.after(pe, "per_done" if j == 0 else (j - 1, "EA_done"))
                    lhs, b = split_free(c["two_heads"], j=8, n=P)[0:NH, j, :], 2 + 2 * (j % 2)
                    pe.matmul(net.ps[:, b, 0:HT], lhs, cum[:, 0:HT], start=True, stop=True)
                    step.done(pe.matmul(net.ps[:, b + 1, 0:HT], lhs, cum[:, HT:T], start=True, stop=True))
                    for b in range(NB):
                        mm = pe.matmul(net.ps[:, 7, NS * j + TS * b:NS * j + TS * b + TS], hs_s[:, b, P * j:P * j + P],
                                       xbc[:, 10 + j // 4, TP + TS * b:TP + TS * b + TS], start=True, stop=True)
                mm.then_inc(off_s_done, 1)

        prep.close()
        ssd_chunks(net, c, xbc, cum, per, DL, hs_p, hs_s, cat)

        gated, squared, summed, root, order = (net.sem(n) for n in ("gated", "squared", "summed", "root", "order"))
        with nc.Block() as block:
            @block.vector
            def _(dve):
                link = Chain(dve, order)
                for j in range(8):
                    link(dve.scalar_tensor_tensor(cat[:, j, :], xbc[:, j, :], small[:, 2 + j:3 + j], cat[:, j, :], ALU.mult, ALU.add))
                    dve.tensor_tensor(cat[:, j, :], cat[:, j, :], zt[:, j, :], ALU.mult).then_inc(gated, 1)
                dve.wait_ge(summed, 8)
                r = xbc[:, 0, :]
                dve.tensor_scalar(halves(r), both(net, 0), 1.0 / 1024, EPS, ALU.mult, ALU.add).then_inc(root, 1)
                dve.wait_ge(root, 2)
                link(dve.reciprocal(r, r))
                for j in range(8):
                    dve.scalar_tensor_tensor(cat[:, j, :], cat[:, j, :], small[:, 27 + j:28 + j], r, ALU.mult, ALU.mult)

            @block.scalar
            def _(act):
                for j in range(8):
                    act.wait_ge(gated, j + 1)
                    act.activation(zt[:, j, :], cat[:, j, :], ACT.Square).then_inc(squared, 1)
                act.wait_ge(root, 1)
                act.activation(xbc[:, 0, :], xbc[:, 0, :], ACT.Sqrt).then_inc(root, 1)

            @block.tensor
            def _(pe):
                for j in range(8):
                    pe.wait_ge(squared, j + 1)
                    for a in range(2):
                        mm = pe.matmul(net.ps[:, a, 0:HT], net.ones[:], zt[:, j, HT * a:HT * a + HT], start=(j == 0), stop=(j == 7), skip_group_check=True)
                    mm.then_inc(summed, 1)


def even_mixer(net, cat):
    nc = net.nc
    with ExitStack() as st:
        sb = lambda n, s: st.enter_context(net.buf(n, s))
        cpk = sb("even_consts", [P, pack(EVEN_C).shape[1]])
        c = unpack(cpk, EVEN_C)
        landed = net.sem("consts_landed")
        with nc.Block() as block:
            @block.sync
            def _(sp):
                sp.dma_start(cpk[:], net.io["even_consts"]).then_inc(landed, 16)
                sp.wait_ge(landed, 16)
        lru(net, cat)
        qkv, gates = sb("qkv", [P, TT, 1304]), sb("gates", [P, TT, 24])
        qT, kT = sb("qT", [P, 4, T]), sb("kT", [P, 2, T])
        qTs = sb("qTs", [P, NB, 4, TS])
        wc, ce, on = sb("wc", [P, 4, 4, 32]), sb("ce", [P, 8]), sb("on", [P, 4, 512])
        even_project(net, qkv, gates, c)
        even_rows_out(net, qkv, qT, kT, qTs, c)
        with net.buf("wv4", [P, 2, 4, 4, 32]) as wv4:
            compress_weights(net, wc, wv4, c, ce)
            prompt_compressed(net, qkv, gates, qT, wc, wv4, on, c)
        prompt_attention(net, qkv, gates, qT, kT, on, c)
        turn_outputs(net, on, cat, c)
        sample_attention(net, qkv, gates, kT, qTs, wc, cat, c)


def store_y(net):
    fin = FinishX(net, None)
    with net.nc.Block() as block:
        @block.vector
        def _(dve):
            fin.on_vector(dve)

        @block.sync
        def _(sp):
            for k in range(KD):
                sp.wait_ge(fin.x_done, k + 1)
                net.store(sp, net.io["y"][:, k, :], net.x[:, k, :])
            net.all_stored(sp)


OUTS = {
    "y": [P, KD, T], "kv_p": [TP, 512], "kv_s": [NS, 512], "win_p": [TP, 256], "win_s": [NB, 512, 256],
    "lru_tails": [P, 4, 27], "lru_hlast": [P, 4, 9], "ffn_tails": [2, P, 2 * FM, 18], "ssd_tails": [P, 12, 27],
    "gla_s_p": [P, 4, P], "gla_s_s": [P, NB, 4, P], "ssd_s_p": [P, 1024], "ssd_s_s": [P, NB, 1024],
}


def trunk_kernel(nc, io):
    with ExitStack() as ctx:
        net = Net(nc, ctx, io)
        load_x(net)
        with net.buf("cat", [P, 12, T]) as cat:
            even_mixer(net, cat)
            mix_and_norm(net, cat, 8, 0)
        net.recycle()
        ffn(net, 0)
        net.recycle()
        with net.buf("cat1", [P, 12, T]) as cat:
            odd_mixer(net, cat)
            mix_and_norm(net, cat, 12, 1)
        net.recycle()
        ffn(net, 1)
        store_y(net)


def tiles(w, m=P):
    k = w.shape[0] // P
    return w.reshape(k, P, w.shape[1] // m, m).transpose(2, 1, 0, 3)


def rows(a, n):
    f = a.reshape(a.shape[:-1] + (n, P))
    return np.moveaxis(f, (-1, -2), (0, 1))


def lay_out(i):
    o = {}
    z = np.zeros
    x = np.concatenate([i["x_prompt"][0], i["x_sample"].reshape(NS, D)], 0)
    o["x"] = x.T.reshape(KD, P, T).transpose(1, 0, 2)
    o["ones"], o["ident"] = constants()["ones"], constants()["ident"]
    o["even_consts"] = pack(EVEN_C)
    o["odd_consts"] = pack(ODD_C)
    we = i["w_in_even"][0]
    wq = we[:, 0:512].reshape(D, 2, 4, DH).transpose(0, 2, 1, 3).reshape(D, 512)
    wt = np.concatenate([wq, we[:, 512:1304]], 1)
    o["w_even_tok"] = wt.reshape(KD, P, 1304).transpose(1, 0, 2)
    o["w_lru"] = tiles(we[:, 1304:])
    taps = i["lru_conv_w"][0]
    o["lru_small"] = rows(np.concatenate([taps, i["lru_conv_b"], i["lru_b_gates"][0], i["lru_lambda"]], 0), 4)
    o["lru_hist"] = rows(i["state_lru_conv"][0], 4)
    o["lru_h0"] = rows(i["state_lru_h"][0], 4)
    wg = z((2, 4, P, P), np.float32)
    g = i["lru_w_gates"][0]
    for t in range(4):
        wg[:, t, 0:64, 0:64] = g[:, 2 * t]
        wg[:, t, 64:, 64:] = g[:, 2 * t + 1]
    o["lru_wg"] = wg.reshape(8, P, P).transpose(1, 0, 2)
    cw = i["nsa_cmp_w"][0].reshape(2, 16, 4)
    o["cmp_w"] = np.concatenate([np.tile(cw[0], (8, 1)), np.tile(cw[1], (8, 1))], 1)
    ck = i["cache_nsa_kv"][0].reshape(PHYS, P, 4, P)
    o["cache_kT"] = ck[:, :, 2, :].transpose(0, 2, 1)
    o["cache_tok"] = ck[:, :, [0, 1, 3], :].reshape(PHYS, P, 3 * P)
    win = i["cache_nsa_win"][0].reshape(NB, 512, 2, P)
    o["win_tok"] = win.reshape(NB, 512, 256)
    o["win_kT"] = win[:, :, 0, :].transpose(0, 2, 1)
    o["win_v"] = win[:, :, 1, :].reshape(NB, 4, P, P).transpose(0, 2, 1, 3)
    o["pages"] = i["page_table"].reshape(1, NB * PAGES)
    wo = i["w_out_even"][0]
    wn = wo[0:512].reshape(2, 4, DH, D).transpose(1, 0, 2, 3).reshape(512, D)
    o["w_mix0"] = tiles(np.concatenate([wn, wo[512:]], 0))
    o["w_mix1"] = tiles(i["w_out_odd"][0])
    for n in ("mix", "ffn"):
        o[f"ln_{n}"] = np.stack([np.stack([rows(i[f"ln_{n}_{s}"][k], KD) for s in "gb"], 1) for k in range(2)])
    up, par, hist = [], [], []
    for k in range(2):
        pairs = lambda a: a.reshape(a.shape[:-1] + (2, FM, P)).swapaxes(-2, -3).reshape(a.shape)
        up.append(tiles(pairs(i["ffn_w_up"][k])))
        par.append(rows(pairs(np.concatenate([i["ffn_conv_w"][k], i["ffn_conv_b"][k][None]], 0)), 2 * FM))
        old = rows(pairs(i["state_ffn_conv"][k]), 2 * FM).reshape(P, 2 * FM, 16)
        hist.append(np.concatenate([z((P, 2 * FM, 2), np.float32), old], 2))
        o[f"w_down{k}"] = tiles(i["ffn_w_down"][k])
    o["w_up"], o["ffn_par"], o["ffn_hist"] = np.stack(up), np.stack(par), np.stack(hist)
    w = i["w_in_odd"][0]
    zc, xc, dc, gq, gk, gv, gg, ga = np.split(w, np.cumsum([1024, 1536, 16, 512, 512, 512, 512]), 1)
    o["w_odd"] = tiles(np.concatenate([xc, zc, gg, gq, gk, gv], 1))
    o["w_odd16"] = np.concatenate([dc, ga], 1).reshape(KD, P, 32).transpose(1, 0, 2)
    o["ssd_conv_par"] = rows(np.concatenate([i["ssd_conv_w"][0], i["ssd_conv_b"]], 0), 12)
    o["ssd_hist"] = rows(i["state_ssd_conv"][0], 12)
    s = z((P, 48), np.float32)
    s[0:NH, 0], s[0:NH, 1] = i["ssd_dt_bias"][0], i["ssd_a_log"][0]
    s[:, 2:10] = np.repeat(i["ssd_d"][0], 64).reshape(8, P).T
    s[:, 27:35] = i["ssd_norm_w"][0].reshape(8, P).T
    s[:, 35] = i["gla_norm_w"][0]
    s[:, 36:40] = i["gla_b_alpha"][0].reshape(4, P).T
    o["odd_small"] = s
    o["w_alpha"] = i["gla_w_alpha"][0]
    o["gla_s0"] = i["state_gla"][0].transpose(2, 0, 1, 3)
    o["ssd_h0"] = i["state_ssd"][0].transpose(3, 0, 1, 2).reshape(P, NB, 1024)
    return {k: np.ascontiguousarray(v) for k, v in o.items()}


def undo(r):
    y = r["y"].transpose(2, 1, 0).reshape(T, D)
    back = lambda a: np.moveaxis(a, (0, 1), (-1, -2)).reshape(a.shape[2:] + (-1,))
    lt, lh, st = r["lru_tails"], r["lru_hlast"], r["ssd_tails"]
    sp = lambda a, n: a[:, :, n:].reshape(P, a.shape[1], NB, n)
    ft_p, ft_s = [], []
    for k in range(2):
        f = r["ffn_tails"][k]
        unpair = lambda a: a.reshape(a.shape[:-1] + (FM, 2, P)).swapaxes(-2, -3).reshape(a.shape)
        ft_p.append(unpair(back(f[:, :, 0:2])))
        ft_s.append(unpair(back(sp(f, 2))))
    gp, gs = r["gla_s_p"], r["gla_s_s"]
    hp, hs = r["ssd_s_p"], r["ssd_s_s"]
    return (
        y[None, :TP], y[TP:].reshape(NB, TS, D),
        r["kv_p"].reshape(1, 1, TP, 4, 2, DH), r["kv_s"].reshape(1, NB, TS, 4, 2, DH),
        r["win_p"].reshape(1, 1, TP, 2, 2, DH), r["win_s"].reshape(1, NB, 512, 2, 2, DH),
        back(lh[:, :, 0])[None, None], back(lh[:, :, 1:])[None],
        back(lt[:, :, 0:3])[None, None], back(sp(lt, 3))[None],
        hp.T.reshape(1, 1, NH, DH, P), hs.transpose(1, 2, 0).reshape(1, NB, NH, DH, P),
        back(st[:, :, 0:3])[None, None], back(sp(st, 3))[None],
        gp.transpose(1, 0, 2)[None, None], gs.transpose(1, 2, 0, 3)[None],
        np.stack(ft_p)[:, None], np.stack(ft_s),
    )


def kernel(**inputs):
    import concourse.bacc as bacc
    from concourse.bass_utils import run_bass_kernel_spmd

    nc = bacc.Bacc("TRN2", target_bir_lowering=False, num_devices=1)
    arrays = lay_out({k: np.asarray(v) for k, v in inputs.items()})
    io = {}
    for name, a in arrays.items():
        io[name] = nc.dram_tensor(f"in_{name}", a.shape, mybir.dt.from_np(a.dtype), kind="ExternalInput").ap()
    for name, shape in OUTS.items():
        io[name] = nc.dram_tensor(f"out_{name}", shape, F32, kind="ExternalOutput").ap()
    trunk_kernel(nc, io)
    r = run_bass_kernel_spmd(nc, [{f"in_{k}": v for k, v in arrays.items()}], core_ids=[0])
    got = {n: r.results[0][f"out_{n}"].reshape(s) for n, s in OUTS.items()}
    return tuple(np.ascontiguousarray(a) for a in undo(got))
```

```python
from contextlib import ExitStack

import numpy as np
import concourse.bass as bass
from concourse import mybir

F32 = mybir.dt.float32
I32 = mybir.dt.int32
F32R = mybir.dt.float32r
ALU = mybir.AluOpType
ACT = mybir.ActivationFunctionType
AX = mybir.AxisListType.X

P = 128
D = 1024
KD = D // P
TP, NB, TS = 512, 8, 8
NS = NB * TS
T = TP + NS
HT = T // 2
TT = 5
DH = 64
PAGES, PHYS = 4, 40
NEG = -1e30
LW = 512
DFF = 2816
FM = DFF // P
ALPHA = 4.0 ** 0.25
EPS = 1e-5
SCH = 128
GCH = 32
NH = 16


def tok(tt):
    n = P if tt < 4 else NS
    return slice(P * tt, P * tt + n), n


def constants():
    c = {}
    p = np.arange(P)
    c["ident"] = np.eye(P)
    c["ones"] = np.ones((P, P))
    inv = np.power(np.float32(500000.0), (-2.0 * np.arange(8, dtype=np.float32) / 16).astype(np.float32))
    pos = np.concatenate([np.arange(TP), TP + np.arange(NS) % TS]).astype(np.float32)
    ang = (inv[p % 8, None] * pos[None, :]).astype(np.float32).astype(np.float64)
    turns = (p % DH < 16)[:, None]
    c["rope_c"] = np.where(turns, np.cos(ang), 1.0)
    c["rope_s"] = np.where(turns, np.where(p % 16 < 8, -1.0, 1.0)[:, None] * np.sin(ang), 0.0)
    c["partner"] = np.where(p % DH < 16, p ^ 8, -1)[None, :] == p[:, None]
    c["causal"] = np.where(p[None, :] <= p[:, None], 0.0, NEG)
    n = np.arange(32)
    seen = np.stack([(16 * n[None, :] + 31 <= (P * t + p)[:, None]) & (n[None, :] < 31) for t in range(4)], 1)
    c["cmp_neg"] = np.where(seen, 0.0, NEG)
    c["cmp_01"] = seen * 1.0
    i = (P * np.arange(4)[None, :, None] + p[:, None, None]) - 16 * n[None, None, :]
    c["wc_lo"] = ((i >= 0) & (i < 16) & (n < 31)) * 1.0
    c["wc_hi"] = ((i >= 16) & (i < 32) & (n < 31)) * 1.0
    c["cmp_pad"] = np.broadcast_to(np.where(n < 31, 0.0, NEG), (P, 32))
    c["head4"] = (p[:, None] // 32 == np.arange(4)[None, :]) * 1.0
    b, j, t = p // 32, (p // 8) % 4, p % 8
    c["group"] = ((b[:, None] == b[None, :]) & (t[:, None] == t[None, :])) * 1.0
    kb, kt = np.arange(NS) // TS, np.arange(NS) % TS
    c["new_neg"] = np.stack([np.where((kb[None, :] == (4 * h + b)[:, None]) & (kt[None, :] <= t[:, None]), 0.0, NEG)
                             for h in range(2)], 1)
    c["win_neg"] = np.where(np.arange(8)[None, :] > t[:, None], 0.0, NEG)
    c["row_head"] = (j[:, None] == np.arange(4)[None, :]) * 1.0
    e = np.stack([(np.arange(NS)[:, None] == ((4 * h + b) * TS + t)[None, :]) for h in range(2)], 1) * 1.0
    c["expand"] = np.concatenate([e, np.zeros_like(e)], 0)
    c["blk_no"] = np.broadcast_to(np.arange(1.0, 7.0), (P, 6))
    col = np.arange(T)
    start = np.where(col < TP, col % SCH == 0, (col - TP) % TS == 0)
    c["ssd_keep"] = np.broadcast_to(1.0 - start, (P, T))
    start = np.where(col < TP, col % GCH == 0, (col - TP) % TS == 0)
    c["gla_keep"] = np.broadcast_to(1.0 - start, (P, T))
    c["upto"] = (p[:, None] <= p[None, :]) * 1.0
    s64 = ((kb[:, None] == kb[None, :]) & (kt[:, None] <= kt[None, :])) * 1.0
    c["upto_s"] = np.concatenate([s64, np.zeros_like(s64)], 0)
    c["upto_g"] = ((p[:, None] <= p[None, :]) & (p[:, None] // GCH == p[None, :] // GCH)) * 1.0
    c["of_b"] = np.concatenate([(kb[:, None] == np.arange(NB)[None, :]) * 1.0, np.zeros((64, NB))], 0)
    return {k: np.ascontiguousarray(v, np.float32).reshape(P, -1) for k, v in c.items()}


ROPE_C = ["rope_c", "rope_s", "partner"]
EVEN_C = ["causal", "cmp_neg", "cmp_01", "wc_lo", "wc_hi", "cmp_pad", "head4",
          "group", "new_neg", "win_neg", "row_head", "expand", "blk_no"]
ODD_C = ["ssd_keep", "gla_keep", "upto", "upto_s", "upto_g", "of_b"]


def pack(names):
    c = constants()
    return np.concatenate([c[n] for n in names], 1)


def unpack(tile, names):
    c, at, out = constants(), 0, {}
    for n in names:
        out[n] = tile[:, at:at + c[n].shape[1]]
        at += c[n].shape[1]
    return out


def split_free(ap, **dims):
    names = list(dims)
    return ap.rearrange(f"p ({' '.join(names)}) -> p {' '.join(names)}", **dims)


class Net:

    def __init__(self, nc, ctx, io):
        self.nc, self.ctx, self.io = nc, ctx, io
        self.n_sems = self.n_bufs = 0
        self.live = []
        self.stored, self.n_stored = nc.alloc_semaphore(name="stored"), 0
        self.ps = ctx.enter_context(nc.psum_tensor("ps", [P, 8, 512], F32))
        self.x = ctx.enter_context(self.buf("x", [P, KD, T]))
        self.xh = self.xl = None
        self.gb = ctx.enter_context(self.buf("ln_gb", [P, 2, KD]))
        self.rstd = ctx.enter_context(self.buf("rstd", [P, T]))
        self.ones = ctx.enter_context(self.buf("ones_t", [P, P]))
        self.ident = ctx.enter_context(self.buf("ident_t", [P, P]))

    def store(self, eng, dst, src):
        eng.dma_start(dst, src).then_inc(self.stored, 16)
        self.n_stored += 16

    def all_stored(self, eng):
        eng.wait_ge(self.stored, self.n_stored)

    def buf(self, name, shape, dtype=F32):
        self.n_bufs += 1
        return self.nc.sbuf_tensor(f"{name}_{self.n_bufs}", shape, dtype)

    def sem(self, name):
        self.n_sems += 1
        self.live.append(self.nc.alloc_semaphore(name=f"{name}_{self.n_sems}"))
        return self.live[-1]

    def recycle(self):
        self.nc.clear_and_free_semaphores(self.live)
        self.nc.all_engine_barrier()
        self.live = []

    def high(self, k):
        return self.xh[:, k, :]

    def low(self, k):
        return self.xl[:, k, :]

    def bank(self, b, parts=P):
        return self.ps[0:parts, b, :]


class Chain:

    def __init__(self, eng, sem):
        self.eng, self.sem, self.n = eng, sem, 0

    def __call__(self, ins):
        self.n += 1
        ins.then_inc(self.sem, 1)
        self.eng.wait_ge(self.sem, self.n)


def load_x(net):
    landed = net.sem("x_landed")
    with net.nc.Block() as block:
        @block.sync
        def _(sp):
            sp.dma_start(net.x[:], net.io["x"]).then_inc(landed, 16)
            sp.dma_start(net.ones[:], net.io["ones"]).then_inc(landed, 16)
            sp.dma_start(net.ident[:], net.io["ident"]).then_inc(landed, 16)
            sp.wait_ge(landed, 48)


class Steps:

    def __init__(self, sem, names):
        self.sem, self.at = sem, {n: i + 1 for i, n in enumerate(names)}

    def after(self, eng, name):
        eng.wait_ge(self.sem, self.at[name])

    def done(self, ins):
        ins.then_inc(self.sem, 1)


def prompt_attention(net, past, kv, gates, qT, kT, wc, wv4, cat, c):
    nc, io = net.nc, net.io
    with ExitStack() as st:
        sb = lambda n, s: st.enter_context(net.buf(n, s))
        pTc, cvd = sb("pT_cmp", [P, 2, 4, P]), sb("cvd", [P, 2, 4, DH])
        g5 = gates.rearrange("p t (h j r) -> p t h j r", h=2, r=3)
        with ExitStack() as cs:
            cb = lambda n, s: cs.enter_context(net.buf(n, s))
            ckT, sc, mx, sm = cb("ckT", [P, 32]), cb("sc", [P, 2, 4, 4, 32]), cb("mx", [P, 32]), cb("sm", [P, 2, 4, 4])
            blocks, order, scored, centred, exped, probs, turned, kept = (net.sem(n) for n in (
                "blocks", "order", "scored", "centred", "exped", "probs", "turned", "kept"))
            with nc.Block() as block:
                @block.tensor
                def _(pe):
                    for h in range(2):
                        for tt in range(4):
                            pe.matmul(net.ps[64 * h:64 * h + 64, 0, 0:32], kv[:, tt, 64 * h:64 * h + 64], wc[:, h, tt, :],
                                      start=(tt == 0), stop=(tt == 3))
                    for h in range(2):
                        for tt in range(4):
                            mm = pe.matmul(net.ps[:, 1, 64 * h:64 * h + 64], wv4[:, h, tt].rearrange("p i n -> p (i n)"),
                                           kv[:, tt, P + 64 * h:P + 64 * h + 64], start=(tt == 0), stop=(tt == 3))
                    mm.then_inc(blocks, 1)
                    pe.wait_ge(kept, 1)
                    for h in range(2):
                        for qt in range(4):
                            for j in range(4):
                                mm = pe.matmul(net.ps[:, 4 + h, P * qt + 32 * j:P * qt + 32 * j + 32],
                                               qT[64 * h:64 * h + 64, j, P * qt:P * qt + P], ckT[64 * h:64 * h + 64, :], start=True, stop=True)
                        mm.then_inc(scored, 1)
                    for h in range(2):
                        pe.wait_ge(probs, h + 1)
                        for qt in range(4):
                            mm = pe.transpose(net.ps[:, 2 + h, P * qt:P * qt + P], sc[:, h, qt].rearrange("p j n -> p (j n)"), net.ident[:])
                        mm.then_inc(turned, 1)

                @block.scalar
                def _(act):
                    for h in range(2):
                        act.wait_ge(centred, h + 1)
                        act.activation(sc[:, h], sc[:, h], ACT.Exp).then_inc(exped, 1)
                    for h in range(2):
                        act.wait_ge(turned, h + 1)
                        act.activation(pTc[:, h], split_free(net.bank(2 + h), t=4, n=P), ACT.Copy)

                @block.vector
                def _(dve):
                    link = Chain(dve, order)
                    neg, keep = (split_free(c[n], t=4, n=32)[:, :, None, :].broadcast_to([P, 4, 4, 32]) for n in ("cmp_neg", "cmp_01"))
                    dve.wait_ge(blocks, 1)
                    dve.tensor_copy(ckT[:], net.ps[:, 0, 0:32])
                    for h in range(2):
                        mm = dve.tensor_tensor(cvd[:, h], net.ps[:, 1, None, 64 * h:64 * h + 64].broadcast_to([P, 4, DH]),
                                               c["head4"][:, :, None].broadcast_to([P, 4, DH]), ALU.mult)
                    mm.then_inc(kept, 1)
                    for h in range(2):
                        s16 = sc[:, h].rearrange("p t j n -> p (t j) n")
                        m16 = mx[:, 16 * h:16 * h + 16]
                        dve.wait_ge(scored, h + 1)
                        link(dve.tensor_tensor(sc[:, h], split_free(net.bank(4 + h), t=4, j=4, n=32), neg, ALU.add))
                        link(dve.tensor_reduce(m16, s16, AX, ALU.max))
                        dve.tensor_tensor(s16, s16, m16[:, :, None].broadcast_to([P, 16, 32]), ALU.subtract).then_inc(centred, 1)
                    for h in range(2):
                        s16, r16 = sc[:, h].rearrange("p t j n -> p (t j) n"), sm[:, h].rearrange("p t j -> p (t j)")
                        dve.wait_ge(exped, h + 1)
                        link(dve.tensor_reduce(r16, s16, AX, ALU.add))
                        link(dve.reciprocal(r16, r16))
                        link(dve.tensor_tensor(sm[:, h], sm[:, h], g5[:, 0:4, h, :, 0], ALU.mult))
                        link(dve.tensor_tensor(sc[:, h], sc[:, h], keep, ALU.mult))
                        dve.tensor_tensor(s16, s16, r16[:, :, None].broadcast_to([P, 16, 32]), ALU.mult).then_inc(probs, 1)

        units = [(qt, br, j, h) for qt in range(4) for br in range(2) for j in range(4) for h in range(2)]
        N = len(units)
        probs, pT = sb("probs", [P, 3, 512]), sb("pT", [P, 2, 512])
        diag, nmx, sums, mxp = sb("diag", [P, 3, P]), sb("nmx", [P, 3]), sb("sums", [P, 3]), sb("mxp", [P, 3])
        S, TURNED, OUT = (0, 1, 2), (3, 4), (6, 7)
        scored, maxed, exped, diag_done, turned, turned_in, summed, out_kept, order = (net.sem(n) for n in (
            "scored", "maxed", "exped", "diag_done", "turned", "turned_in", "summed", "out_kept", "order"))
        with nc.Block() as block:
            @block.sync
            def _(sp):
                past.load_ids(sp)
                past.load(sp)
                for tt in range(4):
                    net.store(sp, io["kv_p"][P * tt:P * tt + P, :], kv[:, tt, 0:512])
                    net.store(sp, io["win_p"][P * tt:P * tt + P, :], kv[:, tt, 512:768])
                net.store(sp, io["kv_s"], kv[0:NS, 4, 0:512])
                for b in range(NB):
                    net.store(sp, io["win_s"][b, 504:512, :], kv[TS * b:TS * b + TS, 4, 512:768])
                    net.store(sp, io["win_s"][b, 0:504, :], io["win_tok"][b, 8:512, :])

            @block.tensor
            def _(pe):
                def scores(u):
                    qt, br, j, h = units[u]
                    n = P * (qt + 1)
                    if u >= 3:
                        pe.wait_ge(exped, u - 2)
                    pe.matmul(net.ps[:, S[u % 3], 0:n], qT[64 * h:64 * h + 64, j, P * qt:P * qt + P],
                              kT[64 * h:64 * h + 64, br, 0:n], start=True, stop=True).then_inc(scored, 1)

                def turn(u):
                    pe.wait_ge(diag_done, u + 1)
                    if u >= 2:
                        pe.wait_ge(turned_in, u - 1)
                    for k in range(units[u][0] + 1):
                        mm = pe.matmul(net.ps[:, TURNED[u % 2], P * k:P * k + P], probs[:, u % 3, P * k:P * k + P], diag[:, u % 3, :], start=True, stop=True)
                    mm.then_inc(turned, 1)

                def weigh(u):
                    qt, br, j, h = units[u]
                    bank = OUT[qt % 2]
                    if u % 16 == 0:
                        if qt >= 2:
                            pe.wait_ge(out_kept, qt - 1)
                        for hh in range(2):
                            for jj in range(4):
                                pe.matmul(net.ps[64 * hh:64 * hh + 64, bank, P * jj:P * jj + P], cvd[:, hh, jj, :], pTc[:, hh, qt, :],
                                          start=(jj == 0), stop=False, skip_group_check=True)
                    pe.wait_ge(turned_in, u + 1)
                    v0 = (384 if br == 0 else 640) + 64 * h
                    for k in range(qt + 1):
                        mm = pe.matmul(net.ps[64 * h:64 * h + 64, bank, P * j:P * j + P], kv[:, k, v0:v0 + 64], pT[:, u % 2, P * k:P * k + P],
                                       start=False, stop=(br == 1 and k == qt), skip_group_check=True)
                    mm.then_inc(summed, 1)

                for i in range(N + 4):
                    if i < N:
                        scores(i)
                    if 2 <= i < N + 2:
                        turn(i - 2)
                    if i >= 4:
                        weigh(i - 4)

            @block.scalar
            def _(act):
                for i in range(N + 5):
                    if 3 <= i < N + 3:
                        u = i - 3
                        n = P * (units[u][0] + 1)
                        act.wait_ge(turned, u + 1)
                        if u >= 2:
                            act.wait_ge(summed, u - 1)
                        act.activation(pT[:, u % 2, 0:n], net.ps[:, TURNED[u % 2], 0:n], ACT.Copy).then_inc(turned_in, 1)
                    if i < N:
                        n = P * (units[i][0] + 1)
                        act.wait_ge(maxed, i + 1)
                        if i >= 3:
                            act.wait_ge(turned, i - 2)
                        act.activation(probs[:, i % 3, 0:n], net.ps[:, S[i % 3], 0:n], ACT.Exp, bias=nmx[:, i % 3:i % 3 + 1],
                                       accum_out=sums[:, i % 3:i % 3 + 1]).then_inc(exped, 1)
                    if i >= 20 and i % 16 == 4:
                        qt = i // 16 - 1
                        act.wait_ge(summed, 16 * qt + 16)
                        act.activation(cat[:, 0:4, P * qt:P * qt + P], split_free(net.bank(OUT[qt % 2]), j=4, n=P), ACT.Copy).then_inc(out_kept, 1)

            @block.vector
            def _(dve):
                link = Chain(dve, order)
                for i in range(N + 2):
                    if i >= 2:
                        u = i - 2
                        qt, br, j, h = units[u]
                        r = sums[:, u % 3:u % 3 + 1]
                        dve.wait_ge(exped, u + 1)
                        if u >= 3:
                            dve.wait_ge(turned, u - 2)
                        link(dve.reciprocal(r, r))
                        dve.tensor_scalar(diag[:, u % 3, :], net.ident[:], r, g5[:, qt, h, j, 1 + br:2 + br], ALU.mult, ALU.mult).then_inc(diag_done, 1)
                    if i < N:
                        qt = units[i][0]
                        dve.wait_ge(scored, i + 1)
                        d = net.ps[:, S[i % 3], P * qt:P * qt + P]
                        link(dve.tensor_tensor(d, d, c["causal"], ALU.add))
                        link(dve.tensor_reduce(mxp[:, i % 3:i % 3 + 1], net.ps[:, S[i % 3], 0:P * qt + P], AX, ALU.max))
                        dve.tensor_scalar(nmx[:, i % 3:i % 3 + 1], mxp[:, i % 3:i % 3 + 1], -1.0, None, ALU.mult).then_inc(maxed, 1)


class SamplePast:

    def __init__(self, net, st):
        self.net = net
        sb = lambda n, s, d=F32: st.enter_context(net.buf(n, s, d))
        self.ids = sb("ids", [1, NB * PAGES], I32)
        self.kslc, self.kwin = sb("kslc", [P, NB, PAGES * P]), sb("kwin", [P, NB, 512])
        self.ptok, self.vwin = sb("ptok", [P, NB, PAGES, 3 * P]), sb("vwin", [P, NB, PAGES, P])
        self.ids_landed, self.landed = net.sem("ids_landed"), net.sem("past_landed")
        self.all_landed = 16 * NB * (2 * PAGES + 2)

    def load_ids(self, sp):
        sp.dma_start(self.ids[:], self.net.io["pages"]).then_inc(self.ids_landed, 16)

    def load(self, sp):
        io = self.net.io
        sp.wait_ge(self.ids_landed, 16)
        for b in range(NB):
            for g in range(PAGES):
                page = sp.value_load(self.ids[0:1, b * PAGES + g:b * PAGES + g + 1], min_val=0, max_val=PHYS - 1)
                sp.dma_start(self.kslc[:, b, P * g:P * g + P], io["cache_kT"][bass.ds(page, 1), :, :].rearrange("a p t -> p (a t)")).then_inc(self.landed, 16)
                sp.dma_start(self.ptok[:, b, g, :], io["cache_tok"][bass.ds(page, 1), :, :].rearrange("a p t -> p (a t)")).then_inc(self.landed, 16)
            sp.dma_start(self.kwin[:, b, :], io["win_kT"][b]).then_inc(self.landed, 16)
            sp.dma_start(self.vwin[:, b], io["win_v"][b]).then_inc(self.landed, 16)


def sample_attention(net, past, kv, gates, kT, qTs, wc, cat, c):
    nc, io = net.nc, net.io
    units = [(half, h) for half in range(2) for h in range(2)]
    runs = [(u, br) for u in range(4) for br in range(2)]
    step = Steps(net.sem("steps_done"), ["compressed", "kept", "c_scored", "c_centred", "c_exp", "c_probs", "c_turned", "c_pT", "c_out", "picked",
                                         "summed_up", "o_turned"])
    with ExitStack() as st:
        sb = lambda n, s: st.enter_context(net.buf(n, s))
        ckT, cv = sb("ckTs", [P, NB, 32]), sb("cv", [32, NB, P])
        gx, grow = sb("gx", [P, 2, 24]), sb("grow", [P, 2, 2, 3])
        pc, pcT, psum4 = sb("pc", [P, 4, 32]), sb("pcT", [32, 4, P]), sb("psum4", [P, 4, 8, 4])
        mx4, sum4 = sb("mx4", [P, 4]), sb("sum4", [P, 4])
        imp, cand, pick = sb("imp", [P, 4, 8]), sb("cand", [P, 4, 6]), sb("pick", [P, 4])
        probs, pT = sb("probs", [P, 2, T]), sb("pTs", [P, 2, TT, P])
        nmx, row_sum, mx = sb("nmx", [P, 8]), sb("row_sum", [P, 8]), sb("mx1", [P, 8])
        so, tmp = sb("so", [P, 4, DH]), sb("so_tmp", [P, 8, DH])
        order, scored, maxed, exped, turned, turned_in, out_done = (net.sem(n) for n in (
            "order", "scored", "maxed", "exped", "turned", "turned_in", "out_done"))
        S, TURNED, OUT = ((0, 1), (2, 3)), (4, 5), 6

        def rows_of(u):
            half, h = units[u]
            return qTs[64 * h:64 * h + 64, 4 * half:4 * half + 4].rearrange("p b j t -> p (b j t)")

        with nc.Block() as block:
            @block.tensor
            def _(pe):
                pe.wait_ge(past.landed, past.all_landed)
                for b in range(NB):
                    for h in range(2):
                        for g in range(PAGES):
                            pe.matmul(net.ps[64 * h:64 * h + 64, 0, 32 * b:32 * b + 32], past.ptok[:, b, g, 64 * h:64 * h + 64],
                                      wc[:, h, g, :], start=(g == 0), stop=(g == 3))
                for b in range(NB):
                    for h in range(2):
                        for g in range(PAGES):
                            pe.matmul(net.ps[0:32, 1 + b // 4, P * (b % 4) + 64 * h:P * (b % 4) + 64 * h + 64], wc[:, 2 + h, g, :],
                                      past.ptok[:, b, g, P + 64 * h:P + 64 * h + 64], start=(g == 0), stop=(g == 3))
                for half in range(2):
                    mm = pe.matmul(net.ps[:, 3, 24 * half:24 * half + 24], split_free(c["expand"], h=2, n=P)[0:NS, half, :], gates[0:NS, 4, :],
                                   start=True, stop=True)
                step.done(mm)
                step.after(pe, "kept")
                for h in range(2):
                    for half in range(2):
                        rows = rows_of(2 * half + h)
                        for b in range(4):
                            mm = pe.matmul(net.ps[32 * b:32 * b + 32, 4 + h, 32 * half:32 * half + 32], rows[:, 32 * b:32 * b + 32],
                                           ckT[64 * h:64 * h + 64, 4 * half + b, :], start=True, stop=True)
                step.done(mm)
                step.after(pe, "c_probs")
                pe.matmul(net.ps[:, 7, 256:384], c["group"], pc[:].rearrange("p u n -> p (u n)"), start=True, stop=True)
                for u in range(4):
                    mm = pe.transpose(net.ps[0:32, 3, P * u:P * u + P], pc[:, u, :], net.ident[:])
                step.done(mm)
                step.after(pe, "c_pT")
                for u, (half, h) in enumerate(units):
                    for b in range(4):
                        mm = pe.matmul(net.ps[32 * b:32 * b + 32, 7, 64 * u:64 * u + 64], pcT[:, u, 32 * b:32 * b + 32],
                                       cv[:, 4 * half + b, 64 * h:64 * h + 64], start=True, stop=True)
                step.done(mm)

                def scores(i):
                    u, br = runs[i]
                    half, h = units[u]
                    hp, rows, keys = slice(64 * h, 64 * h + 64), rows_of(u), (past.kslc, past.kwin)[br]
                    a, b_new = S[i % 2]
                    if i >= 2:
                        pe.wait_ge(turned_in, i - 1)
                    for b in range(4):
                        pe.matmul(net.ps[32 * b:32 * b + 32, a, :], rows[:, 32 * b:32 * b + 32], keys[hp, 4 * half + b, :], start=True, stop=True)
                    pe.matmul(net.ps[:, b_new, 0:NS], rows, kT[hp, br, TP:T], start=True, stop=True).then_inc(scored, 1)

                def turn(i):
                    pe.wait_ge(exped, i + 1)
                    for g in range(PAGES):
                        pe.transpose(net.ps[:, TURNED[i % 2], P * g:P * g + P], probs[:, i % 2, P * g:P * g + P], net.ident[:])
                    pe.transpose(net.ps[0:NS, S[i % 2][1], P:2 * P], probs[:, i % 2, TP:T], net.ident[:]).then_inc(turned, 1)

                def weigh(i):
                    u, br = runs[i]
                    half, h = units[u]
                    pe.wait_ge(turned_in, i + 1)
                    v0 = (384 if br == 0 else 640) + 64 * h
                    for b in range(4):
                        out = net.ps[32 * b:32 * b + 32, OUT, 64 * i:64 * i + 64]
                        for g in range(PAGES):
                            v = past.ptok[:, 4 * half + b, g, 2 * P + 64 * h:2 * P + 64 * h + 64] if br == 0 else past.vwin[:, 4 * half + b, g, 64 * h:64 * h + 64]
                            pe.matmul(out, pT[:, i % 2, g, 32 * b:32 * b + 32], v, start=(g == 0), stop=False)
                        mm = pe.matmul(out, pT[0:NS, i % 2, 4, 32 * b:32 * b + 32], kv[0:NS, 4, v0:v0 + 64], start=False, stop=True)
                    mm.then_inc(out_done, 1)

                scores(0)
                for i in range(8):
                    if i + 1 < 8:
                        scores(i + 1)
                    turn(i)
                    if i:
                        weigh(i - 1)
                weigh(7)
                step.after(pe, "summed_up")
                for half in range(2):
                    mm = pe.transpose(net.ps[:, 0, P * half:P * half + P], so[:, 2 * half:2 * half + 2, :].rearrange("p h d -> p (h d)"), net.ident[:])
                step.done(mm)

            @block.scalar
            def _(act):
                step.after(act, "c_centred")
                step.done(act.activation(pc[:], pc[:], ACT.Exp))
                step.after(act, "c_turned")
                step.done(act.activation(pcT[:], split_free(net.ps[0:32, 3, :], u=4, n=P), ACT.Copy))
                for i in range(8):
                    act.wait_ge(maxed, i + 1)
                    act.activation(probs[:, i % 2, :], net.ps[:, S[i % 2][0]:S[i % 2][0] + 2, :].rearrange("p a n -> p (a n)")[:, 0:T], ACT.Exp,
                                   bias=nmx[:, i:i + 1], accum_out=row_sum[:, i:i + 1]).then_inc(exped, 1)
                    act.wait_ge(turned, i + 1)
                    if i >= 2:
                        act.wait_ge(out_done, i - 1)
                    act.activation(pT[:, i % 2, 0:4, :], split_free(net.bank(TURNED[i % 2]), g=4, n=P), ACT.Copy)
                    act.activation(pT[0:NS, i % 2, 4, :], net.ps[0:NS, S[i % 2][1], P:2 * P], ACT.Copy).then_inc(turned_in, 1)
                step.after(act, "o_turned")
                for half in range(2):
                    o = split_free(net.ps[:, 0, P * half:P * half + P], b=4, j=4, t=TS)
                    for j in range(4):
                        act.activation(cat[:, j, TP + 32 * half:TP + 32 * half + 32].rearrange("p (b t) -> p b t", t=TS), o[:, :, j, :], ACT.Copy)

            @block.vector
            def _(dve):
                link = Chain(dve, order)
                neg_new = split_free(c["new_neg"], h=2, n=NS)
                step.after(dve, "compressed")
                dve.tensor_copy(ckT[:], split_free(net.ps[:, 0, 0:256], b=NB, n=32))
                for half in range(2):
                    dve.tensor_copy(cv[:, 4 * half:4 * half + 4], split_free(net.ps[0:32, 1 + half, :], b=4, n=P))
                    link(dve.tensor_tensor(split_free(gx[:, half], h=2, j=4, r=3), split_free(net.ps[:, 3, 24 * half:24 * half + 24], h=2, j=4, r=3),
                                           c["row_head"][:, None, :, None].broadcast_to([P, 2, 4, 3]), ALU.mult))
                    ins = dve.tensor_reduce(grow[:, half], gx[:, half].rearrange("p (h j r) -> p h r j", h=2, r=3), AX, ALU.add)
                step.done(ins)
                step.after(dve, "c_scored")
                for h in range(2):
                    ins = dve.tensor_tensor(pc[:, h:4:2, :], split_free(net.ps[:, 4 + h, 0:64], f=2, n=32), c["cmp_pad"][:, None, :].broadcast_to([P, 2, 32]), ALU.add)
                link(ins)
                link(dve.tensor_reduce(mx4[:], pc[:], AX, ALU.max))
                step.done(dve.tensor_tensor(pc[:], pc[:], mx4[:, :, None].broadcast_to([P, 4, 32]), ALU.subtract))
                step.after(dve, "c_exp")
                link(dve.tensor_reduce(sum4[:], pc[:], AX, ALU.add))
                link(dve.reciprocal(sum4[:], sum4[:]))
                step.done(dve.tensor_tensor(pc[:], pc[:], sum4[:, :, None].broadcast_to([P, 4, 32]), ALU.mult))
                step.after(dve, "c_out")
                c_gate = grow[:].rearrange("p f h r -> p (f h) r")[:, :, 0:1]
                dve.tensor_tensor(so[:], split_free(net.ps[:, 7, 0:256], u=4, n=DH), c_gate.broadcast_to([P, 4, DH]), ALU.mult)
                link(dve.tensor_copy(psum4[:], split_free(net.ps[:, 7, 256:384], u=4, j=8, i=4)))
                link(dve.tensor_reduce(imp[:], psum4[:, :, :, 0:3], AX, ALU.add))
                link(dve.scalar_tensor_tensor(cand[:], psum4[:, :, 1:7, 3], 0.5, imp[:, :, 1:7], ALU.mult, ALU.add))
                link(dve.scalar_tensor_tensor(cand[:], psum4[:, :, 0:6, 3], 0.5, cand[:], ALU.mult, ALU.add))
                link(dve.tensor_reduce(pick[:], cand[:], AX, ALU.min))
                for u in range(4):
                    ins = dve.tensor_scalar(cand[:, u], cand[:, u], pick[:, u:u + 1], None, ALU.is_le)
                link(ins)
                link(dve.tensor_tensor(cand[:], cand[:], c["blk_no"][:, None, :].broadcast_to([P, 4, 6]), ALU.mult))
                link(dve.tensor_reduce(pick[:], cand[:], AX, ALU.max))
                for u in range(4):
                    ins = dve.tensor_scalar(cand[:, u], c["blk_no"], pick[:, u:u + 1], NEG, ALU.is_equal, ALU.mult)
                step.done(ins)
                step.after(dve, "picked")
                for i, (u, br) in enumerate(runs):
                    a, b_new = S[i % 2]
                    dve.wait_ge(scored, i + 1)
                    if br == 0:
                        s = split_free(net.ps[:, a, 64:448], j=6, n=64)
                        link(dve.tensor_tensor(s, s, cand[:, u, :, None].broadcast_to([P, 6, 64]), ALU.add))
                    else:
                        link(dve.tensor_tensor(net.ps[:, a, 0:8], net.ps[:, a, 0:8], c["win_neg"], ALU.add))
                    link(dve.tensor_tensor(net.ps[:, b_new, 0:NS], net.ps[:, b_new, 0:NS], neg_new[:, units[u][0], :], ALU.add))
                    link(dve.tensor_reduce(mx[:, i:i + 1], net.ps[:, a:a + 2, :].rearrange("p a n -> p (a n)")[:, 0:T], AX, ALU.max))
                    dve.tensor_scalar(nmx[:, i:i + 1], mx[:, i:i + 1], -1.0, None, ALU.mult).then_inc(maxed, 1)
                dve.wait_ge(exped, 8)
                link(dve.reciprocal(row_sum[:], row_sum[:]))
                rs = split_free(row_sum[:], u=4, r=2)
                link(dve.tensor_tensor(rs, rs, grow[:].rearrange("p f h r -> p (f h) r")[:, :, 1:3], ALU.mult))
                dve.wait_ge(out_done, 8)
                link(dve.tensor_tensor(tmp[:], split_free(net.bank(OUT), i=8, n=DH), row_sum[:, :, None].broadcast_to([P, 8, DH]), ALU.mult))
                link(dve.tensor_tensor(so[:], so[:], tmp[:, 0:8:2, :], ALU.add))
                step.done(dve.tensor_tensor(so[:], so[:], tmp[:, 1:8:2, :], ALU.add))

            @block.sync
            def _(sp):
                net.all_stored(sp)


def products(net, pe, out_bank, w, x, kt, m=P):
    for a in range(2):
        for k in range(kt):
            mm = pe.matmul(net.ps[0:m, out_bank + a, 0:HT], w[:, k, :], x[:, k, HT * a:HT * a + HT], start=(k == 0), stop=(k == kt - 1))
    return mm


class SplitWeights:

    def __init__(self, net, st, slots, *sources):
        self.net, self.slots = net, slots
        self.chunks, self.tiles = [], []
        size = 0
        for w_dram, n_tiles, kt in sources:
            per = -(-kt // 8)
            n = -(-kt // per)
            size = max(size, n)
            for m in range(n_tiles):
                self.tiles.append((len(self.chunks), len(self.chunks) + per, kt))
                self.chunks += [(w_dram, m, k0, min(n, kt - k0)) for k0 in range(0, kt, n)]
        self.raws = 2
        self.raw = st.enter_context(net.buf("w_raw", [P, self.raws, size, P]))
        self.high = st.enter_context(net.buf("w_high", [P, slots, size, P], F32R))
        self.low = st.enter_context(net.buf("w_low", [P, slots, size, P], F32R))
        self.landed = [net.sem(f"w_landed{i}") for i in range(self.raws)]
        self.high_done, self.low_done, self.used = net.sem("w_high_done"), net.sem("w_low_done"), net.sem("w_used")

    def load(self, sp, i):
        w_dram, m, k0, n = self.chunks[i]
        r = i % self.raws
        if i >= self.raws:
            sp.wait_ge(self.low_done, i - self.raws + 1)
        sp.dma_start(self.raw[:, r, 0:n, :], w_dram[m, :, k0:k0 + n, :]).then_inc(self.landed[r], 16)

    def split_high(self, act, i):
        s, r, n = i % self.slots, i % self.raws, self.chunks[i][3]
        act.wait_ge(self.landed[r], 16 * (i // self.raws + 1))
        if i >= self.slots:
            act.wait_ge(self.used, i - self.slots + 1)
        act.activation(self.high[:, s, 0:n, :], self.raw[:, r, 0:n, :], ACT.Copy).then_inc(self.high_done, 1)

    def split_low(self, dve, i):
        s, r, n = i % self.slots, i % self.raws, self.chunks[i][3]
        dve.wait_ge(self.high_done, i + 1)
        dve.tensor_tensor(self.low[:, s, 0:n, :], self.raw[:, r, 0:n, :], self.high[:, s, 0:n, :].bitcast(F32), ALU.subtract).then_inc(self.low_done, 1)

    def ahead(self, m=None):
        lo, hi = (0, self.slots) if m is None else (self.slots + self.tiles[m][0], self.slots + self.tiles[m][1])
        return range(min(lo, len(self.chunks)), min(hi, len(self.chunks)))

    def multiply(self, pe, m, out_bank, high, low, ready=None):
        start, end, kt = self.tiles[m]
        for i in range(start, end):
            _, _, k0, n = self.chunks[i]
            s = i % self.slots
            pe.wait_ge(self.low_done, i + 1)
            for k in range(n):
                if ready is not None:
                    ready(pe, k0 + k)
                for a in range(2):
                    cols = slice(HT * a, HT * a + HT)
                    out = self.net.ps[:, out_bank + a, 0:HT]
                    first, last = k0 + k == 0, k0 + k == kt - 1
                    pe.matmul(out, self.high[:, s, k, :], high(k0 + k)[:, cols], start=first, stop=False)
                    pe.matmul(out, self.high[:, s, k, :], low(k0 + k)[:, cols], start=False, stop=False)
                    mm = pe.matmul(out, self.low[:, s, k, :], high(k0 + k)[:, cols], start=False, stop=last)
            mm.then_inc(self.used, 1)

    def product_out(self, eng, m):
        eng.wait_ge(self.used, self.tiles[m][1])


class Split:

    def __init__(self, net, src, high, low):
        self.src, self.high, self.low = src, high, low
        self.high_done, self.low_done = net.sem("x_high_done"), net.sem("x_low_done")

    def split_high(self, act, k):
        act.activation(self.high(k), self.src(k), ACT.Copy).then_inc(self.high_done, 1)

    def split_low(self, dve, k):
        dve.wait_ge(self.high_done, k + 1)
        dve.tensor_tensor(self.low(k), self.src(k), self.high(k).bitcast(F32), ALU.subtract).then_inc(self.low_done, 1)

    def ready(self, pe, k):
        pe.wait_ge(self.low_done, k + 1)


class FinishX:

    def __init__(self, net, st, norm=True):
        self.net, self.norm, self.splits = net, norm, st is not None
        if self.splits:
            net.xh = st.enter_context(net.buf("x_high", [P, KD, T], F32R))
            net.xl = st.enter_context(net.buf("x_low", [P, KD, T], F32R))
        self.split = Split(net, lambda k: net.x[:, k, :], lambda k: net.xh[:, k, :], lambda k: net.xl[:, k, :])
        self.scaled, self.x_done = net.sem("x_scaled"), net.sem("x_done")

    def on_vector(self, dve):
        net = self.net
        for k in range(KD + 2):
            if k < KD and self.norm:
                dve.tensor_tensor(net.x[:, k, :], net.x[:, k, :], net.rstd[:], ALU.mult).then_inc(self.scaled, 1)
            if k >= 2 and self.splits:
                if self.norm:
                    dve.wait_ge(self.x_done, k - 1)
                self.split.split_low(dve, k - 2)

    def on_scalar(self, act):
        net = self.net
        for k in range(KD):
            if not self.norm:
                self.split.split_high(act, k)
                continue
            g, b = net.gb[:, 0, k:k + 1], net.gb[:, 1, k:k + 1]
            act.wait_ge(self.scaled, k + 1)
            if self.splits:
                act.activation(net.xh[:, k, :], net.x[:, k, :], ACT.Identity, bias=b, scale=g).then_inc(self.split.high_done, 1)
            act.activation(net.x[:, k, :], net.x[:, k, :], ACT.Identity, bias=b, scale=g).then_inc(self.x_done, 1)

    def ready(self, pe, k):
        self.split.ready(pe, k)


def both(net, b, m=P):
    return net.ps[0:m, b:b + 2, 0:HT]


def wide(net, b, m=P):
    return net.ps[0:m, b:b + 2, :].rearrange("p a n -> p (a n)")[:, 0:T]


def halves(ap):
    return ap.rearrange("p (a n) -> p a n", a=2)


def copy_to_conv(act, net, b, p_tok, s_tok):
    act.activation(p_tok[:, 0:HT], net.ps[:, b, 0:HT], ACT.Copy)
    act.activation(p_tok[:, HT:TP], net.ps[:, b + 1, 0:TP - HT], ACT.Copy)
    return act.activation(s_tok, split_free(net.ps[:, b + 1, TP - HT:HT], b=NB, t=TS), ACT.Copy)


def conv_cols(taps):
    h = taps - 1
    return h + TP + NB * (h + TS)


def conv_parts(buf, taps):
    h = taps - 1
    s = buf[:, h + TP:].rearrange("p (b n) -> p b n", n=h + TS)
    return buf[:, h:h + TP], s[:, :, h:], s[:, :, 0:h], buf[:, TP:TP + h], s[:, :, TS:]


def conv_out_parts(buf, taps):
    h = taps - 1
    s = buf[:, h + TP:]
    return buf[:, 0:TP], [s[:, (h + TS) * b:(h + TS) * b + TS] for b in range(NB)]


def tokens_of(buf, taps):
    h = taps - 1
    return buf[:, 0:TP], buf[:, h + TP:].rearrange("p (b n) -> p b n", n=h + TS)[:, :, 0:TS]


def tok3(ap):
    return ap[:, TP:T].rearrange("p (b t) -> p b t", t=TS)


def even_project(net, cat, kv, gates, qT, kT, qTs, tails, hlast, wc, wv4, ce, c):
    nc, io = net.nc, net.io
    CC = conv_cols(4)
    SC = TP + NB * (1 + TS)
    M = 19
    ROPE = [8, 9, 10, 11, 12, 13, 14]
    TURN = [(15, 12, 0), (16, 13, 256), (16, 15, None), (17, 14, 512), (18, 16, 128), (19, 17, 384), (20, 18, 640)]
    with ExitStack() as st:
        sb = lambda n, s: st.enter_context(net.buf(n, s))
        wt = SplitWeights(net, st, 3, (io["w_even"], M, KD))
        fin = FinishX(net, st, norm=False)
        hx, xc = sb("hx", [P, 4, CC]), sb("xc", [P, 4, CC])
        hh = hx[:, :, 0:SC]
        gg = cat[:, 4:8, :]
        wg = sb("wg", [P, 8, P])
        small = sb("small", [P, 4, 8])
        hist, h0 = sb("hist", [P, 4, NB, 3]), sb("h0", [P, 4, NB])
        rg, ig, la = sb("rg", [P, 2, T]), sb("ig", [P, 2, T]), sb("la", [P, 2, T])
        a, u = sb("a", [P, 2, SC]), sb("u", [P, 4, SC])
        sp8, tmp4 = sb("sp8", [P, 4]), sb("tmp4", [P, 4, 4])
        rope = sb("rope", [P, 2 * T + P])
        rope_c, rope_s, partner = rope[:, 0:T], rope[:, T:2 * T], rope[:, 2 * T:]
        xr, kc = cat[:, 0:3, :], cat[:, 3, :]
        (small_landed, halo, copied, conved, order, lam1, lam2, gated, sig, prep, tanhs, sqrt_in, sqrt_out, uprod, scanned,
         perm_done, roped, turned, kept, lru_done) = (net.sem(n) for n in (
             "small_landed", "halo", "copied", "conved", "order", "lam1", "lam2", "gated", "sig", "prep", "tanhs", "sqrt_in",
             "sqrt_out", "uprod", "scanned", "perm_done", "roped", "turned", "kept", "lru_done"))

        cmp_landed = net.sem("cmp_landed")

        def rope_out(t):
            return qT[:, t - 8, :] if t < 12 else (kc, kT[:, 0, :], kT[:, 1, :])[t - 12]

        def lru_slot(m, first):
            i = (m - first) // 3
            return i if m >= first and (m - first) % 3 == 0 and i < 4 else None

        with nc.Block() as block:
            @block.sync
            def _(sp):
                for m in range(2):
                    wt.load(sp, m)
                for dst, name in ((small, "lru_small"), (hist, "lru_hist"), (h0, "lru_h0"), (wg, "lru_wg"), (rope, "rope_consts")):
                    sp.dma_start(dst[:], io[name]).then_inc(small_landed, 16)
                sp.dma_start(ce[:], io["cmp_w"]).then_inc(cmp_landed, 16)
                for m in range(2, M):
                    wt.load(sp, m)
                sp.wait_ge(lru_done, 1)
                net.store(sp, io["lru_tails"], tails[:])
                net.store(sp, io["lru_hlast"], hlast[:])

            @block.gpsimd
            def _(pool):
                pool.wait_ge(small_landed, 80)
                for i in range(4):
                    p_tok, s_tok, s_hist, _, _ = conv_parts(hx[:, i, :], 4)
                    pool.memset(hx[:, i, 0:3], 0.0)
                    pool.tensor_copy(s_hist, hist[:, i])
                    if i < 2:
                        pool.memset(a[:, i, TP:].rearrange("p (b n) -> p b n", n=1 + TS)[:, :, 0:1], 0.0)
                    ins = pool.tensor_copy(u[:, i, TP:].rearrange("p (b n) -> p b n", n=1 + TS)[:, :, 0], h0[:, i])
                ins.then_inc(halo, 1)
                pool.wait_ge(conved, 4)

                def input_gate(i):
                    xp, xs = tokens_of(xc[:, i, :], 4)
                    uv = u[:, i, TP:].rearrange("p (b n) -> p b n", n=1 + TS)[:, :, 1:]
                    pool.wait_ge(sig, 2 * i + 2)
                    pool.tensor_tensor(u[:, i, 0:TP], ig[:, i % 2, 0:TP], xp, ALU.mult)
                    pool.tensor_tensor(uv, tok3(ig[:, i % 2, :]), xs, ALU.mult).then_inc(uprod, 1)

                def result(i):
                    hv = hh[:, i, TP:].rearrange("p (b n) -> p b n", n=1 + TS)
                    pool.wait_ge(scanned, i + 1)
                    pool.wait_ge(copied, 5 + i)
                    pool.tensor_tensor(cat[:, 4 + i, 0:TP], hh[:, i, 0:TP], gg[:, i, 0:TP], ALU.mult)
                    pool.tensor_tensor(tok3(cat[:, 4 + i, :]), hv[:, :, 1:], tok3(gg[:, i, :]), ALU.mult)

                input_gate(0)
                for i in range(4):
                    if i < 3:
                        input_gate(i + 1)
                    result(i)
                for j in range(4):
                    pool.wait_ge(roped, j + 1)
                    pool.tensor_copy(qTs[:, :, j, :], tok3(qT[:, j, :]))

            @block.tensor
            def _(pe):
                def gate(i, g):
                    if i == 0 and g == 0:
                        pe.wait_ge(small_landed, 80)
                        pe.wait_ge(conved, 4)
                    if 2 * i + g:
                        pe.wait_ge(sig, 2 * i + g)
                    pe.matmul(net.ps[:, 4, :], wg[:, 4 * g + i, :], xc[:, i, 0:TP], start=True, stop=True)
                    pe.matmul(net.ps[:, 5, 0:NS], wg[:, 4 * g + i, :], tokens_of(xc[:, i, :], 4)[1], start=True, stop=True).then_inc(gated, 1)

                def partners(n):
                    t = ROPE[n]
                    pe.wait_ge(copied, t + 1)
                    if n:
                        pe.wait_ge(roped, n)
                    pe.matmul(net.ps[:, 6, 0:HT], partner, xr[:, t % 3, 0:HT], start=True, stop=True)
                    pe.matmul(net.ps[:, 7, 0:HT], partner, xr[:, t % 3, HT:T], start=True, stop=True).then_inc(perm_done, 1)

                def turn(n):
                    _, t, _ = TURN[n]
                    src = rope_out(t) if t < 15 else xr[:, t % 3, :]
                    if t < 15:
                        pe.wait_ge(roped, t - 8 + 1)
                    else:
                        pe.wait_ge(copied, t + 1)
                    if n:
                        pe.wait_ge(kept, n)
                    else:
                        pe.wait_ge(sig, 8)
                    for tt in range(TT):
                        cols, m = tok(tt)
                        out = net.ps[0:m, 4, P * tt:P * tt + P] if tt < 4 else net.ps[0:m, 5, 0:P]
                        mm = pe.transpose(out, src[:, cols], net.ident[:])
                    mm.then_inc(turned, 1)

                for m in range(M + 2):
                    if m < M:
                        if m >= 2:
                            pe.wait_ge(copied, m - 1)
                        wt.multiply(pe, m, 2 * (m % 2), net.high, net.low, fin.ready if m == 0 else None)
                    for g in range(2):
                        i = lru_slot(m, 4 + g)
                        if i is not None:
                            gate(i, g)
                    if m - 1 in ROPE:
                        partners(ROPE.index(m - 1))
                    for n, (slot, _, _) in enumerate(TURN):
                        if slot == m:
                            turn(n)

            @block.scalar
            def _(act):
                def keep(n):
                    _, t, col = TURN[n]
                    act.wait_ge(turned, n + 1)
                    p4, s1 = split_free(net.bank(4), t=4, n=P), net.ps[0:NS, 5, 0:P]
                    if col is None:
                        act.activation(gates[:, 0:4, :], p4[:, :, 0:24], ACT.Sigmoid)
                        act.activation(gates[0:NS, 4, :], s1[:, 0:24], ACT.Sigmoid).then_inc(kept, 1)
                    else:
                        act.activation(kv[:, 0:4, col:col + P], p4, ACT.Copy)
                        act.activation(kv[0:NS, 4, col:col + P], s1, ACT.Copy).then_inc(kept, 1)

                wt.split_high(act, 0)
                fin.on_scalar(act)
                for i in wt.ahead()[1:]:
                    wt.split_high(act, i)
                act.wait_ge(small_landed, 80)
                act.wait_ge(halo, 1)
                for m in range(M + 2):
                    b = 2 * (m % 2)
                    i = lru_slot(m, 7)
                    if i is not None:
                        act.wait_ge(sqrt_in, i + 1)
                        act.activation(la[:, i % 2, :], rg[:, i % 2, :], ACT.Sqrt).then_inc(sqrt_out, 1)
                    if m < M:
                        wt.product_out(act, m)
                        for i in wt.ahead(m):
                            wt.split_high(act, i)
                    if m < 4:
                        p_tok, s_tok, *_ = conv_parts(hx[:, m, :], 4)
                        copy_to_conv(act, net, b, p_tok, s_tok).then_inc(copied, 1)
                    elif m < 8:
                        act.activation(halves(gg[:, m - 4, :]), both(net, b), ACT.Gelu_apprx_tanh).then_inc(copied, 1)
                    elif m < M:
                        if 11 <= m < 18:
                            act.wait_ge(roped, m - 10)
                        elif m == 18:
                            act.wait_ge(turned, 3)
                        act.activation(halves(xr[:, m % 3, :]), both(net, b), ACT.Copy, scale=DH ** -0.5 if m < 12 else 1.0).then_inc(copied, 1)
                    if m == 3:
                        act.wait_ge(lam1, 1)
                        act.activation(tmp4[:, 1, :], tmp4[:, 0, :], ACT.Exp, scale=-1.0).then_inc(lam2, 1)
                    for g in range(2):
                        i = lru_slot(m, 4 + g)
                        if i is not None:
                            act.wait_ge(gated, 2 * i + g + 1)
                            if g and i >= 2:
                                act.wait_ge(uprod, i - 1)
                            act.activation((rg, ig)[g][:, i % 2, :], wide(net, 4), ACT.Sigmoid, bias=small[:, i, 5 + g:6 + g]).then_inc(sig, 1)
                    i = lru_slot(m, 5)
                    if i is not None:
                        act.wait_ge(prep, i + 1)
                        if i >= 2:
                            act.wait_ge(scanned, i - 1)
                        av = a[:, i % 2, TP:].rearrange("p (b n) -> p b n", n=1 + TS)[:, :, 1:]
                        act.activation(a[:, i % 2, 0:TP], la[:, i % 2, 0:TP], ACT.Exp)
                        act.activation(av, tok3(la[:, i % 2, :]), ACT.Exp)
                        act.activation(rg[:, i % 2, :], la[:, i % 2, :], ACT.Tanh).then_inc(tanhs, 1)
                    for n, (slot, _, _) in enumerate(TURN):
                        if slot == m:
                            keep(n)

            @block.vector
            def _(dve):
                link = Chain(dve, order)

                def rope_tile(n):
                    t = ROPE[n]
                    x, out, ps = xr[:, t % 3, :], rope_out(t), both(net, 6)
                    dve.wait_ge(perm_done, n + 1)
                    dve.tensor_tensor(ps, ps, halves(rope_s), ALU.mult)
                    link(dve.tensor_tensor(x, x, rope_c, ALU.mult))
                    dve.tensor_tensor(halves(out), halves(x), ps, ALU.add).then_inc(roped, 1)

                wt.split_low(dve, 0)
                fin.on_vector(dve)
                for i in wt.ahead()[1:]:
                    wt.split_low(dve, i)
                dve.wait_ge(small_landed, 80)
                lam = small[:, :, 7]
                link(dve.scalar_tensor_tensor(tmp4[:, 0, :], lam, -1.0, lam, ALU.mult, ALU.max))
                dve.tensor_scalar(tmp4[:, 2, :], lam, -1.0, 0.0, ALU.mult, ALU.max).then_inc(lam1, 1)
                for m in range(M + 2):
                    if m - 2 in ROPE:
                        rope_tile(ROPE.index(m - 2))
                    if m < M:
                        for i in wt.ahead(m):
                            wt.split_low(dve, i)
                    if m == 18:
                        dve.wait_ge(cmp_landed, 16)
                        lo, hi = (split_free(c[n], t=4, n=32) for n in ("wc_lo", "wc_hi"))
                        for q in range(4):
                            ins = dve.tensor_scalar(wc[:, q], lo, ce[:, q:q + 1], None, ALU.mult)
                        link(ins)
                        for q in range(4):
                            ins = dve.scalar_tensor_tensor(wc[:, q], hi, ce[:, 4 + q:5 + q], wc[:, q], ALU.mult, ALU.add)
                        link(ins)
                        for i in range(4):
                            dve.tensor_copy(wv4[:, :, :, i, :], wc[:, 2:4])
                    if m < 4:
                        dve.wait_ge(copied, m + 1)
                        n = CC - 3
                        x, y = hx[:, m, :], xc[:, m, :]
                        link(dve.tensor_scalar(y[:, 0:n], x[:, 0:n], small[:, m, 0:1], small[:, m, 4:5], ALU.mult, ALU.add))
                        for k in range(1, 4):
                            ins = dve.scalar_tensor_tensor(y[:, 0:n], x[:, k:k + n], small[:, m, k:k + 1], y[:, 0:n], ALU.mult, ALU.add)
                            if k < 3:
                                link(ins)
                            else:
                                ins.then_inc(conved, 1)
                        *_, p_tail, s_tail = conv_parts(x, 4)
                        link(dve.tensor_copy(tails[:, m, 0:3], p_tail))
                        link(dve.tensor_copy(tails[:, m, 3:27].rearrange("p (b n) -> p b n", n=3), s_tail))
                    if m == 4:
                        dve.wait_ge(lam2, 1)
                        log1p(dve, link, tmp4[:, 1, :], tmp4[:, 0, :], tmp4[:, 3, :], sp8[:])
                        link(dve.tensor_tensor(sp8[:], sp8[:], tmp4[:, 2, :], ALU.add))
                        link(dve.tensor_scalar(sp8[:], sp8[:], -8.0, None, ALU.mult))
                    i = lru_slot(m, 5)
                    if i is not None:
                        dve.wait_ge(sig, 2 * i + 1)
                        dve.tensor_scalar(la[:, i % 2, :], rg[:, i % 2, :], sp8[:, i:i + 1], None, ALU.mult).then_inc(prep, 1)
                    i = lru_slot(m, 7)
                    if i is not None:
                        uv = u[:, i, TP:].rearrange("p (b n) -> p b n", n=1 + TS)[:, :, 1:]
                        dve.wait_ge(uprod, i + 1)
                        dve.wait_ge(sqrt_out, i + 1)
                        dve.tensor_tensor(u[:, i, 0:TP], u[:, i, 0:TP], la[:, i % 2, 0:TP], ALU.mult)
                        link(dve.tensor_tensor(uv, uv, tok3(la[:, i % 2, :]), ALU.mult))
                        dve.tensor_tensor_scan(hh[:, i, :], a[:, i % 2, :], u[:, i, :], 0.0, ALU.mult, ALU.add).then_inc(scanned, 1)
                        dve.wait_ge(scanned, i + 1)
                        hv = hh[:, i, TP:].rearrange("p (b n) -> p b n", n=1 + TS)
                        dve.tensor_copy(hlast[:, i, 0:1], hh[:, i, TP - 1:TP])
                        ins = dve.tensor_copy(hlast[:, i, 1:9], hv[:, :, TS])
                        if i == 3:
                            ins.then_inc(lru_done, 1)
                    i = lru_slot(m, 6)
                    if i is not None:
                        dve.wait_ge(tanhs, i + 1)
                        th = rg[:, i % 2, :]
                        link(dve.tensor_scalar(la[:, i % 2, :], th, -1.0, 1.0, ALU.mult, ALU.add))
                        link(dve.reciprocal(la[:, i % 2, :], la[:, i % 2, :]))
                        dve.scalar_tensor_tensor(th, th, -2.0, la[:, i % 2, :], ALU.mult, ALU.mult).then_inc(sqrt_in, 1)


def log1p(dve, link, e, w, w2, out):
    link(dve.tensor_scalar(w2, e, 2.0, None, ALU.add))
    link(dve.reciprocal(w2, w2))
    link(dve.tensor_tensor(w, e, w2, ALU.mult))
    link(dve.tensor_tensor(w2, w, w, ALU.mult))
    link(dve.tensor_scalar(out, w2, 1.0 / 15, None, ALU.mult))
    for k in (13, 11, 9, 7, 5, 3):
        link(dve.scalar_tensor_tensor(out, out, 1.0 / k, w2, ALU.add, ALU.mult))
    link(dve.scalar_tensor_tensor(out, out, 1.0, w, ALU.add, ALU.mult))
    link(dve.tensor_scalar(out, out, 2.0, None, ALU.mult))


class ProjectAndNorm:

    def __init__(self, net, wt, m0, high, low, ready, ln_name, layer, sq, mean):
        self.net, self.wt, self.m0, self.high, self.low, self.ready = net, wt, m0, high, low, ready
        self.gb = net.io[ln_name][layer]
        self.sq, self.mean = sq, mean
        self.gb_landed, self.z_done, self.order, self.summed, self.centred, self.squared, self.var_done, self.root = (
            net.sem(n) for n in ("gb_landed", "z_done", "order", "summed", "centred", "squared", "var_done", "root"))

    def on_sync(self, sp):
        sp.dma_start(self.net.gb[:], self.gb).then_inc(self.gb_landed, 16)
        sp.wait_ge(self.gb_landed, 16)
        self.net.all_stored(sp)

    def on_tensor(self, pe):
        net = self.net

        def sum_of(k):
            pe.wait_ge(self.z_done, k + 1)
            for a in range(2):
                mm = pe.matmul(net.ps[:, 4 + a, 0:HT], net.ones[:], net.x[:, k, HT * a:HT * a + HT], start=(k == 0), stop=(k == KD - 1), skip_group_check=True)
            return mm

        for m in range(KD):
            if m >= 2:
                pe.wait_ge(self.z_done, m - 1)
            self.wt.multiply(pe, self.m0 + m, 2 * (m % 2), self.high, self.low, self.ready if m == 0 else None)
            if m:
                sum_of(m - 1)
        sum_of(KD - 1).then_inc(self.summed, 1)
        for k in range(KD):
            pe.wait_ge(self.squared, k + 1)
            for a in range(2):
                mm = pe.matmul(net.ps[:, 6 + a, 0:HT], net.ones[:], self.sq[:, k % 2, HT * a:HT * a + HT], start=(k == 0), stop=(k == KD - 1), skip_group_check=True)
            mm.then_inc(self.var_done, 1)

    def on_scalar(self, act):
        net = self.net
        for m in range(KD):
            for i in self.wt.ahead(self.m0 + m):
                self.wt.split_high(act, i)
        for k in range(KD):
            act.wait_ge(self.centred, k + 1)
            if k >= 2:
                act.wait_ge(self.var_done, k - 1)
            act.activation(self.sq[:, k % 2, :], net.x[:, k, :], ACT.Square).then_inc(self.squared, 1)
        act.wait_ge(self.root, 1)
        act.activation(net.rstd[:], net.rstd[:], ACT.Sqrt).then_inc(self.root, 1)

    def on_vector(self, dve):
        net, link = self.net, Chain(dve, self.order)
        for m in range(KD):
            for i in self.wt.ahead(self.m0 + m):
                self.wt.split_low(dve, i)
            self.wt.product_out(dve, self.m0 + m)
            dve.scalar_tensor_tensor(halves(net.x[:, m, :]), halves(net.x[:, m, :]), ALPHA, both(net, 2 * (m % 2)), ALU.mult, ALU.add).then_inc(self.z_done, 1)
        dve.wait_ge(self.summed, 1)
        link(dve.tensor_scalar(halves(self.mean), both(net, 4), 1.0 / D, None, ALU.mult))
        for k in range(KD):
            dve.tensor_tensor(net.x[:, k, :], net.x[:, k, :], self.mean, ALU.subtract).then_inc(self.centred, 1)
        dve.wait_ge(self.var_done, KD)
        dve.tensor_scalar(halves(net.rstd[:]), both(net, 6), 1.0 / D, EPS, ALU.mult, ALU.add).then_inc(self.root, 1)
        dve.wait_ge(self.root, 2)
        link(dve.reciprocal(net.rstd[:], net.rstd[:]))


def mix_and_norm(net, cat, kt, layer, norm_w=None):
    nc = net.nc
    with ExitStack() as st:
        cat_high, cat_low = (st.enter_context(net.buf(n, [P, kt, T], F32R)) for n in ("cat_high", "cat_low"))
        high, low = lambda k: cat_high[:, k, :], lambda k: cat_low[:, k, :]
        parts = Split(net, lambda k: cat[:, k, :], high, low)
        wt = SplitWeights(net, st, 3, (net.io[f"w_mix{layer}"], KD, kt))
        sq, mean = st.enter_context(net.buf("sq", [P, 2, T])), st.enter_context(net.buf("mean", [P, T]))
        proj = ProjectAndNorm(net, wt, 0, high, low, parts.ready, "ln_mix", layer, sq, mean[:])

        normed = net.sem("normed")

        def chunk_ks(i):
            _, m, k0, n = wt.chunks[i]
            return range(k0, k0 + n) if m == 0 else ()

        with nc.Block() as block:
            @block.sync
            def _(sp):
                for i in range(len(wt.chunks)):
                    wt.load(sp, i)
                proj.on_sync(sp)

            @block.tensor
            def _(pe):
                proj.on_tensor(pe)

            @block.scalar
            def _(act):
                for i in wt.ahead():
                    wt.split_high(act, i)
                    for k in chunk_ks(i):
                        if norm_w is not None and k < 8:
                            act.wait_ge(normed, k + 1)
                        parts.split_high(act, k)
                proj.on_scalar(act)

            @block.vector
            def _(dve):
                def norm(k):
                    if norm_w is not None and k < 8:
                        dve.scalar_tensor_tensor(cat[:, k, :], cat[:, k, :], norm_w[:, k:k + 1], net.rstd[:], ALU.mult, ALU.mult).then_inc(normed, 1)

                norm(0)
                for i in wt.ahead():
                    wt.split_low(dve, i)
                    for k in chunk_ks(i):
                        norm(k + 1)
                        parts.split_low(dve, k)
                proj.on_vector(dve)


def ffn(net, layer):
    nc, io = net.nc, net.io
    CC = conv_cols(3)
    N = CC - 2
    with ExitStack() as st:
        sb = lambda n, s: st.enter_context(net.buf(n, s))
        tails = sb("ffn_tails", [P, 2 * FM, 18])
        gh = st.enter_context(net.buf("g_high", [P, FM, T], F32R))
        gl = st.enter_context(net.buf("g_low", [P, FM, T], F32R))
        with ExitStack() as up:
            sb = lambda n, s: up.enter_context(net.buf(n, s))
            wt = SplitWeights(net, up, 3, (io["w_up"][layer], 2 * FM, KD), (io[f"w_down{layer}"], KD, FM))
            fin = FinishX(net, up)
            ub, uc = sb("ub", [P, 2, CC]), sb("uc", [P, 4, CC])
            par = sb("ffn_par", [P, 2 * FM, 4])
            hist = tails[:, :, 2:18].rearrange("p m (b n) -> p m b n", n=2)
            small_landed, halo, copied, conved, gelued, order, made, g_high, tailed, zeroed, g_low = (
                net.sem(n) for n in ("small_landed", "halo", "copied", "conved", "gelued", "order", "made", "g_high_done", "tailed", "zeroed", "g_low_done"))
            down = ProjectAndNorm(net, wt, 2 * FM, lambda k: gh[:, k, :], lambda k: gl[:, k, :],
                                  lambda pe, k: pe.wait_ge(g_low, k + 1), "ln_ffn", layer, ub[:, :, 0:T], uc[:, 1, 0:T])
            with nc.Block() as block:
                @block.sync
                def _(sp):
                    for i in range(wt.raws):
                        wt.load(sp, i)
                    sp.dma_start(par[:], io["ffn_par"][layer]).then_inc(small_landed, 16)
                    sp.dma_start(tails[:], io["ffn_hist"][layer]).then_inc(small_landed, 16)
                    for i in range(wt.raws, len(wt.chunks)):
                        wt.load(sp, i)
                    sp.wait_ge(tailed, 4 * FM)
                    net.store(sp, io["ffn_tails"][layer], tails[:])
                    down.on_sync(sp)

                @block.gpsimd
                def _(pool):
                    pool.memset(ub[:, :, 0:2], 0.0).then_inc(zeroed, 1)
                    pool.wait_ge(small_landed, 32)
                    for m in range(2 * FM + 2):
                        if m >= 2:
                            pool.wait_ge(copied, m - 1)
                            *_, p_tail, s_tail = conv_parts(ub[:, m % 2, :], 3)
                            pool.tensor_copy(tails[:, m - 2, 0:2], p_tail).then_inc(tailed, 1)
                            pool.tensor_copy(tails[:, m - 2, 2:18].rearrange("p (b n) -> p b n", n=2), s_tail).then_inc(tailed, 1)
                            pool.wait_ge(conved, m - 1)
                        if m < 2 * FM:
                            pool.tensor_copy(conv_parts(ub[:, m % 2, :], 3)[2], hist[:, m]).then_inc(halo, 1)

                @block.tensor
                def _(pe):
                    for m in range(2 * FM):
                        if m >= 4:
                            pe.wait_ge(copied, m - 3)
                        wt.multiply(pe, m, 2 * (m % 4), net.high, net.low, fin.ready if m == 0 else None)
                    pe.wait_ge(copied, 2 * FM)
                    down.on_tensor(pe)

                @block.scalar
                def _(act):
                    def gelu(i):
                        act.wait_ge(conved, 2 * i + 1)
                        u = uc[:, (2 * i) % 4, 0:N]
                        act.activation(u, u, ACT.Gelu_apprx_tanh).then_inc(gelued, 1)

                    def high(i):
                        act.wait_ge(made, i + 1)
                        gp, gs = tokens_of(uc[:, (2 * i) % 4, :], 3)
                        act.activation(gh[:, i, 0:TP], gp, ACT.Copy)
                        act.activation(tok3(gh[:, i, :]), gs, ACT.Copy).then_inc(g_high, 1)

                    wt.split_high(act, 0)
                    fin.on_scalar(act)
                    for i in wt.ahead()[1:]:
                        wt.split_high(act, i)
                    act.wait_ge(zeroed, 1)
                    for m in range(2 * FM):
                        p_tok, s_tok, *_ = conv_parts(ub[:, m % 2, :], 3)
                        wt.product_out(act, m)
                        act.wait_ge(halo, m + 1)
                        copy_to_conv(act, net, 2 * (m % 4), p_tok, s_tok).then_inc(copied, 1)
                        for i in wt.ahead(m):
                            wt.split_high(act, i)
                        if m % 2 == 0 and m >= 2:
                            gelu(m // 2 - 1)
                        if m % 2 and m >= 3:
                            high((m + 1) // 2 - 2)
                    gelu(FM - 1)
                    high(FM - 1)
                    act.wait_ge(tailed, 4 * FM)
                    down.on_scalar(act)

                @block.vector
                def _(dve):
                    link = Chain(dve, order)

                    def conv(m):
                        x, y = ub[:, m % 2, :], uc[:, m % 4, :]
                        dve.wait_ge(copied, m + 1)
                        if m % 2 == 0 and m >= 4:
                            dve.wait_ge(g_low, m // 2 - 1)
                        link(dve.tensor_scalar(y[:, 0:N], x[:, 0:N], par[:, m, 0:1], par[:, m, 3:4], ALU.mult, ALU.add))
                        link(dve.scalar_tensor_tensor(y[:, 0:N], x[:, 1:1 + N], par[:, m, 1:2], y[:, 0:N], ALU.mult, ALU.add))
                        dve.scalar_tensor_tensor(y[:, 0:N], x[:, 2:2 + N], par[:, m, 2:3], y[:, 0:N], ALU.mult, ALU.add).then_inc(conved, 1)
                        for i in wt.ahead(m):
                            wt.split_low(dve, i)

                    def make(i):
                        u = uc[:, (2 * i) % 4, 0:N]
                        dve.wait_ge(gelued, i + 1)
                        dve.wait_ge(conved, 2 * i + 2)
                        dve.tensor_tensor(u, u, uc[:, (2 * i + 1) % 4, 0:N], ALU.mult).then_inc(made, 1)

                    def low(i):
                        gp, gs = tokens_of(uc[:, (2 * i) % 4, :], 3)
                        dve.wait_ge(g_high, i + 1)
                        dve.tensor_tensor(gl[:, i, 0:TP], gp, gh[:, i, 0:TP].bitcast(F32), ALU.subtract)
                        dve.tensor_tensor(tok3(gl[:, i, :]), gs, tok3(gh[:, i, :]).bitcast(F32), ALU.subtract).then_inc(g_low, 1)

                    wt.split_low(dve, 0)
                    fin.on_vector(dve)
                    for i in wt.ahead()[1:]:
                        wt.split_low(dve, i)
                    dve.wait_ge(small_landed, 32)
                    for i in range(FM):
                        if i >= 2:
                            low(i - 2)
                        conv(2 * i)
                        if i:
                            make(i - 1)
                        conv(2 * i + 1)
                    low(FM - 2)
                    make(FM - 1)
                    low(FM - 1)
                    down.on_vector(dve)



def odd_mixer(net, cat):
    nc, io = net.nc, net.io
    CC = conv_cols(4)
    N = CC - 3
    with ExitStack() as st:
        sb = lambda n, s: st.enter_context(net.buf(n, s))
        cpk = sb("odd_consts", [P, pack(ODD_C).shape[1]])
        c = unpack(cpk, ODD_C)
        zt = sb("zt", [P, 8, T])
        xbc = sb("xbc", [P, 12, T])
        small = sb("odd_small", [P, 48])
        decays = OddDecays(net, c, small)
        decays.kept(st)
        with ExitStack() as gla_st:
            qk = cat
            vtok = gla_st.enter_context(net.buf("vtok", [P, TT, 512]))
            decays.for_gla(gla_st)
            with ExitStack() as project_st:
                decays.passing(project_st, qk)
                odd_project(net, cpk, small, zt, xbc, decays, vtok, qk)
            hs_s = gla_st.enter_context(net.buf("hs_s", [P, NB, 1024]))
            ssd_landed = net.sem("ssd_landed")
            gla(net, c, small, decays, vtok, qk, hs_s, ssd_landed)
            ssd(net, c, small, zt, xbc, decays, cat, hs_s, ssd_landed)
        mix_and_norm(net, cat, 12, 1, small[:, 27:35])


class OddDecays:
    H, NC_G, NC_S = 4, TP // GCH, TP // SCH

    def __init__(self, net, c, small):
        self.net, self.c, self.small = net, c, small
        self.g = Steps(net.sem("gla_steps"), ["raw", "alpha0", "biased0", "alpha1", "biased1", "abs", "exp", "logs", "cum"])
        self.s = Steps(net.sem("ssd_steps"), ["raw", "neg_a", "abs", "exp", "left", "exp_left", "diag", "DL_sum", "DL", "turned", "per"])
        self.order, self.prod, self.wa_landed = net.sem("decays_order"), net.sem("dt_ga_prod"), net.sem("wa_landed")

    def kept(self, st):
        sb = lambda n, s: st.enter_context(self.net.buf(n, s))
        self.cum_a, self.per = sb("cumA", [NH, T]), sb("per_tok", [P, TT, 3, NH])
        self.DL = sb("DL", [P, NH, self.NC_S + NB])

    def for_gla(self, st):
        sb = lambda n, s: st.enter_context(self.net.buf(n, s))
        self.cum = sb("cum", [P, self.H, T])
        self.dec = sb("dec", [P, self.H, self.NC_G + NB])

    def passing(self, st, qk):
        sb = lambda n, s: st.enter_context(self.net.buf(n, s))
        self.na, self.al, self.diag = sb("na", [NH, 1]), sb("al", [NH, self.NC_S + NB]), sb("diag", [NH, NH, self.NC_S + NB])
        self.la = qk[:, 0:4, :]
        self.dtr, self.dt, self.w, self.w2, self.e = (qk[0:NH, i, :] for i in (4, 5, 6, 7, 8))
        self.ga, self.wa = qk[32:48, 9, :], qk[32:48, 10, 0:512]

    def load(self, sp):
        sp.dma_start(self.wa[:], self.net.io["w_alpha"]).then_inc(self.wa_landed, 16)

    def on_tensor(self, pe, m, w48):
        net, g, s = self.net, self.g, self.s
        if m == 6:
            products(net, pe, 4, w48, net.x, KD, 48).then_inc(self.prod, 1)
        elif m in (8, 10):
            i = (m - 8) // 2
            g.after(pe, ("raw", "biased0")[i])
            if i == 0:
                pe.wait_ge(self.wa_landed, 16)
                s.after(pe, "raw")
            for h in (2 * i, 2 * i + 1):
                for a in range(2):
                    mm = pe.matmul(net.ps[:, 4 + 2 * (h % 2) + a, 0:HT], self.wa[:, P * h:P * h + P], self.ga[:, HT * a:HT * a + HT], start=True, stop=True)
            g.done(mm)
        elif m == 21:
            s.after(pe, "diag")
            g.after(pe, "biased1")
            s.done(pe.matmul(net.ps[:, 4, 0:192], net.ones[0:NH, :], self.diag[:].rearrange("p h c -> p (h c)"), start=True, stop=True))
        elif m == 23:
            s.after(pe, "DL")
            for tt in range(TT):
                cols, n = tok(tt)
                for i, src in enumerate((self.cum_a, self.dt, self.w2)):
                    mm = pe.transpose(net.ps[0:n, 5, 48 * tt + 16 * i:48 * tt + 16 * i + 16], src[:, cols], net.ident[0:NH, 0:NH])
            s.done(mm)

    def on_scalar(self, act, m):
        net, g, s, la, cum = self.net, self.g, self.s, self.la, self.cum
        if m == 6:
            act.wait_ge(self.prod, 1)
            s.done(act.activation(halves(self.dtr[:]), both(net, 4, 16), ACT.Copy))
            g.done(act.activation(halves(self.ga[:]), net.ps[32:48, 4:6, 0:HT], ACT.Copy))
        elif m in (8, 10):
            i = (m - 8) // 2
            g.after(act, f"alpha{i}")
            for h in (2 * i, 2 * i + 1):
                ins = act.activation(halves(la[:, h, :]), both(net, 4 + 2 * (h % 2)), ACT.Identity, bias=self.small[:, 36 + h:37 + h])
            g.done(ins)
            if i == 1:
                s.after(act, "raw")
                s.done(act.activation(self.na[:], self.small[0:NH, 1:2], ACT.Exp))
        elif m == 13:
            s.after(act, "abs")
            s.done(act.activation(self.e[:], self.e[:], ACT.Exp, scale=-1.0))
        elif m == 14:
            g.after(act, "abs")
            g.done(act.activation(cum[:], cum[:], ACT.Exp, scale=-1.0))
        elif m == 15:
            g.after(act, "exp")
            g.done(act.activation(cum[:], cum[:], ACT.Ln, bias=1.0))
        elif m == 18:
            g.after(act, "cum")
            for e, d in zip(self.ends(cum), (self.dec[:, :, 0:self.NC_G], self.dec[:, :, self.NC_G:])):
                act.activation(d, e, ACT.Exp, scale=1.0 / 16)
        elif m == 19:
            s.after(act, "left")
            s.done(act.activation(self.w2[:], self.w2[:], ACT.Exp))
        elif m == 21:
            s.after(act, "DL_sum")
            s.done(act.activation(self.DL[:].rearrange("p h c -> p (h c)"), net.ps[:, 4, 0:192], ACT.Exp))

    def ends(self, ap):
        return ap[:, :, GCH - 1:TP:GCH], ap[:, :, TP + TS - 1:T:TS]

    def on_vector(self, dve, m):
        net, c, g, s, la, cum, al = self.net, self.c, self.g, self.s, self.la, self.cum, self.al
        dtr, dt, w, w2, e, cum_a, NC = self.dtr, self.dt, self.w, self.w2, self.e, self.cum_a, self.NC_S
        if m == 11:
            self.link = Chain(dve, self.order)
        link = self.link if m >= 11 else None
        if m == 12:
            s.after(dve, "neg_a")
            link(dve.tensor_scalar(dtr[:], dtr[:], self.small[0:NH, 0:1], None, ALU.add))
            s.done(dve.scalar_tensor_tensor(e[:], dtr[:], -1.0, dtr[:], ALU.mult, ALU.max))
        elif m == 13:
            g.after(dve, "biased1")
            g.done(dve.scalar_tensor_tensor(cum[:], la[:], -1.0, la[:], ALU.mult, ALU.max))
        elif m == 14:
            s.after(dve, "exp")
            log1p(dve, link, e[:], w[:], w2[:], dt[:])
            link(dve.scalar_tensor_tensor(dt[:], dtr[:], 0.0, dt[:], ALU.max, ALU.add))
        elif m == 15:
            link(dve.tensor_scalar(w[:], dt[:], self.na[:], -1.0, ALU.mult, ALU.mult))
            link(dve.tensor_tensor_scan(cum_a[:], c["ssd_keep"][0:NH, :], w[:], 0.0, ALU.mult, ALU.add))
        elif m == 16:
            g.after(dve, "logs")
            link(dve.scalar_tensor_tensor(la[:], la[:], 0.0, cum[:], ALU.min, ALU.subtract))
        elif m == 17:
            for h in range(self.H):
                ins = dve.tensor_tensor_scan(cum[:, h, :], c["gla_keep"], la[:, h, :], 0.0, ALU.mult, ALU.add)
            g.done(ins)
        elif m == 18:
            link(dve.tensor_copy(al[:, 0:NC], cum_a[:, SCH - 1:TP:SCH]))
            link(dve.tensor_copy(al[:, NC:], cum_a[:, TP + TS - 1:T:TS]))
            dve.tensor_tensor(w2[:, 0:TP].rearrange("p (c n) -> p c n", n=SCH), al[:, 0:NC, None].broadcast_to([NH, NC, SCH]),
                              cum_a[:, 0:TP].rearrange("p (c n) -> p c n", n=SCH), ALU.subtract)
            s.done(dve.tensor_tensor(tok3(w2[:]), al[:, NC:, None].broadcast_to([NH, NB, TS]), tok3(cum_a[:]), ALU.subtract))
        elif m == 20:
            s.after(dve, "exp_left")
            s.done(dve.tensor_tensor(self.diag[:], net.ident[0:NH, 0:NH, None].broadcast_to([NH, NH, NC + NB]),
                                     al[:, None, :].broadcast_to([NH, NH, NC + NB]), ALU.mult))
        elif m == 23:
            s.after(dve, "turned")
            v = split_free(net.ps[:, 5, 0:240], t=TT, q=3, h=NH)
            dve.tensor_copy(self.per[:, 0:4], v[:, 0:4])
            s.done(dve.tensor_copy(self.per[0:NS, 4], v[0:NS, 4]))


def odd_project(net, cpk, small, zt, xbc, decays, vtok, qk):
    nc, io = net.nc, net.io
    CC = conv_cols(4)
    N = CC - 3
    M = 36
    with ExitStack() as st:
        sb = lambda n, s: st.enter_context(net.buf(n, s))
        wt = SplitWeights(net, st, 3, (io["w_odd"], M, KD))
        fin = FinishX(net, st)
        w48 = sb("w48", [P, KD, 48])
        ub = sb("ub", [P, 2, CC])
        uc = sb("uc", [P, 2, CC])
        par, hist, tails = sb("conv_par", [P, 12, 5]), sb("conv_hist", [P, 12, NB, 3]), sb("conv_tails", [P, 12, 27])
        vbuf = ub[:, :, 0:T]
        small_landed, copied, conved, order, halo, silued, v_turned, v_kept = (
            net.sem(n) for n in ("small_landed", "copied", "conved", "order", "halo", "silued", "v_turned", "v_kept"))
        with nc.Block() as block:
            @block.sync
            def _(sp):
                loads = ((par, "ssd_conv_par"), (hist, "ssd_hist"), (cpk, "odd_consts"), (small, "odd_small"), (w48, "w_odd48"))
                for m in range(wt.raws):
                    wt.load(sp, m)
                for dst, name in loads:
                    sp.dma_start(dst[:], io[name]).then_inc(small_landed, 16)
                decays.load(sp)
                for m in range(wt.raws, M):
                    wt.load(sp, m)

            @block.tensor
            def _(pe):
                def turn_v(i):
                    b = 4 + 2 * (i % 2)
                    if i == 0:
                        decays.s.after(pe, "per")
                    pe.wait_ge(copied, 32 + i + 1)
                    if i >= 2:
                        pe.wait_ge(v_kept, i - 1)
                    for tt in range(TT):
                        cols, m = tok(tt)
                        out = net.ps[0:m, b, P * tt:P * tt + P] if tt < 4 else net.ps[0:m, b + 1, 0:P]
                        mm = pe.transpose(out, vbuf[:, i % 2, cols], net.ident[:])
                    mm.then_inc(v_turned, 1)

                for m in range(M):
                    if m >= 2:
                        pe.wait_ge(copied, m - 1)
                    if m == 6:
                        pe.wait_ge(small_landed, 80)
                    decays.on_tensor(pe, m, w48)
                    wt.multiply(pe, m, 2 * (m % 2), net.high, net.low, fin.ready if m == 0 else None)
                    if m > 32:
                        turn_v(m - 33)
                turn_v(3)

            @block.gpsimd
            def _(pool):
                pool.wait_ge(small_landed, 80)
                pool.memset(ub[:, :, 0:3], 0.0)
                for m in range(12):
                    if m >= 2:
                        pool.wait_ge(conved, 2 * (m - 1))
                    pool.tensor_copy(conv_parts(ub[:, m % 2, :], 4)[2], hist[:, m]).then_inc(halo, 1)

            @block.scalar
            def _(act):
                def silu_conv(m):
                    act.wait_ge(conved, 2 * m + 2)
                    yp, ys = tokens_of(uc[:, m % 2, :], 4)
                    act.activation(xbc[:, m, 0:TP], yp, ACT.Silu)
                    act.activation(tok3(xbc[:, m, :]), ys, ACT.Silu).then_inc(silued, 1)

                wt.split_high(act, 0)
                fin.on_scalar(act)
                for i in wt.ahead()[1:]:
                    wt.split_high(act, i)
                for m in range(M):
                    b = 2 * (m % 2)
                    wt.product_out(act, m)
                    for i in wt.ahead(m):
                        wt.split_high(act, i)
                    if m:
                        decays.on_scalar(act, m - 1)
                    if m < 12:
                        act.wait_ge(halo, m + 1)
                        p_tok, s_tok, *_ = conv_parts(ub[:, m % 2, :], 4)
                        copy_to_conv(act, net, b, p_tok, s_tok).then_inc(copied, 1)
                        if m:
                            silu_conv(m - 1)
                        continue
                    if m == 12:
                        silu_conv(11)
                    if m == 24:
                        decays.s.after(act, "per")
                    if m < 20:
                        act.activation(halves(zt[:, m - 12, :]), both(net, b), ACT.Silu).then_inc(copied, 1)
                    elif m < 24:
                        act.activation(halves(qk[:, 8 + m - 20, :]), both(net, b), ACT.Silu).then_inc(copied, 1)
                    elif m >= 32:
                        if m >= 34:
                            act.wait_ge(v_turned, m - 33)
                        act.activation(halves(vbuf[:, m % 2, :]), both(net, b), ACT.Copy).then_inc(copied, 1)
                    else:
                        act.activation(halves(qk[:, m - 24, :]), both(net, b), ACT.Copy, scale=P ** -0.5 if m < 28 else 1.0).then_inc(copied, 1)

            @block.vector
            def _(dve):
                link = Chain(dve, order)
                wt.split_low(dve, 0)
                fin.on_vector(dve)
                for i in wt.ahead()[1:]:
                    wt.split_low(dve, i)
                dve.wait_ge(small_landed, 80)
                for m in range(12):
                    x, y = ub[:, m % 2, :], uc[:, m % 2, :]
                    dve.wait_ge(copied, m + 1)
                    if m >= 2:
                        dve.wait_ge(silued, m - 1)
                    link(dve.tensor_scalar(y[:, 0:N], x[:, 0:N], par[:, m, 0:1], par[:, m, 4:5], ALU.mult, ALU.add))
                    for k in range(1, 4):
                        ins = dve.scalar_tensor_tensor(y[:, 0:N], x[:, k:k + N], par[:, m, k:k + 1], y[:, 0:N], ALU.mult, ALU.add)
                        if k < 3:
                            link(ins)
                        else:
                            ins.then_inc(conved, 1)
                    *_, p_tail, s_tail = conv_parts(x, 4)
                    link(dve.tensor_copy(tails[:, m, 0:3], p_tail))
                    dve.tensor_copy(tails[:, m, 3:27].rearrange("p (b n) -> p b n", n=3), s_tail).then_inc(conved, 1)
                    for i in wt.ahead(m):
                        wt.split_low(dve, i)
                    decays.on_vector(dve, m)
                for m in range(12, M):
                    for i in wt.ahead(m):
                        wt.split_low(dve, i)
                    decays.on_vector(dve, m)
                for i in range(4):
                    b = 4 + 2 * (i % 2)
                    dve.wait_ge(v_turned, i + 1)
                    dve.tensor_copy(vtok[:, 0:4, P * i:P * i + P], split_free(net.bank(b), t=4, n=P))
                    dve.tensor_copy(vtok[0:NS, 4, P * i:P * i + P], net.ps[0:NS, b + 1, 0:P]).then_inc(v_kept, 1)
        with nc.Block() as block:
            @block.sync
            def _(sp):
                net.store(sp, io["ssd_tails"], tails[:])
                net.all_stored(sp)


def gla(net, c, small, decays, vtok, qk, hs_s, ssd_landed):
    nc, io = net.nc, net.io
    H = 4
    NC = TP // GCH
    cum, dec = decays.cum, decays.dec
    with ExitStack() as st:
        sb = lambda n, s: st.enter_context(net.buf(n, s))
        la, ke = sb("la", [P, H, T]), sb("ke", [P, H, T])
        squares, ssq = sb("squares", [P, H, P]), sb("ssq", [P, TT, H])
        kdt = sb("kdt", [P, TT, 512])
        sp_, ss = sb("s_p", [P, 2, H, P]), sb("s_s", [P, NB, H, P])
        q, k, gg = qk[:, 0:4, :], qk[:, 4:8, :], qk[:, 8:12, :]
        o = [la[:, tt, 0:512] for tt in range(4)] + [cum[:, 0, 0:512]]
        qm = [split_free(cum[:, 1 + i, 0:256], h=H, n=NS) for i in range(2)]
        kdm = [k[0:NS, i, 0:512] for i in range(2)]
        att = [split_free(k[:, 2 + i, 0:512], h=H, n=P) for i in range(2)]
        state_landed, exp_up, q_done, exp_down, ke_done, left, exp_left, k_done, turned = (
            net.sem(n) for n in ("state_landed", "exp_up", "q_done", "exp_down", "ke_done", "left", "exp_left", "k_done", "turned"))

        def chunks(ap):
            return (ap[:, 0:TP].rearrange("p (c n) -> p c n", n=GCH), ap[:, TP:T].rearrange("p (c n) -> p c n", n=TS))

        with nc.Block() as block:
            @block.sync
            def _(sp):
                sp.dma_start(ss[:], io["gla_s0"]).then_inc(state_landed, 16)
                sp.wait_ge(state_landed, 16)
                sp.dma_start(hs_s[:], io["ssd_h0"]).then_inc(ssd_landed, 16)

            @block.tensor
            def _(pe):
                pe.wait_ge(k_done, H)
                for tt in range(TT):
                    cols, m = tok(tt)
                    for h in range(H):
                        mm = pe.transpose(net.ps[0:m, tt, P * h:P * h + P], k[:, h, cols], net.ident[:])
                    mm.then_inc(turned, 1)

            @block.gpsimd
            def _(pool):
                for h in range(H):
                    pool.wait_ge(exp_down, h + 1)
                    pool.tensor_tensor(ke[:, h, :], ke[:, h, :], k[:, h, :], ALU.mult).then_inc(ke_done, 1)

            @block.scalar
            def _(act):
                for h in range(H):
                    act.activation(la[:, h, :], cum[:, h, :], ACT.Exp, scale=1.0 / 16).then_inc(exp_up, 1)
                    act.activation(ke[:, h, :], cum[:, h, :], ACT.Exp, scale=-1.0 / 16).then_inc(exp_down, 1)
                for h in range(H):
                    act.wait_ge(left, h + 1)
                    act.activation(la[:, h, :], la[:, h, :], ACT.Exp, scale=1.0 / 16).then_inc(exp_left, 1)
                for tt in range(TT):
                    _, m = tok(tt)
                    act.wait_ge(turned, tt + 1)
                    act.activation(kdt[0:m, tt, :], net.ps[0:m, tt, :], ACT.Copy)

            @block.vector
            def _(dve):
                for h in range(H):
                    dve.wait_ge(exp_up, h + 1)
                    dve.tensor_tensor(q[:, h, :], q[:, h, :], la[:, h, :], ALU.mult).then_inc(q_done, 1)
                for h in range(H):
                    dve.wait_ge(q_done, h + 1)
                    for x, e, y, n, w in zip(chunks(cum[:, h, :]), decays.ends(cum), chunks(la[:, h, :]), (NC, NB), (GCH, TS)):
                        ins = dve.tensor_tensor(y, e[:, h, :, None].broadcast_to([P, n, w]), x, ALU.subtract)
                    ins.then_inc(left, 1)
                for h in range(H):
                    dve.wait_ge(exp_left, h + 1)
                    dve.wait_ge(ke_done, h + 1)
                    dve.tensor_tensor(k[:, h, :], k[:, h, :], la[:, h, :], ALU.mult).then_inc(k_done, 1)

        scored, masked, o_done, o_kept, inter_done, kv_done, stepped, kdm_done, kv_used = (
            net.sem(n) for n in ("scored", "masked", "o_done", "o_kept", "inter_done", "kv_done", "stepped", "kdm_done", "kv_used"))
        zeroed, squared, normed, meaned, root, turned, rms_used, order, zeroed_qm, qm_done = (
            net.sem(n) for n in ("zeroed", "squared", "normed", "meaned", "root", "turned", "rms_used", "order", "zeroed_qm", "qm_done"))
        A, O, KV = (0, 1), (2, 3), (4, 5, 6, 7)
        chunk_list = [(tt, ch) for tt in range(TT) for ch in range(4 if tt < 4 else NB)]
        with nc.Block() as block:
            @block.tensor
            def _(pe):
                def scores(tt):
                    cols, m = tok(tt)
                    if tt >= 2:
                        pe.wait_ge(masked, tt - 1)
                    for h in range(H):
                        mm = pe.matmul(net.ps[0:m, A[tt % 2], P * h:P * h + m], ke[:, h, cols], q[:, h, cols], start=True, stop=True)
                    mm.then_inc(scored, 1)

                def new_kv(n):
                    tt, ch = chunk_list[n]
                    lo, w = (GCH * ch, GCH) if tt < 4 else (TS * ch, TS)
                    if n >= 4:
                        pe.wait_ge(kv_used, n - 3)
                    if tt == 4:
                        pe.wait_ge(kdm_done, ch + 1)
                    for h in range(H):
                        if tt < 4:
                            lhs, rhs = kdt[lo:lo + w, tt, P * h:P * h + P], vtok[lo:lo + w, tt, P * h:P * h + P]
                        else:
                            lhs, rhs = kdm[ch % 2][:, P * h:P * h + P], vtok[0:NS, 4, P * h:P * h + P]
                        mm = pe.matmul(net.ps[:, KV[n % 4], P * h:P * h + P], lhs, rhs, start=True, stop=True)
                    mm.then_inc(kv_done, 1)

                pe.wait_ge(zeroed, 1)
                new_kv(0)
                new_kv(1)
                scores(0)
                n = 0
                for tt in range(TT):
                    cols, m = tok(tt)
                    pe.wait_ge(masked, tt + 1)
                    if tt >= 2:
                        pe.wait_ge(o_kept, tt - 1)
                    for h in range(H):
                        pe.matmul(net.ps[0:m, O[tt % 2], P * h:P * h + P], att[tt % 2][0:m, h, 0:m], vtok[0:m, tt, P * h:P * h + P],
                                  start=(h == 0), stop=False, skip_group_check=True)
                    for ch in range(4 if tt < 4 else NB):
                        if n + 2 < len(chunk_list):
                            new_kv(n + 2)
                        if ch == 1 and tt + 1 < TT:
                            scores(tt + 1)
                        lo, w = (GCH * ch, GCH) if tt < 4 else (TS * ch, TS)
                        if tt < 4 and n:
                            pe.wait_ge(kv_used, n)
                        if tt == 4:
                            pe.wait_ge(qm_done, ch + 1)
                        for h in range(H):
                            last = h == H - 1 and (tt < 4 or ch == NB - 1)
                            if tt < 4:
                                mm = pe.matmul(net.ps[lo:lo + w, O[tt % 2], P * h:P * h + P], q[:, h, cols.start + lo:cols.start + lo + w], sp_[:, n % 2, h, :],
                                               start=False, stop=last, skip_group_check=True)
                            else:
                                mm = pe.matmul(net.ps[0:NS, O[0], P * h:P * h + P], qm[ch % 2][:, h, :], ss[:, ch, h, :],
                                               start=False, stop=last, skip_group_check=True)
                        mm.then_inc(inter_done, 1)
                        n += 1
                pe.wait_ge(kv_used, len(chunk_list))
                for tt in range(TT):
                    cols, m = tok(tt)
                    pe.wait_ge(normed, tt + 1)
                    if tt == 4:
                        pe.wait_ge(rms_used, 1)
                    for h in range(H):
                        mm = pe.transpose(net.ps[:, KV[tt % 4], P * h:P * h + m], o[tt][0:m, P * h:P * h + P], net.ident[0:m, 0:m])
                    mm.then_inc(turned, 1)

            @block.scalar
            def _(act):
                for tt in range(TT):
                    cols, m = tok(tt)
                    act.wait_ge(inter_done, 4 * (tt + 1) if tt < 4 else 16 + NB)
                    if tt:
                        act.wait_ge(squared, tt)
                    for h in range(H):
                        ins = act.activation(squares[0:m, h, :], net.ps[0:m, O[tt % 2], P * h:P * h + P], ACT.Square, accum_out=ssq[0:m, tt, h:h + 1])
                    ins.then_inc(squared, 1)
                    act.activation(o[tt][0:m], net.ps[0:m, O[tt % 2], :], ACT.Copy).then_inc(o_kept, 1)
                act.wait_ge(meaned, 1)
                act.activation(ssq[:, 0:4], ssq[:, 0:4], ACT.Sqrt)
                act.activation(ssq[0:NS, 4], ssq[0:NS, 4], ACT.Sqrt).then_inc(root, 1)

            @block.gpsimd
            def _(pool):
                for b in range(NB):
                    if b >= 2:
                        pool.wait_ge(kv_done, 16 + b - 1)
                    pool.tensor_scalar(kdm[b % 2], kdt[0:NS, 4, :], c["of_b"][0:NS, b:b + 1], 1.0, ALU.mult, ALU.mult).then_inc(kdm_done, 1)
                    if b >= 2:
                        pool.wait_ge(inter_done, 16 + b - 1)
                    pool.memset(qm[b % 2], 0.0).then_inc(zeroed_qm, 1)
                    pool.wait_ge(zeroed_qm, b + 1)
                    at = TS * b
                    pool.tensor_copy(qm[b % 2][:, :, at:at + TS], q[:, :, TP + at:TP + at + TS]).then_inc(qm_done, 1)

            @block.vector
            def _(dve):
                link = Chain(dve, order)
                dve.memset(sp_[:, 0], 0.0).then_inc(zeroed, 1)
                def mask_scores(tt):
                    _, m = tok(tt)
                    mask = (c["upto_g"] if tt < 4 else c["upto_s"])[0:m, None, 0:m].broadcast_to([m, H, m])
                    dve.wait_ge(scored, tt + 1)
                    if tt >= 2:
                        dve.wait_ge(inter_done, 4 * (tt - 1))
                    dve.tensor_tensor(att[tt % 2][0:m, :, 0:m], split_free(net.ps[0:m, A[tt % 2], :], h=H, n=P)[:, :, 0:m], mask, ALU.mult).then_inc(masked, 1)

                mask_scores(0)
                n = 0
                for tt in range(TT):
                    for ch in range(4 if tt < 4 else NB):
                        dve.wait_ge(kv_done, n + 1)
                        if n == 0:
                            dve.wait_ge(zeroed, 1)
                        elif tt < 4:
                            dve.wait_ge(kv_used, n)
                            dve.wait_ge(inter_done, n)
                        else:
                            dve.wait_ge(inter_done, n + 1)
                        for h in range(H):
                            old = sp_[:, n % 2, h, :] if tt < 4 else ss[:, ch, h, :]
                            new = sp_[:, (n + 1) % 2, h, :] if tt < 4 else old
                            ins = dve.scalar_tensor_tensor(new, old, dec[:, h, n:n + 1], net.ps[:, KV[n % 4], P * h:P * h + P], ALU.mult, ALU.add)
                        ins.then_inc(kv_used, 1)
                        n += 1
                        if ch == 2 and tt + 1 < TT:
                            mask_scores(tt + 1)
                dve.wait_ge(o_kept, TT)
                parts = (ssq[:, 0:4], ssq[0:NS, 4])
                for x in parts:
                    ins = dve.tensor_scalar(x, x, 1.0 / P, EPS, ALU.mult, ALU.add)
                ins.then_inc(meaned, 1)
                dve.wait_ge(root, 1)
                for x in parts:
                    ins = dve.reciprocal(x, x)
                link(ins)

                def gate(tt):
                    cols, m = tok(tt)
                    dve.wait_ge(turned, tt + 1)
                    x = gg[:, :, cols]
                    dve.scalar_tensor_tensor(x, x, small[:, 35:36], split_free(net.bank(KV[tt % 4]), h=H, n=P)[:, :, 0:m], ALU.mult, ALU.mult).then_inc(rms_used, 1)

                for tt in range(TT):
                    _, m = tok(tt)
                    x = split_free(o[tt][0:m], h=H, n=P)
                    dve.tensor_tensor(x, x, ssq[0:m, tt, :, None].broadcast_to([m, H, P]), ALU.mult).then_inc(normed, 1)
                    if tt:
                        gate(tt - 1)
                gate(TT - 1)

            @block.sync
            def _(sp):
                sp.wait_ge(kv_used, 16 + NB)
                net.store(sp, io["gla_s_p"], sp_[:, 0])
                net.store(sp, io["gla_s_s"], ss[:])


def ssd_chunks(net, c, xbc, cum, per, DL, hs_p, hs_s, cat):
    nc, io = net.nc, net.io
    TILE = [4, 0, 1, 2, 3]
    SLOTS = 4 * TT
    XS, BCB, D, Y, OFF, KV = 0, 2, (3, 4), 5, 7, (1, 6)
    kv_at = {s: [] for s in range(SLOTS)}
    kv_no, n_kv = {}, 0
    for s in range(4, SLOTS):
        n, q = divmod(s, 4)
        for key in ([("p", n, q - 2)] if q >= 2 else []) + [("s", (s - 4) // 2, s % 2)]:
            kv_at[s].append((n_kv, key))
            kv_no[key] = n_kv
            n_kv += 1
    with ExitStack() as st:
        sb = lambda n, s: st.enter_context(net.buf(n, s))
        xdt, xdd, xdd_s = sb("xdt", [P, 2, 1024]), sb("xdd", [P, 2, 1024]), sb("xdd_s", [NS, 1024])
        bt, cbm, btm = sb("bt", [P, 2, 2, P]), sb("cbm", [P, 2, 2, P]), sb("btm", [NS, NB, 2, P])
        L = sb("L", [P, 3, 4, P])
        (zeroed, order, decays, clamped, exped, mixed, y_done, y_summed, off_done, xs_turned, xdt_done, xdd_done, bcb_done,
         b_kept, cb_kept, btm_done, hp_decayed, hs_decayed, kv_done, kv_used) = (net.sem(n) for n in (
             "zeroed", "order", "decays", "clamped", "exped", "mixed", "y_done", "y_summed", "off_done", "xs_turned", "xdt_done",
             "xdd_done", "bcb_done", "b_kept", "cb_kept", "btm_done", "hp_decayed", "hs_decayed", "kv_done", "kv_used"))
        with nc.Block() as block:
            @block.tensor
            def _(pe):
                def sum_decays(s):
                    n, q = divmod(s, 4)
                    cols, m = tok(TILE[n])
                    if s >= 2:
                        pe.wait_ge(clamped, s - 1)
                    for i in range(4):
                        mm = pe.matmul(net.ps[0:m, D[s % 2], P * i:P * i + m], net.ident[0:NH, 4 * q + i:4 * q + i + 1].broadcast_to([NH, m]),
                                       cum[:, cols], start=True, stop=True)
                    mm.then_inc(decays, 1)

                def turn_xs(n, g):
                    cols, m = tok(TILE[n])
                    if n or g:
                        pe.wait_ge(xdt_done, 2 * n + g)
                    for i in range(4):
                        mm = pe.transpose(net.ps[0:m, XS, P * i:P * i + P], xbc[:, 4 * g + i, cols], net.ident[:])
                    mm.then_inc(xs_turned, 1)

                def turn_b(n):
                    cols, m = tok(TILE[n])
                    if n:
                        pe.wait_ge(b_kept, n)
                        pe.wait_ge(cb_kept, n)
                    for g in range(2):
                        pe.transpose(net.ps[0:m, BCB, P * g:P * g + P], xbc[:, 8 + g, cols], net.ident[:])
                    for g in range(2):
                        mm = pe.matmul(net.ps[0:m, BCB, 256 + P * g:256 + P * g + m], xbc[:, 8 + g, cols], xbc[:, 10 + g, cols], start=True, stop=True)
                    mm.then_inc(bcb_done, 1)

                def from_state(n, g):
                    cols, m = tok(TILE[n])
                    pe.wait_ge(y_summed, 2 * n + g)
                    if n > 1:
                        pe.wait_ge(kv_used, kv_no["p", n - 1, g] + 1)
                    else:
                        pe.wait_ge(zeroed, 1)
                    for j in range(4):
                        f = 512 * g + P * j
                        mm = pe.matmul(net.ps[:, OFF, P * j:P * j + P], hs_p[:, f:f + P], xbc[:, 10 + g, cols], start=True, stop=True)
                    mm.then_inc(off_done, 1)

                def new_state(no, key):
                    kind, i, g = key
                    if no >= 2:
                        pe.wait_ge(kv_used, no - 1)
                    if kind == "p":
                        pe.wait_ge(b_kept, i + 1)
                        pe.wait_ge(xdd_done, 2 * i + g + 1)
                        lhs, rhs = bt[:, i % 2, g, :], xdd[:, i % 2, 512 * g:512 * g + 512]
                    else:
                        pe.wait_ge(btm_done, i + 1)
                        pe.wait_ge(xdd_done, 2)
                        lhs, rhs = btm[:, i, g, :], xdd_s[:, 512 * g:512 * g + 512]
                    pe.matmul(net.ps[:, KV[no % 2], :], lhs, rhs, start=True, stop=True).then_inc(kv_done, 1)

                sum_decays(0)
                turn_xs(0, 0)
                turn_b(0)
                turn_xs(0, 1)
                for s in range(SLOTS):
                    n, q = divmod(s, 4)
                    g = q // 2
                    cols, m = tok(TILE[n])
                    if s + 1 < SLOTS:
                        sum_decays(s + 1)
                    if n + 1 < TT:
                        if q == 1:
                            turn_b(n + 1)
                        elif q in (0, 2):
                            turn_xs(n + 1, g)
                    if n and q % 2:
                        from_state(n, g)
                    if q % 2 == 0 and 2 * n + g:
                        pe.wait_ge(y_summed, 2 * n + g)
                    pe.wait_ge(mixed, s + 1)
                    for i in range(4):
                        hd = 4 * q + i
                        lo, at = 64 * (hd % 2), P * (hd % 8 // 2)
                        mm = pe.matmul(net.ps[lo:lo + 64, Y, at:at + m], xdt[0:m, n % 2, 64 * hd:64 * hd + 64], L[0:m, s % 3, i, 0:m], start=True, stop=True)
                    mm.then_inc(y_done, 1)
                    for no, key in kv_at[s]:
                        new_state(no, key)

            @block.scalar
            def _(act):
                def keep_b(n):
                    _, m = tok(TILE[n])
                    act.wait_ge(bcb_done, n + 1)
                    if n == 2:
                        act.wait_ge(btm_done, NB)
                    elif n > 2:
                        act.wait_ge(kv_done, kv_no["p", n - 2, 1] + 1)
                    act.activation(bt[0:m, n % 2, :, :], split_free(net.ps[0:m, BCB, 0:256], g=2, n=P), ACT.Copy).then_inc(b_kept, 1)

                keep_b(0)
                for s in range(SLOTS):
                    n, q = divmod(s, 4)
                    _, m = tok(TILE[n])
                    act.wait_ge(clamped, s + 1)
                    act.activation(L[0:m, s % 3, :, 0:m], L[0:m, s % 3, :, 0:m], ACT.Exp).then_inc(exped, 1)
                    if q == 2 and n + 1 < TT:
                        keep_b(n + 1)

            @block.gpsimd
            def _(pool):
                def leave(n, g):
                    _, m = tok(TILE[n])
                    dst = xdd[0:m, n % 2] if n else xdd_s
                    pool.wait_ge(xdt_done, 2 * n + g + 1)
                    if n > 2:
                        pool.wait_ge(kv_done, kv_no["p", n - 2, g] + 1)
                    pool.tensor_tensor(split_free(dst[:, 512 * g:512 * g + 512], h=8, n=64), split_free(xdt[0:m, n % 2, 512 * g:512 * g + 512], h=8, n=64),
                                       per[0:m, TILE[n], 2, 8 * g:8 * g + 8, None].broadcast_to([m, 8, 64]), ALU.mult).then_inc(xdd_done, 1)

                def decay(s, hs, at, heads):
                    hs = split_free(hs, h=heads, n=64)
                    return pool.tensor_tensor(hs, hs, DL[:, s:s + heads, at:at + 1].broadcast_to([P, heads, 64]), ALU.mult)

                leave(0, 0)
                leave(0, 1)
                pool.wait_ge(b_kept, 1)
                for b in range(NB):
                    pool.tensor_scalar(btm[:, b].rearrange("p g n -> p (g n)"), bt[0:NS, 0].rearrange("p g n -> p (g n)"), c["of_b"][0:NS, b:b + 1], 1.0,
                                       ALU.mult, ALU.mult).then_inc(btm_done, 1)
                b = 0
                for s in range(SLOTS):
                    n, q = divmod(s, 4)
                    if q % 2:
                        if n:
                            pool.wait_ge(off_done, 2 * (n - 1) + q // 2 + 1)
                            decay(8 * (q // 2), hs_p[:, 512 * (q // 2):512 * (q // 2) + 512], TILE[n], 8).then_inc(hp_decayed, 1)
                        if n + 1 < TT:
                            leave(n + 1, q // 2)
                    if b < NB and (s in (1, 2) or (n and q % 2 == 0)):
                        decay(0, hs_s[:, b, :], 4 + b, NH).then_inc(hs_decayed, 1)
                        b += 1

            @block.vector
            def _(dve):
                link = Chain(dve, order)

                def clamp(s):
                    n, q = divmod(s, 4)
                    _, m = tok(TILE[n])
                    dve.wait_ge(decays, s + 1)
                    if s >= 3:
                        dve.wait_ge(y_done, s - 2)
                    for i in range(4):
                        ins = dve.tensor_scalar(L[0:m, s % 3, i, 0:m], net.ps[0:m, D[s % 2], P * i:P * i + m],
                                                per[0:m, TILE[n], 0, 4 * q + i:4 * q + i + 1], 0.0, ALU.subtract, ALU.min)
                    ins.then_inc(clamped, 1)

                def scale_xs(n, g):
                    _, m = tok(TILE[n])
                    dve.wait_ge(xs_turned, 2 * n + g + 1)
                    if n > 1:
                        dve.wait_ge(y_done, 4 * (n - 1))
                    if n > 1:
                        dve.wait_ge(xdd_done, 2 * (n - 1))
                    dve.tensor_tensor(split_free(xdt[0:m, n % 2, 512 * g:512 * g + 512], h=8, n=64), split_free(net.ps[0:m, XS, :], h=8, n=64),
                                      per[0:m, TILE[n], 1, 8 * g:8 * g + 8, None].broadcast_to([m, 8, 64]), ALU.mult).then_inc(xdt_done, 1)

                def mask_cb(n):
                    _, m = tok(TILE[n])
                    mask = (c["upto"] if n else c["upto_s"])[0:m, None, 0:m].broadcast_to([m, 2, m])
                    dve.wait_ge(b_kept, n + 1)
                    dve.tensor_tensor(cbm[0:m, n % 2, :, 0:m], split_free(net.ps[0:m, BCB, 256:512], g=2, n=P)[:, :, 0:m], mask, ALU.mult).then_inc(cb_kept, 1)

                def sum_y(n, g):
                    cols, m = tok(TILE[n])
                    y = split_free(net.bank(Y), j=4, n=P)[:, :, 0:m]
                    out = cat[:, 4 * g:4 * g + 4, cols]
                    if n:
                        dve.wait_ge(off_done, 2 * (n - 1) + g + 1)
                        link(dve.tensor_tensor(out, split_free(net.bank(OFF), j=4, n=P), out, ALU.mult))
                    dve.wait_ge(y_done, 4 * n + 2 * g + 2)
                    dve.tensor_tensor(out, y, out, ALU.add).then_inc(y_summed, 1)

                def add_states(s):
                    for no, (kind, i, g) in kv_at[s]:
                        if kind == "p":
                            dve.wait_ge(hp_decayed, 2 * (i - 1) + g + 1)
                            h = hs_p[:, 512 * g:512 * g + 512]
                        else:
                            dve.wait_ge(hs_decayed, i + 1)
                            h = hs_s[:, i, 512 * g:512 * g + 512]
                        dve.wait_ge(kv_done, no + 1)
                        dve.tensor_tensor(h, h, net.ps[:, KV[no % 2], :], ALU.add).then_inc(kv_used, 1)

                dve.memset(hs_p[:], 0.0).then_inc(zeroed, 1)
                clamp(0)
                scale_xs(0, 0)
                mask_cb(0)
                scale_xs(0, 1)
                for s in range(SLOTS):
                    n, q = divmod(s, 4)
                    _, m = tok(TILE[n])
                    if s and q % 2 == 0:
                        sum_y(*divmod(s // 2 - 1, 2))
                    if s:
                        add_states(s - 1)
                    if s + 1 < SLOTS:
                        clamp(s + 1)
                    dve.wait_ge(exped, s + 1)
                    dve.wait_ge(cb_kept, n + 1)
                    l = L[0:m, s % 3, :, 0:m]
                    dve.tensor_tensor(l, l, cbm[0:m, n % 2, q // 2:q // 2 + 1, 0:m].broadcast_to([m, 4, m]), ALU.mult).then_inc(mixed, 1)
                    if n + 1 < TT:
                        if q == 2:
                            mask_cb(n + 1)
                        elif q % 2:
                            scale_xs(n + 1, q // 2)
                sum_y(TT - 1, 1)
                add_states(SLOTS - 1)

            @block.sync
            def _(sp):
                sp.wait_ge(kv_used, n_kv)
                net.store(sp, io["ssd_s_p"], hs_p[:])
                net.store(sp, io["ssd_s_s"], hs_s[:])


def ssd(net, c, small, zt, xbc, decays, cat, hs_s, ssd_landed):
    nc, io = net.nc, net.io
    cum, per, DL = decays.cum_a, decays.per, decays.DL
    with ExitStack() as st:
        sb = lambda n, s: st.enter_context(net.buf(n, s))
        EA = cat[:, 0:8, :]
        hs_p = sb("hs_p", [P, 1024])
        two_heads = hs_p[0:NH, :]
        cm = sb("cm", [P, NB, 2, NS])
        y_tok, eat = sb("y_tok", [NS, 1024]), sb("eat", [NS, NH])
        EA_sum, EA_done, heads_made, cm_zeroed, cm_done, off_s_done, eat_done, y_scaled, y_turned = (net.sem(n) for n in (
            "EA_sum", "EA_done", "heads_made", "cm_zeroed", "cm_done", "off_s_done", "eat_done", "y_scaled", "y_turned"))
        with nc.Block() as block:
            @block.sync
            def _(sp):
                net.all_stored(sp)

            @block.tensor
            def _(pe):
                pe.wait_ge(ssd_landed, 16)
                pe.wait_ge(heads_made, 1)
                for j in range(8):
                    lhs, b = two_heads[:, P * j:P * j + P], 2 * (j % 2)
                    if j >= 2:
                        pe.wait_ge(EA_done, j - 1)
                    pe.matmul(net.ps[:, b, 0:HT], lhs, cum[:, 0:HT], start=True, stop=True)
                    pe.matmul(net.ps[:, b + 1, 0:HT], lhs, cum[:, HT:T], start=True, stop=True).then_inc(EA_sum, 1)
                pe.wait_ge(cm_done, NB)
                for b in range(NB):
                    for g in range(2):
                        mm = pe.matmul(net.ps[0:NS, 6 + g, :], cm[:, b, g, :], hs_s[:, b, 512 * g:512 * g + 512], start=(b == 0), stop=(b == NB - 1))
                mm.then_inc(off_s_done, 1)
                pe.wait_ge(y_scaled, 2)
                pe.wait_ge(EA_done, 8)
                for j in range(8):
                    mm = pe.transpose(net.ps[:, 0, NS * j:NS * j + NS], y_tok[:, P * j:P * j + P], net.ident[0:NS, 0:NS])
                mm.then_inc(y_turned, 1)

            @block.gpsimd
            def _(pool):
                pool.memset(cm[:], 0.0).then_inc(cm_zeroed, 1)
                pool.wait_ge(cm_zeroed, 1)
                for b in range(NB):
                    pool.tensor_copy(cm[:, b, :, TS * b:TS * b + TS], xbc[:, 10:12, TP + TS * b:TP + TS * b + TS]).then_inc(cm_done, 1)

            @block.scalar
            def _(act):
                act.activation(eat[:], per[0:NS, 4, 0, :], ACT.Exp).then_inc(eat_done, 1)
                for j in range(8):
                    act.wait_ge(EA_sum, j + 1)
                    act.activation(halves(EA[:, j, :]), both(net, 2 * (j % 2)), ACT.Exp).then_inc(EA_done, 1)

            @block.vector
            def _(dve):
                dve.tensor_copy(split_free(two_heads, h=NH, n=64), net.ident[0:NH, 0:NH, None].broadcast_to([NH, NH, 64])).then_inc(heads_made, 1)
                dve.wait_ge(off_s_done, 1)
                dve.wait_ge(eat_done, 1)
                for g in range(2):
                    dve.tensor_tensor(split_free(y_tok[:, 512 * g:512 * g + 512], h=8, n=64), split_free(net.ps[0:NS, 6 + g, :], h=8, n=64),
                                      eat[:, 8 * g:8 * g + 8, None].broadcast_to([NS, 8, 64]), ALU.mult).then_inc(y_scaled, 1)
                dve.wait_ge(y_turned, 1)
                dve.tensor_copy(EA[:, :, TP:T], split_free(net.bank(0), j=8, n=NS))

        ssd_chunks(net, c, xbc, cum, per, DL, hs_p, hs_s, cat)

        gated, squared, summed, root, order = (net.sem(n) for n in ("gated", "squared", "summed", "root", "order"))
        with nc.Block() as block:
            @block.sync
            def _(sp):
                net.all_stored(sp)

            @block.vector
            def _(dve):
                link = Chain(dve, order)
                for j in range(8):
                    link(dve.scalar_tensor_tensor(cat[:, j, :], xbc[:, j, :], small[:, 2 + j:3 + j], cat[:, j, :], ALU.mult, ALU.add))
                    dve.tensor_tensor(cat[:, j, :], cat[:, j, :], zt[:, j, :], ALU.mult).then_inc(gated, 1)
                dve.wait_ge(summed, 8)
                r = net.rstd[:]
                dve.tensor_scalar(halves(r), both(net, 0), 1.0 / 1024, EPS, ALU.mult, ALU.add).then_inc(root, 1)
                dve.wait_ge(root, 2)
                link(dve.reciprocal(r, r))

            @block.scalar
            def _(act):
                for j in range(8):
                    act.wait_ge(gated, j + 1)
                    act.activation(zt[:, j, :], cat[:, j, :], ACT.Square).then_inc(squared, 1)
                act.wait_ge(root, 1)
                act.activation(net.rstd[:], net.rstd[:], ACT.Sqrt).then_inc(root, 1)

            @block.tensor
            def _(pe):
                for j in range(8):
                    pe.wait_ge(squared, j + 1)
                    for a in range(2):
                        mm = pe.matmul(net.ps[:, a, 0:HT], net.ones[:], zt[:, j, HT * a:HT * a + HT], start=(j == 0), stop=(j == 7), skip_group_check=True)
                    mm.then_inc(summed, 1)


def even_mixer(net, cat):
    nc = net.nc
    with ExitStack() as st:
        sb = lambda n, s: st.enter_context(net.buf(n, s))
        cpk = sb("even_consts", [P, pack(EVEN_C).shape[1]])
        c = unpack(cpk, EVEN_C)
        landed = net.sem("consts_landed")
        with nc.Block() as block:
            @block.sync
            def _(sp):
                sp.dma_start(cpk[:], net.io["even_consts"]).then_inc(landed, 16)
                sp.wait_ge(landed, 16)
        kv, gates = sb("kv", [P, TT, 768]), sb("gates", [P, TT, 24])
        qT, kT = sb("qT", [P, 4, T]), sb("kT", [P, 2, T])
        qTs = sb("qTs", [P, NB, 4, TS])
        tails, hlast = sb("lru_tails", [P, 4, 27]), sb("lru_hlast", [P, 4, 9])
        wc, ce = sb("wc", [P, 4, 4, 32]), sb("ce", [P, 8])
        wv4 = sb("wv4", [P, 2, 4, 4, 32])
        even_project(net, cat, kv, gates, qT, kT, qTs, tails, hlast, wc, wv4, ce, c)
        past = SamplePast(net, st)
        prompt_attention(net, past, kv, gates, qT, kT, wc, wv4, cat, c)
        sample_attention(net, past, kv, gates, kT, qTs, wc, cat, c)


def store_y(net):
    fin = FinishX(net, None)
    with net.nc.Block() as block:
        @block.vector
        def _(dve):
            fin.on_vector(dve)

        @block.scalar
        def _(act):
            fin.on_scalar(act)

        @block.sync
        def _(sp):
            for k in range(KD):
                sp.wait_ge(fin.x_done, k + 1)
                net.store(sp, net.io["y"][:, k, :], net.x[:, k, :])
            net.all_stored(sp)


OUTS = {
    "y": [P, KD, T], "kv_p": [TP, 512], "kv_s": [NS, 512], "win_p": [TP, 256], "win_s": [NB, 512, 256],
    "lru_tails": [P, 4, 27], "lru_hlast": [P, 4, 9], "ffn_tails": [2, P, 2 * FM, 18], "ssd_tails": [P, 12, 27],
    "gla_s_p": [P, 4, P], "gla_s_s": [P, NB, 4, P], "ssd_s_p": [P, 1024], "ssd_s_s": [P, NB, 1024],
}


def trunk_kernel(nc, io):
    with ExitStack() as ctx:
        net = Net(nc, ctx, io)
        load_x(net)
        with net.buf("cat", [P, 8, T]) as cat:
            even_mixer(net, cat)
            mix_and_norm(net, cat, 8, 0)
        net.recycle()
        ffn(net, 0)
        net.recycle()
        with net.buf("cat1", [P, 12, T]) as cat:
            odd_mixer(net, cat)
        net.recycle()
        ffn(net, 1)
        store_y(net)


def tiles(w, m=P):
    k = w.shape[0] // P
    return w.reshape(k, P, w.shape[1] // m, m).transpose(2, 1, 0, 3)


def rows(a, n):
    f = a.reshape(a.shape[:-1] + (n, P))
    return np.moveaxis(f, (-1, -2), (0, 1))


def lay_out(i):
    o = {}
    z = np.zeros
    x = np.concatenate([i["x_prompt"][0], i["x_sample"].reshape(NS, D)], 0)
    o["x"] = x.T.reshape(KD, P, T).transpose(1, 0, 2)
    o["ones"], o["ident"] = constants()["ones"], constants()["ident"]
    o["even_consts"] = pack(EVEN_C)
    o["odd_consts"] = pack(ODD_C)
    we = i["w_in_even"][0]
    wq = we[:, 0:512].reshape(D, 2, 4, DH).transpose(0, 2, 1, 3).reshape(D, 512)
    part = lambda n: we[:, 512 + P * n:640 + P * n]
    gate = np.concatenate([we[:, 1280:1304], z((D, P - 24), np.float32)], 1)
    o["w_even"] = tiles(np.concatenate([we[:, 1304:], wq, part(0), part(2), part(4), gate, part(1), part(3), part(5)], 1))
    o["rope_consts"] = pack(ROPE_C)
    taps = i["lru_conv_w"][0]
    o["lru_small"] = rows(np.concatenate([taps, i["lru_conv_b"], i["lru_b_gates"][0], i["lru_lambda"]], 0), 4)
    o["lru_hist"] = rows(i["state_lru_conv"][0], 4)
    o["lru_h0"] = rows(i["state_lru_h"][0], 4)
    wg = z((2, 4, P, P), np.float32)
    g = i["lru_w_gates"][0]
    for t in range(4):
        wg[:, t, 0:64, 0:64] = g[:, 2 * t]
        wg[:, t, 64:, 64:] = g[:, 2 * t + 1]
    o["lru_wg"] = wg.reshape(8, P, P).transpose(1, 0, 2)
    cw = i["nsa_cmp_w"][0].reshape(2, 16, 4)
    o["cmp_w"] = np.concatenate([np.tile(cw[0], (8, 1)), np.tile(cw[1], (8, 1))], 1)
    ck = i["cache_nsa_kv"][0].reshape(PHYS, P, 4, P)
    o["cache_kT"] = ck[:, :, 2, :].transpose(0, 2, 1)
    o["cache_tok"] = ck[:, :, [0, 1, 3], :].reshape(PHYS, P, 3 * P)
    win = i["cache_nsa_win"][0].reshape(NB, 512, 2, P)
    o["win_tok"] = win.reshape(NB, 512, 256)
    o["win_kT"] = win[:, :, 0, :].transpose(0, 2, 1)
    o["win_v"] = win[:, :, 1, :].reshape(NB, 4, P, P).transpose(0, 2, 1, 3)
    o["pages"] = i["page_table"].reshape(1, NB * PAGES)
    wo = i["w_out_even"][0]
    wn = wo[0:512].reshape(2, 4, DH, D).transpose(1, 0, 2, 3).reshape(512, D)
    o["w_mix0"] = tiles(np.concatenate([wn, wo[512:]], 0))
    o["w_mix1"] = tiles(i["w_out_odd"][0])
    for n in ("mix", "ffn"):
        o[f"ln_{n}"] = np.stack([np.stack([rows(i[f"ln_{n}_{s}"][k], KD) for s in "gb"], 1) for k in range(2)])
    up, par, hist = [], [], []
    for k in range(2):
        pairs = lambda a: a.reshape(a.shape[:-1] + (2, FM, P)).swapaxes(-2, -3).reshape(a.shape)
        up.append(tiles(pairs(i["ffn_w_up"][k])))
        par.append(rows(pairs(np.concatenate([i["ffn_conv_w"][k], i["ffn_conv_b"][k][None]], 0)), 2 * FM))
        old = rows(pairs(i["state_ffn_conv"][k]), 2 * FM).reshape(P, 2 * FM, 16)
        hist.append(np.concatenate([z((P, 2 * FM, 2), np.float32), old], 2))
        o[f"w_down{k}"] = tiles(i["ffn_w_down"][k])
    o["w_up"], o["ffn_par"], o["ffn_hist"] = np.stack(up), np.stack(par), np.stack(hist)
    w = i["w_in_odd"][0]
    zc, xc, dc, gq, gk, gv, gg, ga = np.split(w, np.cumsum([1024, 1536, 16, 512, 512, 512, 512]), 1)
    o["w_odd"] = tiles(np.concatenate([xc, zc, gg, gq, gk, gv], 1))
    o["w_odd48"] = np.concatenate([dc, z((D, 16), np.float32), ga], 1).reshape(KD, P, 48).transpose(1, 0, 2)
    o["ssd_conv_par"] = rows(np.concatenate([i["ssd_conv_w"][0], i["ssd_conv_b"]], 0), 12)
    o["ssd_hist"] = rows(i["state_ssd_conv"][0], 12)
    s = z((P, 48), np.float32)
    s[0:NH, 0], s[0:NH, 1] = i["ssd_dt_bias"][0], i["ssd_a_log"][0]
    s[:, 2:10] = np.repeat(i["ssd_d"][0], 64).reshape(8, P).T
    s[:, 27:35] = i["ssd_norm_w"][0].reshape(8, P).T
    s[:, 35] = i["gla_norm_w"][0]
    s[:, 36:40] = i["gla_b_alpha"][0].reshape(4, P).T
    o["odd_small"] = s
    o["w_alpha"] = i["gla_w_alpha"][0]
    o["gla_s0"] = i["state_gla"][0].transpose(2, 0, 1, 3)
    o["ssd_h0"] = i["state_ssd"][0].transpose(3, 0, 1, 2).reshape(P, NB, 1024)
    return {k: np.ascontiguousarray(v) for k, v in o.items()}


def undo(r):
    y = r["y"].transpose(2, 1, 0).reshape(T, D)
    back = lambda a: np.moveaxis(a, (0, 1), (-1, -2)).reshape(a.shape[2:] + (-1,))
    lt, lh, st = r["lru_tails"], r["lru_hlast"], r["ssd_tails"]
    sp = lambda a, n: a[:, :, n:].reshape(P, a.shape[1], NB, n)
    ft_p, ft_s = [], []
    for k in range(2):
        f = r["ffn_tails"][k]
        unpair = lambda a: a.reshape(a.shape[:-1] + (FM, 2, P)).swapaxes(-2, -3).reshape(a.shape)
        ft_p.append(unpair(back(f[:, :, 0:2])))
        ft_s.append(unpair(back(sp(f, 2))))
    gp, gs = r["gla_s_p"], r["gla_s_s"]
    hp, hs = r["ssd_s_p"], r["ssd_s_s"]
    return (
        y[None, :TP], y[TP:].reshape(NB, TS, D),
        r["kv_p"].reshape(1, 1, TP, 4, 2, DH), r["kv_s"].reshape(1, NB, TS, 4, 2, DH),
        r["win_p"].reshape(1, 1, TP, 2, 2, DH), r["win_s"].reshape(1, NB, 512, 2, 2, DH),
        back(lh[:, :, 0])[None, None], back(lh[:, :, 1:])[None],
        back(lt[:, :, 0:3])[None, None], back(sp(lt, 3))[None],
        hp.T.reshape(1, 1, NH, DH, P), hs.transpose(1, 2, 0).reshape(1, NB, NH, DH, P),
        back(st[:, :, 0:3])[None, None], back(sp(st, 3))[None],
        gp.transpose(1, 0, 2)[None, None], gs.transpose(1, 2, 0, 3)[None],
        np.stack(ft_p)[:, None], np.stack(ft_s),
    )


def kernel(**inputs):
    import concourse.bacc as bacc
    from concourse.bass_utils import run_bass_kernel_spmd

    nc = bacc.Bacc("TRN2", target_bir_lowering=False, num_devices=1)
    arrays = lay_out({k: np.asarray(v) for k, v in inputs.items()})
    io = {}
    for name, a in arrays.items():
        io[name] = nc.dram_tensor(f"in_{name}", a.shape, mybir.dt.from_np(a.dtype), kind="ExternalInput").ap()
    for name, shape in OUTS.items():
        io[name] = nc.dram_tensor(f"out_{name}", shape, F32, kind="ExternalOutput").ap()
    trunk_kernel(nc, io)
    r = run_bass_kernel_spmd(nc, [{f"in_{k}": v for k, v in arrays.items()}], core_ids=[0])
    got = {n: r.results[0][f"out_{n}"].reshape(s) for n, s in OUTS.items()}
    return tuple(np.ascontiguousarray(a) for a in undo(got))
```
